# Optimizing a Trainium2 kernel written in Bass

```python
import jax, jax.numpy as jnp
from jax import lax
import numpy as np
import math

D_MODEL = 1024
BATCH = 1
SEQ = 1024
DEPTH = 1

GRID_W = 64
CTX_LEN = 256
D_MIX = D_MODEL
D_ATTN = D_MIX // 2
D_CONV = D_MIX - D_ATTN
HEAD_DIM = 64
N_HEADS = D_ATTN // HEAD_DIM
WIN_H = 8
WIN_W = 16
CONV_K = 3
ROPE_THETA = 10000.0
RMS_EPS = 1e-6
SPLIT_POINTS = (D_ATTN, 2 * D_ATTN, 3 * D_ATTN, 4 * D_ATTN,
                4 * D_ATTN + D_CONV, 4 * D_ATTN + 2 * D_CONV, 4 * D_ATTN + 3 * D_CONV)
D_IN = 4 * D_ATTN + 4 * D_CONV


def rmsnorm(x, g):
    xf = x.astype(jnp.float32)
    y = xf * lax.rsqrt(jnp.mean(xf * xf, axis=-1, keepdims=True) + RMS_EPS)
    return (y * g.astype(jnp.float32)).astype(x.dtype)

def adaln(cond, w_ada, b_ada):
    m = jax.nn.silu(cond) @ w_ada + b_ada
    return jnp.split(m, 3, axis=-1)

def heads(t):
    return t.reshape(*t.shape[:-1], N_HEADS, HEAD_DIM)

def axial_rope(t, n_cols):
    S = t.shape[1]
    nf = HEAD_DIM // 4
    inv = ROPE_THETA ** (-jnp.arange(nf, dtype=jnp.float32) / nf)
    pos = jnp.arange(S, dtype=jnp.int32)
    row = (pos // n_cols).astype(jnp.float32)
    col = (pos % n_cols).astype(jnp.float32)
    ang = jnp.stack([row[:, None] * inv, col[:, None] * inv], axis=1)
    cos = jnp.cos(ang)[:, None, :, None, :]
    sin = jnp.sin(ang)[:, None, :, None, :]
    tf = t.astype(jnp.float32).reshape(*t.shape[:-1], 2, 2, nf)
    rot = jnp.stack([-tf[..., 1, :], tf[..., 0, :]], axis=-2)
    return (tf * cos + rot * sin).reshape(t.shape).astype(t.dtype)

def neighbourhood_attention(q, k, v, kc, vc, rpb):
    Bn, S, H, Dh = q.shape
    rows = S // GRID_W
    wh = min(WIN_H, rows)
    scale = Dh ** -0.5
    q_plain = q.reshape(Bn, rows, GRID_W, H, Dh)
    q_rot = axial_rope(q, GRID_W).reshape(Bn, rows, GRID_W, H, Dh)
    k_rot = axial_rope(k, GRID_W).reshape(Bn, rows, GRID_W, H, Dh)
    v_g = v.reshape(Bn, rows, GRID_W, H, Dh)
    qi = jnp.arange(rows)
    row_start = jnp.clip(qi - wh // 2, 0, rows - wh)
    row_idx = row_start[:, None] + jnp.arange(wh)[None, :]
    k_rows = k_rot[:, row_idx]
    v_rows = v_g[:, row_idx]
    cols = jnp.arange(GRID_W)
    col_start = jnp.clip(cols - WIN_W // 2, 0, GRID_W - WIN_W)
    col_valid = (cols[None, :] >= col_start[:, None]) & (cols[None, :] < col_start[:, None] + WIN_W)
    dr = row_idx - qi[:, None] + (WIN_H - 1)
    dc = jnp.clip(cols[None, :] - cols[:, None] + (WIN_W - 1), 0, 2 * WIN_W - 2)
    bias = rpb[:, dr[:, None, :, None], dc[None, :, None, :]].astype(jnp.float32)
    s_lat = jnp.einsum('biqhd,birkhd->bhiqrk', q_rot, k_rows,
                       preferred_element_type=jnp.float32) * scale + bias
    s_lat = jnp.where(col_valid[:, None, :], s_lat, -jnp.inf)
    s_ctx = jnp.einsum('biqhd,blhd->bhiql', q_plain, kc,
                       preferred_element_type=jnp.float32) * scale
    n_lat = wh * GRID_W
    s = jnp.concatenate([s_lat.reshape(*s_lat.shape[:4], n_lat), s_ctx], axis=-1)
    p = jax.nn.softmax(s, axis=-1).astype(v.dtype)
    p_lat = p[..., :n_lat].reshape(s_lat.shape)
    p_ctx = p[..., n_lat:]
    o = (jnp.einsum('bhiqrk,birkhd->biqhd', p_lat, v_rows)
         + jnp.einsum('bhiql,blhd->biqhd', p_ctx, vc))
    return o.reshape(Bn, S, H * Dh)

def context_attention(qc, kc, vc):
    Bn, L, H, Dh = qc.shape
    s = jnp.einsum('blhd,bmhd->bhlm', qc, kc, preferred_element_type=jnp.float32) * (Dh ** -0.5)
    p = jax.nn.softmax(s, axis=-1).astype(vc.dtype)
    return jnp.einsum('bhlm,bmhd->blhd', p, vc).reshape(Bn, L, H * Dh)

def centred_short_conv(u, w, b):
    L = u.shape[1]
    pad = CONV_K // 2
    up = jnp.pad(u, ((0, 0), (pad, pad), (0, 0)))
    y = b
    for i in range(CONV_K):
        y = y + up[:, i:i + L] * w[i]
    return y

def gated_short_conv(u, bg, cg, zc, conv_w, conv_b):
    return bg * centred_short_conv(cg * u, conv_w, conv_b) * jax.nn.silu(zc)

def hybrid_layer(x, ctx, c, c_ctx, w_ada, b_ada, norm_g, w_in, q_norm_g, k_norm_g,
                 rpb, conv_w, conv_b, w_out, update_ctx):
    shift, scale, gate = adaln(c, w_ada, b_ada)
    shift_c, scale_c, gate_c = adaln(c_ctx, w_ada, b_ada)
    h = rmsnorm(x, norm_g) * (1 + scale[:, None]) + shift[:, None]
    hc = rmsnorm(ctx, norm_g) * (1 + scale_c) + shift_c
    q, k, v, za, u, bg, cg, zc = jnp.split(h @ w_in, SPLIT_POINTS, axis=-1)
    q = rmsnorm(heads(q), q_norm_g)
    k = rmsnorm(heads(k), k_norm_g)
    if update_ctx:
        qc, kc, vc, zac, uc, bgc, cgc, zcc = jnp.split(hc @ w_in, SPLIT_POINTS, axis=-1)
    else:
        kc, vc = jnp.split(hc @ w_in[:, D_ATTN:3 * D_ATTN], 2, axis=-1)
    kc = rmsnorm(heads(kc), k_norm_g)
    vc = heads(vc)
    attn = neighbourhood_attention(q, k, heads(v), kc, vc, rpb) * jax.nn.silu(za)
    conv = gated_short_conv(u, bg, cg, zc, conv_w, conv_b)
    x_new = x + gate[:, None] * (jnp.concatenate([attn, conv], axis=-1) @ w_out)
    if update_ctx:
        qc = rmsnorm(heads(qc), q_norm_g)
        attn_c = context_attention(qc, kc, vc) * jax.nn.silu(zac)
        conv_c = gated_short_conv(uc, bgc, cgc, zcc, conv_w, conv_b)
        ctx_new = ctx + gate_c * (jnp.concatenate([attn_c, conv_c], axis=-1) @ w_out)
    else:
        ctx_new = ctx
    return x_new, ctx_new

def first_inputs(seed: int = 0) -> dict:
    key = jax.random.key(seed)
    ks = jax.random.split(key, 14)
    f32 = jnp.float32
    x = jax.random.normal(ks[0], (BATCH, SEQ, D_MODEL), f32)
    c = jax.random.normal(ks[1], (BATCH, D_MODEL), f32)
    ctx = jax.random.normal(ks[2], (BATCH, CTX_LEN, D_MODEL), f32)
    c_ctx = jax.random.normal(ks[3], (D_MODEL,), f32)
    w_ada = jax.random.normal(ks[4], (DEPTH, D_MODEL, 3 * D_MODEL), f32) * (0.5 * D_MODEL ** -0.5)
    b_ada = jax.random.normal(ks[5], (DEPTH, 3 * D_MODEL), f32) * 0.01
    norm_g = 1.0 + 0.1 * jax.random.normal(ks[6], (DEPTH, D_MODEL), f32)
    w_in = jax.random.normal(ks[7], (DEPTH, D_MODEL, D_IN), f32) * D_MODEL ** -0.5
    q_norm_g = 1.0 + 0.1 * jax.random.normal(ks[8], (DEPTH, HEAD_DIM), f32)
    k_norm_g = 1.0 + 0.1 * jax.random.normal(ks[9], (DEPTH, HEAD_DIM), f32)
    rpb = 0.1 * jax.random.normal(ks[10], (DEPTH, N_HEADS, 2 * WIN_H - 1, 2 * WIN_W - 1), f32)
    conv_w = jax.random.normal(ks[11], (DEPTH, CONV_K, D_CONV), f32) * CONV_K ** -0.5
    conv_b = 0.01 * jax.random.normal(ks[12], (DEPTH, D_CONV), f32)
    w_out = jax.random.normal(ks[13], (DEPTH, D_MIX, D_MODEL), f32) * D_MIX ** -0.5
    return {"x": x, "c": c, "ctx": ctx, "c_ctx": c_ctx, "w_ada": w_ada, "b_ada": b_ada,
            "norm_g": norm_g, "w_in": w_in, "q_norm_g": q_norm_g, "k_norm_g": k_norm_g,
            "rpb": rpb, "conv_w": conv_w, "conv_b": conv_b, "w_out": w_out}

def first_block(x, c, ctx, c_ctx, w_ada, b_ada, norm_g, w_in, q_norm_g, k_norm_g,
              rpb, conv_w, conv_b, w_out):
    for l in range(DEPTH):
        x, ctx = hybrid_layer(x, ctx, c, c_ctx, w_ada[l], b_ada[l], norm_g[l], w_in[l],
                              q_norm_g[l], k_norm_g[l], rpb[l], conv_w[l], conv_b[l], w_out[l],
                              update_ctx=(l < DEPTH - 1))
    return x


MEM_LEN = 256
N_DIFF_HEADS = 4
DIFF_V_DIM = 2 * HEAD_DIM
N_FOX_HEADS = 8
N_MEM_HEADS = 4
MEM_HEAD_DIM = D_MODEL // N_MEM_HEADS
D_FF = 4 * D_MODEL
N_BUCKETS = 32
MAX_DISTANCE = 128
Q_BLOCK = 128
EPS = 1e-6

DIFF_QK_W = N_DIFF_HEADS * 2 * HEAD_DIM
DIFF_V_W = N_DIFF_HEADS * DIFF_V_DIM
FOX_W = N_FOX_HEADS * HEAD_DIM
IN_SPLITS = [DIFF_QK_W, DIFF_QK_W, DIFF_V_W, FOX_W, FOX_W, FOX_W, N_FOX_HEADS, D_MODEL, D_MODEL]
IN_COLS = int(sum(IN_SPLITS))
IN_OFFSETS = [int(v) for v in np.cumsum(IN_SPLITS)[:-1]]


def _rmsnorm(x, g):
    xf = x.astype(jnp.float32)
    y = xf * lax.rsqrt(jnp.mean(xf * xf, axis=-1, keepdims=True) + EPS)
    return (y * g.astype(jnp.float32)).astype(x.dtype)

def _split_heads(t, n_heads):
    b, s, _ = t.shape
    return t.reshape(b, s, n_heads, -1).transpose(0, 2, 1, 3)

def _merge_blocks(o):
    nb, b, h, qb, d = o.shape
    return o.transpose(1, 0, 3, 2, 4).reshape(b, nb * qb, h, d)

def _t5_bucket(dist):
    dist = jnp.maximum(dist, 0)
    max_exact = N_BUCKETS // 2
    d = jnp.maximum(dist, 1).astype(jnp.float32)
    large = max_exact + (jnp.log(d / max_exact) / math.log(MAX_DISTANCE / max_exact)
                         * (N_BUCKETS - max_exact)).astype(jnp.int32)
    large = jnp.minimum(large, N_BUCKETS - 1)
    return jnp.where(dist < max_exact, dist, large)

def _hybrid_mixer(h, w_in, b_forget, lq1, lk1, lq2, lk2, g_subln, rel_bias,
                  w_diff_out, w_fox_out, w_o, lambda_init):
    b, s, _ = h.shape
    proj = h @ w_in
    qa, ka, va, qb, kb, vb, fl, ga, gb = jnp.split(proj, IN_OFFSETS, axis=-1)

    qa = _split_heads(qa, 2 * N_DIFF_HEADS).reshape(b, N_DIFF_HEADS, 2, s, HEAD_DIM)
    ka = _split_heads(ka, 2 * N_DIFF_HEADS).reshape(b, N_DIFF_HEADS, 2, s, HEAD_DIM)
    qa1, qa2 = qa[:, :, 0], qa[:, :, 1]
    ka1, ka2 = ka[:, :, 0], ka[:, :, 1]
    va = _split_heads(va, N_DIFF_HEADS)
    lam = (jnp.exp(jnp.sum(lq1.astype(jnp.float32) * lk1.astype(jnp.float32)))
           - jnp.exp(jnp.sum(lq2.astype(jnp.float32) * lk2.astype(jnp.float32)))
           + lambda_init)

    qb = _split_heads(qb, N_FOX_HEADS)
    kb = _split_heads(kb, N_FOX_HEADS)
    vb = _split_heads(vb, N_FOX_HEADS)
    log_f = jax.nn.log_sigmoid(fl.astype(jnp.float32) + b_forget.astype(jnp.float32))
    cum = jnp.cumsum(log_f, axis=1).transpose(0, 2, 1)

    scale = HEAD_DIM ** -0.5
    table = rel_bias.astype(jnp.float32)
    k_pos = jnp.arange(s)

    def block(i):
        q0 = i * Q_BLOCK
        q_pos = q0 + jnp.arange(Q_BLOCK)
        dist = q_pos[:, None] - k_pos[None, :]
        causal = dist >= 0
        rel = jnp.transpose(table[_t5_bucket(dist)], (2, 0, 1))
        sl = lambda t: lax.dynamic_slice_in_dim(t, q0, Q_BLOCK, axis=2)
        s1 = jnp.einsum('bhqd,bhkd->bhqk', sl(qa1), ka1).astype(jnp.float32) * scale + rel
        s2 = jnp.einsum('bhqd,bhkd->bhqk', sl(qa2), ka2).astype(jnp.float32) * scale + rel
        a1 = jax.nn.softmax(jnp.where(causal, s1, -jnp.inf), axis=-1)
        a2 = jax.nn.softmax(jnp.where(causal, s2, -jnp.inf), axis=-1)
        oa = jnp.einsum('bhqk,bhkd->bhqd', (a1 - lam * a2).astype(va.dtype), va)
        c_q = lax.dynamic_slice_in_dim(cum, q0, Q_BLOCK, axis=2)
        sb = (jnp.einsum('bhqd,bhkd->bhqk', sl(qb), kb).astype(jnp.float32) * scale
              + (c_q[..., None] - cum[:, :, None, :]))
        pb = jax.nn.softmax(jnp.where(causal, sb, -jnp.inf), axis=-1)
        ob = jnp.einsum('bhqk,bhkd->bhqd', pb.astype(vb.dtype), vb)
        return oa, ob

    oa, ob = lax.map(block, jnp.arange(s // Q_BLOCK))
    ya = _rmsnorm(_merge_blocks(oa), g_subln) * (1.0 - lambda_init)
    ya = ya.reshape(b, s, DIFF_V_W)
    yb = _merge_blocks(ob).reshape(b, s, FOX_W)
    merged = jax.nn.sigmoid(ga) * (ya @ w_diff_out) + jax.nn.sigmoid(gb) * (yb @ w_fox_out)
    return merged @ w_o

def _memory_cross_attention(h, mem_n, w_q, w_kv, w_o):
    b, s, _ = h.shape
    q = _split_heads(h @ w_q, N_MEM_HEADS)
    k, v = jnp.split(mem_n @ w_kv, 2, axis=-1)
    k = _split_heads(k, N_MEM_HEADS)
    v = _split_heads(v, N_MEM_HEADS)
    sc = jnp.einsum('bhqd,bhkd->bhqk', q, k).astype(jnp.float32) * (MEM_HEAD_DIM ** -0.5)
    p = jax.nn.softmax(sc, axis=-1).astype(v.dtype)
    o = jnp.einsum('bhqk,bhkd->bhqd', p, v).transpose(0, 2, 1, 3).reshape(b, s, D_MODEL)
    return o @ w_o

def _sq_relu_mlp(h, w1, w2):
    a = jax.nn.relu(h @ w1)
    return (a * a) @ w2

def second_inputs(seed: int = 0) -> dict:
    key = jax.random.key(seed)
    ks = jax.random.split(key, 24)
    n = lambda k, shape, s: jax.random.normal(k, shape, jnp.float32) * s
    gain = lambda k, shape: 1.0 + 0.02 * jax.random.normal(k, shape, jnp.float32)
    L = DEPTH
    return {
        "x": n(ks[0], (BATCH, SEQ, D_MODEL), 1.0),
        "mem": n(ks[1], (BATCH, MEM_LEN, D_MODEL), 1.0),
        "w_in": n(ks[2], (L, D_MODEL, IN_COLS), D_MODEL ** -0.5),
        "b_forget": 3.0 + n(ks[3], (L, N_FOX_HEADS), 1.0),
        "lambda_q1": n(ks[4], (L, HEAD_DIM), 0.1),
        "lambda_k1": n(ks[5], (L, HEAD_DIM), 0.1),
        "lambda_q2": n(ks[6], (L, HEAD_DIM), 0.1),
        "lambda_k2": n(ks[7], (L, HEAD_DIM), 0.1),
        "g_subln": gain(ks[8], (L, DIFF_V_DIM)),
        "rel_bias": n(ks[9], (N_BUCKETS, N_DIFF_HEADS), 0.5),
        "w_diff_out": n(ks[10], (L, DIFF_V_W, D_MODEL), DIFF_V_W ** -0.5),
        "w_fox_out": n(ks[11], (L, FOX_W, D_MODEL), FOX_W ** -0.5),
        "w_o": n(ks[12], (L, D_MODEL, D_MODEL), D_MODEL ** -0.5),
        "g_mix": gain(ks[13], (L, D_MODEL)),
        "g_mem_q": gain(ks[14], (L, D_MODEL)),
        "g_mem_kv": gain(ks[15], (L, D_MODEL)),
        "w_q_mem": n(ks[16], (L, D_MODEL, D_MODEL), D_MODEL ** -0.5),
        "w_kv_mem": n(ks[17], (L, D_MODEL, 2 * D_MODEL), D_MODEL ** -0.5),
        "w_o_mem": n(ks[18], (L, D_MODEL, D_MODEL), D_MODEL ** -0.5),
        "g_mlp": gain(ks[19], (L, D_MODEL)),
        "w1": n(ks[20], (L, D_MODEL, D_FF), D_MODEL ** -0.5),
        "w2": n(ks[21], (L, D_FF, D_MODEL), D_FF ** -0.5),
        "g_final": gain(ks[22], (D_MODEL,)),
    }

def second_block(x, mem, w_in, b_forget, lambda_q1, lambda_k1, lambda_q2, lambda_k2, g_subln,
              rel_bias, w_diff_out, w_fox_out, w_o, g_mix, g_mem_q, g_mem_kv, w_q_mem,
              w_kv_mem, w_o_mem, g_mlp, w1, w2, g_final):
    for l in range(DEPTH):
        lambda_init = 0.8 - 0.6 * math.exp(-0.3 * l)
        x = x + _hybrid_mixer(_rmsnorm(x, g_mix[l]), w_in[l], b_forget[l], lambda_q1[l],
                              lambda_k1[l], lambda_q2[l], lambda_k2[l], g_subln[l], rel_bias,
                              w_diff_out[l], w_fox_out[l], w_o[l], lambda_init)
        x = x + _memory_cross_attention(_rmsnorm(x, g_mem_q[l]), _rmsnorm(mem, g_mem_kv[l]),
                                        w_q_mem[l], w_kv_mem[l], w_o_mem[l])
        x = x + _sq_relu_mlp(_rmsnorm(x, g_mlp[l]), w1[l], w2[l])
    return _rmsnorm(x, g_final)


def setup_inputs(seed=0):
    out = dict(first_inputs(seed))
    for name, value in second_inputs(seed + 1).items():
        if name != "x":
            out[name + "_2"] = value
    return out


def reference(
    x, c, ctx, c_ctx, w_ada, b_ada, norm_g, w_in, q_norm_g, k_norm_g, rpb, conv_w, conv_b,
    w_out, mem_2, w_in_2, b_forget_2, lambda_q1_2, lambda_k1_2, lambda_q2_2, lambda_k2_2,
    g_subln_2, rel_bias_2, w_diff_out_2, w_fox_out_2, w_o_2, g_mix_2, g_mem_q_2, g_mem_kv_2,
    w_q_mem_2, w_kv_mem_2, w_o_mem_2, g_mlp_2, w1_2, w2_2, g_final_2,
):
    x = first_block(
        x, c, ctx, c_ctx, w_ada, b_ada, norm_g, w_in, q_norm_g, k_norm_g, rpb, conv_w, conv_b,
        w_out,
    )
    return second_block(
        x, mem_2, w_in_2, b_forget_2, lambda_q1_2, lambda_k1_2, lambda_q2_2, lambda_k2_2,
        g_subln_2, rel_bias_2, w_diff_out_2, w_fox_out_2, w_o_2, g_mix_2, g_mem_q_2, g_mem_kv_2,
        w_q_mem_2, w_kv_mem_2, w_o_mem_2, g_mlp_2, w1_2, w2_2, g_final_2,
    )


_drawn_inputs = setup_inputs


def setup_inputs(seed=0):
    import zlib

    import numpy as np

    out = dict(_drawn_inputs(seed))
    spreads = {}
    factors = {'ctx': 3.772,
     'b_ada': 5.406,
     'q_norm_g': 8.0,
     'k_norm_g': 8.0,
     'rpb': 8.0,
     'conv_b': 8.0,
     'lambda_q1_2': 8.0,
     'lambda_k1_2': 3.299,
     'lambda_q2_2': 2.8,
     'g_subln_2': 7.045,
     'g_mix_2': 3.27,
     'g_mem_q_2': 8.0,
     'g_mem_kv_2': 8.0,
     'g_mlp_2': 8.674,
     'g_final_2': 8.732}
    for name, (base, spread) in spreads.items():
        noise = np.random.default_rng([zlib.crc32(name.encode()), seed]).standard_normal(out[name].shape)
        drawn = base * np.exp(spread * noise) if base else spread * noise
        out[name] = __import__('jax').numpy.asarray(drawn.astype(out[name].dtype))
    for name, factor in factors.items():
        out[name] = (out[name] * factor).astype(out[name].dtype)
    return out
```

```python
import math
from contextlib import ExitStack

import numpy as np

import concourse.bass as bass
from concourse import mybir

F = mybir.dt.float32
R = mybir.dt.float32r
ALU = mybir.AluOpType
ACT = mybir.ActivationFunctionType
AX = mybir.AxisListType

P = 128
D = 1024
T = 1024
C = 256
KT = D // P
NT = T // P
CT = C // P
BANK = 512
HD = 64
GRID_W = 64
NEG = -1.0e30
EPS = 1e-6
BIG = 3.0e38
LAMBDA_INIT = 0.8 - 0.6 * math.exp(-0.3 * 0)

T_CTX = 0
T_ATT = T_CTX + 8
T_CONV = T_ATT + 16
T_OUT = T_CONV + 16
T_MIX = T_OUT + 8
T_MERGE = T_MIX + 24
T_WO = T_MERGE + 24
T_MEM = T_WO + 8
T_WOM = T_MEM + 24
T_MLP = T_WOM + 8
N_TILES = T_MLP + 64

FILL = {n: i for i, n in enumerate(
    ["x0", "ctx", "mix", "x1", "y", "merged", "mem", "x2", "memo", "x3"])}
NORM = {n: i for i, n in enumerate(["x0", "ctx", "x1", "mem", "x2", "x3", "final"])}
LINEAR = {"out": 0, "wo": 1, "wom": 2}

V_NORM, V_MIXG, V_MEMQ, V_MEMKV, V_MLPG, V_FIN, V_BADA = 0, 8, 16, 24, 32, 40, 48
V_QG, V_KG, V_CW, V_CB, V_SUB, V_BF = 72, 73, 74, 86, 90, 91
V_COLS = V_BF + 8
C_ID, C_TRI, C_ONE, C_BD, C_PERM = 0, 128, 256, 384, 512
C_COLS = 640

SEMS = """small_in lam_in ada_in0 ada_in1 ada_in2 ada_in3 ada_used x_in ctx_in mem_in rope_in wfl_in toeplitz
perm_ready raw_in0 raw_in1 w_hi w_split tile_done c_exp c_step ada_step const_ready sq_ready
acc_done ss_ready rms_ready rstd_ready scaled hi_ready lo_ready ck_ready ck_sq ck_ss ck_rms ck_rstd
ck_done cv_done qk_raw qk_sq qk_ss qk_rms qk_rstd qk_normed qk_plain_hi qk_plain_lo qk_perm qk_sin
qk_cos qk_roped qk_hi qk_lo v_hi v_lo za_exp za_step c_hi c_lo band_in0 band_in1 band_step na_scores
na_cmax na_logits na_probs na_pt na_pt_hi na_pt_lo na_pv na_inv na_out na_ot pair_done cv_u cv_exp
cv_gated cv_step conv_done lin_evac xres_in0 xres_in1 spilled fl_proj fl_z fl_exp fl_ln fl_logf
fl_cum fl_cumq fl_negc fl_out lam_step lam_exp df_hi df_lo strip_in df_scores df_logits df_probs
df_inv df_scaled df_comb df_pt df_pt_hi df_pt_lo df_pv df_out df_ms df_rstd df_normed df_ot df_done
fx_hi fx_lo fx_ck_in fx_cq fx_bias fx_bias_m fx_scores fx_logits fx_probs fx_pt fx_pt_hi fx_pt_lo
fx_pv fx_inv fx_out fx_ot fx_done mg_exp mg_step mg_done mm_hi mm_lo mm_scores mm_max mm_probs mm_pt
mm_pt_hi mm_pt_lo mm_pv mm_inv mm_out mm_ot mm_done a_relu a_sq a_hi a_lo mlp_acc y_ready y_out
seq_act seq_dve seq_pool seq_pe""".split()


def program(nc, x_t, ctx_t, mem_t, cond_t, small, lam4, consts, rope, masks, rpb_pad, rel_rows,
            w_fl, w_ada, w_stream, y_t):
    ctx = ExitStack()
    with ctx:
        S = {n: ctx.enter_context(nc.semaphore(n)) for n in SEMS}

        def alloc(stack, name, shape, dt=F):
            return stack.enter_context(nc.sbuf_tensor(name, shape, dt))

        vec = alloc(ctx, "vec", [P, V_COLS])
        con = alloc(ctx, "con", [P, C_COLS])
        mod = alloc(ctx, "mod", [P, 24, 2])
        gs = alloc(ctx, "gs", [P, KT, 2])
        eps = alloc(ctx, "eps", [P, 1])
        one = alloc(ctx, "one", [P, 1])
        qg8 = alloc(ctx, "qg8", [P, 1])
        subg = alloc(ctx, "subg", [P, 1])
        nm = alloc(ctx, "nm", [P, 4])
        cm = alloc(ctx, "cm", [P, 2])
        rsum = alloc(ctx, "rsum", [P, 4])
        rinv = alloc(ctx, "rinv", [P, 4])
        act_hi = alloc(ctx, "act_hi", [P, KT, T], R)
        act_lo = alloc(ctx, "act_lo", [P, KT, T], R)
        res = alloc(ctx, "res", [P, KT, T])
        raw = alloc(ctx, "raw", [P, 2, KT, P])
        w_hi = alloc(ctx, "w_hi", [P, 2, KT, P], R)
        w_lo = alloc(ctx, "w_lo", [P, 2, KT, P], R)
        stage = alloc(ctx, "stage", [P, 2, T])
        ps = ctx.enter_context(nc.psum_tensor("ps", [P, 8 * BANK], F))

        ident = con[:, C_ID:C_ID + P]
        tri = con[:, C_TRI:C_TRI + P]
        ones = con[:, C_ONE:C_ONE + P]
        bd64 = con[:, C_BD:C_BD + P]

        st = ExitStack()
        ADA_R = 12
        ada = alloc(st, "ada", [P, ADA_R, KT, P])
        cond = alloc(st, "cond", [P, KT, 2])
        cexp = alloc(st, "cexp", [P, KT, 2])
        st.close()

        st1 = ExitStack()
        kcF = alloc(st1, "kcF", [P, 4, C])
        vcF = alloc(st1, "vcF", [P, CT, 512])
        perm = alloc(st1, "perm", [P, P], R)
        st = ExitStack()
        hc_hi = alloc(st, "hc_hi", [P, KT, C], R)
        hc_lo = alloc(st, "hc_lo", [P, KT, C], R)
        ctxF = alloc(st, "ctxF", [P, KT, C])
        ksq = alloc(st, "ksq", [P, C])
        krs = alloc(st, "krs", [P, C])
        kraw = alloc(st, "kraw", [P, C])
        accc = alloc(st, "accc", [P, C])
        rsc = alloc(st, "rsc", [P, C])
        acc0b = alloc(st, "acc0b", [P, T])
        rs0b = alloc(st, "rs0b", [P, T])
        st.close()
        qp_hi = alloc(st1, "qp_hi", [P, T], R)
        qp_lo = alloc(st1, "qp_lo", [P, T], R)
        qr_hi = alloc(st1, "qr_hi", [P, T], R)
        qr_lo = alloc(st1, "qr_lo", [P, T], R)
        kr_hi = alloc(st1, "kr_hi", [P, T], R)
        kr_lo = alloc(st1, "kr_lo", [P, T], R)
        v_hi = alloc(st1, "v_hi", [P, NT, P], R)
        v_lo = alloc(st1, "v_lo", [P, NT, P], R)
        kc_hi = alloc(st1, "kc_hi", [P, C], R)
        kc_lo = alloc(st1, "kc_lo", [P, C], R)
        vc_hi = alloc(st1, "vc_hi", [P, CT, P], R)
        vc_lo = alloc(st1, "vc_lo", [P, CT, P], R)
        pt_hi = alloc(st1, "pt_hi", [P, 7 * P], R)
        pt_lo = alloc(st1, "pt_lo", [P, 7 * P], R)
        band_u = [alloc(st1, f"band_u{a}", [P, 14, GRID_W]) for a in range(2)]
        rope_sb = alloc(st1, "rope_sb", [P, 2, T])
        mask_sb = alloc(st1, "mask_sb", [P, 10, GRID_W])
        st1.close()
        tA, tB, tC, tD = (res[:, j, :] for j in (4, 5, 6, 7))
        band_m = [tC[:, 0:576], tA[:, 0:576]]
        o1 = tD.rearrange("p (t d) -> p t d", d=P)

        st = ExitStack()
        cv_a = alloc(st, "cv_a", [P, T])
        cv_b = alloc(st, "cv_b", [P, T])
        cv_y = alloc(st, "cv_y", [P, T])
        st.close()

        st4 = ExitStack()
        acc = alloc(st4, "acc", [P, T])
        rs = alloc(st4, "rs", [P, T])
        q_hi = alloc(st4, "q_hi", [P, T], R)
        q_lo = alloc(st4, "q_lo", [P, T], R)
        k_hi = alloc(st4, "k_hi", [P, T], R)
        k_lo = alloc(st4, "k_lo", [P, T], R)
        va_hi = alloc(st4, "va_hi", [P, NT, P], R)
        va_lo = alloc(st4, "va_lo", [P, NT, P], R)
        strip = alloc(st4, "strip", [P, T])
        pb = alloc(st4, "pb", [P, 2, T])
        p8_hi = alloc(st4, "p8_hi", [P, T], R)
        p8_lo = alloc(st4, "p8_lo", [P, T], R)
        o2 = alloc(st4, "o2", [P, NT, P])
        cumq = alloc(st4, "cumq", [P, NT, 8])
        cq2 = alloc(st4, "cq2", [P, NT, 2])
        nlam = alloc(st4, "nlam", [P, 1])
        ms8 = alloc(st4, "ms8", [P, NT])
        osq = alloc(st4, "osq", [P, P])
        st = ExitStack()
        wfl = alloc(st, "wfl", [P, KT, 8])
        wfl_hi = alloc(st, "wfl_hi", [P, KT, 8], R)
        wfl_lo = alloc(st, "wfl_lo", [P, KT, 8], R)
        zf = alloc(st, "zf", [P, NT, 8])
        ef = alloc(st, "ef", [P, NT, 8])
        logf = alloc(st, "logf", [P, NT, 8])
        negc = alloc(st, "negc", [8, T])
        lamv = alloc(st, "lamv", [P, 4, HD])
        lamp = alloc(st, "lamp", [P, HD])
        lam2 = alloc(st, "lam2", [P, 2])
        st.close()
        bt = alloc(st4, "bt", [P, 2, T])
        nck = [alloc(st4, f"nck{a}", [P, T]) for a in range(2)]
        st4.close()

        st = ExitStack()
        y_hi = alloc(st, "y_hi", [P, KT, T], R)
        y_lo = alloc(st, "y_lo", [P, KT, T], R)
        g_a = alloc(st, "g_a", [P, T])
        g_b = alloc(st, "g_b", [P, T])
        st.close()

        st = ExitStack()
        acc2 = alloc(st, "acc2", [P, T])
        rs2 = alloc(st, "rs2", [P, T])
        memF = alloc(st, "memF", [P, KT, C])
        m_hi = alloc(st, "m_hi", [P, KT, C], R)
        m_lo = alloc(st, "m_lo", [P, KT, C], R)
        mq_hi = alloc(st, "mq_hi", [P, 2, T], R)
        mq_lo = alloc(st, "mq_lo", [P, 2, T], R)
        mk_hi = alloc(st, "mk_hi", [P, 2, C], R)
        mk_lo = alloc(st, "mk_lo", [P, 2, C], R)
        mv_hi = alloc(st, "mv_hi", [P, 2, C], R)
        mv_lo = alloc(st, "mv_lo", [P, 2, C], R)
        mp = alloc(st, "mp", [P, 2, C])
        mpt_hi = alloc(st, "mpt_hi", [P, 2, C], R)
        mpt_lo = alloc(st, "mpt_lo", [P, 2, C], R)
        mo = alloc(st, "mo", [P, NT, C])
        st.close()

        st = ExitStack()
        acc3 = alloc(st, "acc3", [P, T])
        rs3 = alloc(st, "rs3", [P, T])
        a_hi = alloc(st, "a_hi", [P, KT, T], R)
        a_lo = alloc(st, "a_lo", [P, KT, T], R)
        st.close()

        negc_dram = nc.dram_tensor("negc_dram", [8, T], F).ap()
        band_dram = nc.dram_tensor("band_dram", [8, P, 14, GRID_W], F).ap()
        strip_dram = nc.dram_tensor("strip_dram", [4, P, T], F).ap()
        spill = [nc.dram_tensor(f"spill{j}", [P, KT, T], F).ap() for j in range(2)]

        NB = {"x0": (res, T, act_hi, act_lo, acc0b, rs0b), "ctx": (ctxF, C, hc_hi, hc_lo, accc, rsc),
              "x1": (res, T, act_hi, act_lo, acc, rs), "mem": (memF, C, m_hi, m_lo, acc2, rs2),
              "x2": (res, T, act_hi, act_lo, acc2, rs2), "x3": (res, T, act_hi, act_lo, acc3, rs3),
              "final": (res, T, None, None, acc3, rs3)}
        GAIN = {"x1": V_MIXG, "mem": V_MEMKV, "x2": V_MEMQ, "x3": V_MLPG, "final": V_FIN}

        def gain(name, k):
            if name in ("x0", "ctx"):
                j = 0 if name == "x0" else 1
                return gs[:, k, j:j + 1]
            return vec[:, GAIN[name] + k:GAIN[name] + k + 1]

        def shift(name, k):
            if name in ("x0", "ctx"):
                j = 0 if name == "x0" else 1
                return mod[:, k, j:j + 1]
            return None

        def bank(b, c0=0, c1=BANK):
            return ps[:, b * BANK + c0:b * BANK + c1]

        def bcast(src, n):
            return bass.AP(src.tensor, src.offset, [[0, P], [1, n]])

        def window(qt):
            if qt < 2:
                return 0, 512, 6 - 2 * qt
            if qt >= 6:
                return 512, 512, 14 - 2 * qt
            return (qt - 2) * P, 576, None

        block = ctx.enter_context(nc.Block())

        @block.sync
        def _(sp):
            sp.dma_start(vec[:, :], small).then_inc(S["small_in"], 16)
            sp.dma_start(con[:, :], consts).then_inc(S["small_in"], 16)
            sp.dma_start(cond[:, :, :], cond_t).then_inc(S["small_in"], 16)
            for n in range(8):
                if n >= 4:
                    sp.wait_ge(S["ada_used"], 3 * (n - 4) + 3)
                j = 3 * n % ADA_R
                sp.dma_start(ada[:, j:j + 3, :, :],
                             w_ada[3 * n:3 * n + 3].rearrange("t p (k c) -> p t k c", k=KT)
                             ).then_inc(S[f"ada_in{n % 4}"], 16)
            for s in range(2):
                sp.dma_start(raw[:, s, :, :],
                             w_stream[s].rearrange("p (k c) -> p k c", k=KT)
                             ).then_inc(S[f"raw_in{s}"], 16)
            with sp.Fori(1, N_TILES // 2) as h:
                for s in range(2):
                    sp.wait_ge(S["w_split"], 2 * h + s - 1)
                    sp.dma_start(raw[:, s, :, :],
                                 w_stream[bass.ds(2 * h + s, 1)].rearrange("o p (k c) -> (o p) k c", k=KT)
                                 ).then_inc(S[f"raw_in{s}"], 16)
            for k in range(KT):
                sp.wait_ge(S["y_ready"], k + 1)
                sp.dma_start(y_t[:, k, :], res[:, k, :]).then_inc(S["y_out"], 16)
            sp.wait_ge(S["y_out"], 16 * KT)

        @block.gpsimd
        def _(pool):
            def split(h, s, free=True):
                pool.wait_ge(S[f"raw_in{s}"], 16 * h + 16)
                if free:
                    pool.wait_ge(S["tile_done"], 2 * h + s - 1)
                pool.sem_inc(S["seq_pool"], 1)
                nc.gpsimd.tensor_copy(w_hi[:, s, :, :], raw[:, s, :, :]).then_inc(S["w_hi"], 1)
                pool.wait_ge(S["w_hi"], 2 * h + s + 1)
                nc.gpsimd.tensor_tensor(w_lo[:, s, :, :], raw[:, s, :, :], w_hi[:, s, :, :].bitcast(F),
                                        ALU.subtract).then_inc(S["w_split"], 1)

            def split_range(first, n):
                with pool.Fori(first // 2, (first + n) // 2) as h:
                    split(h, 0)
                    split(h, 1)

            split(0, 0, free=False)
            split(0, 1, free=False)
            split_range(T_CTX + 2, 8)
            pool.wait_ge(S["rope_in"], 32)
            with pool.Fori(0, 4) as i:
                h0 = 2 * i + (T_ATT // 2)
                split(h0 + 1, 0)
                pool.wait_ge(S["qk_plain_lo"], 2 * i + 1)
                nc.gpsimd.tensor_tensor(tA, tA, rope_sb[:, 0, :], ALU.mult).then_inc(S["qk_cos"], 1)
                split(h0 + 1, 1)
                pool.wait_ge(S["qk_plain_lo"], 2 * i + 2)
                nc.gpsimd.tensor_tensor(tC, tC, rope_sb[:, 0, :], ALU.mult).then_inc(S["qk_cos"], 1)
                pool.wait_ge(S["qk_lo"], 2 * i + 2)
                for a in range(2):
                    pool.wait_ge(S[f"band_in{a}"], 16 * i + 16)
                    pool.sem_inc(S["seq_pool"], 1)
                    nc.gpsimd.tensor_tensor(band_m[a].rearrange("p (r c) -> p r c", c=GRID_W),
                                            band_u[a][:, 2:11, :], mask_sb[:, 0:9, :],
                                            ALU.add).then_inc(S["band_step"], 1)
                    pool.wait_ge(S["band_step"], 4 * i + 2 * a + 1)
                    nc.gpsimd.tensor_tensor(band_u[a][:, :, :], band_u[a][:, :, :],
                                            mask_sb[:, 9:10, :].to_broadcast([P, 14, GRID_W]),
                                            ALU.add).then_inc(S["band_step"], 1)
                split(h0 + 2, 0)
                split(h0 + 2, 1)
            split_range(T_CONV + 2, 16)
            split_range(T_OUT + 2, 8)
            with pool.Fori(0, 4) as i:
                h0 = 3 * i + (T_MIX // 2)
                split(h0 + 1, 0)
                split(h0 + 1, 1)
                split(h0 + 2, 0)
                for u in range(NT):
                    n = P * (u + 1)
                    pool.wait_ge(S["df_inv"], 16 * i + 2 * u + 2)
                    pool.sem_inc(S["seq_pool"], 1)
                    p2 = pb[:, u % 2, 0:n]
                    nc.gpsimd.tensor_scalar(out=p2, in0=p2, scalar1=rinv[:, 2 * (u % 2) + 1:2 * (u % 2) + 2],
                                            scalar2=None, op0=ALU.mult).then_inc(S["df_scaled"], 1)
                split(h0 + 2, 1)
                split(h0 + 3, 0)
                split(h0 + 3, 1)
                pool.wait_ge(S["fl_cumq"], 1)
                pool.wait_ge(S["fx_done"], i + 1)
                pool.sem_inc(S["seq_pool"], 1)
                nc.gpsimd.tensor_copy(cq2[:, :, :], cumq[:, :, bass.ds(2 * i, 2)]).then_inc(S["fx_cq"], 1)
                pool.wait_ge(S["fx_cq"], i + 1)
                for u in range(2 * NT):
                    a, qt = divmod(u, NT)
                    n = P * (qt + 1)
                    g = 16 * i + u
                    b = bt[:, u % 2, 0:n]
                    if qt == 0:
                        pool.wait_ge(S["fx_ck_in"], 32 * i + 32)
                    if u >= 2:
                        pool.wait_ge(S["fx_logits"], g - 1)
                    pool.sem_inc(S["seq_pool"], 1)
                    nc.gpsimd.tensor_scalar(out=b, in0=nck[a][:, 0:n], scalar1=cq2[:, qt, a:a + 1],
                                            scalar2=None, op0=ALU.add).then_inc(S["fx_bias"], 1)
                    pool.wait_ge(S["fx_bias"], g + 1)
                    pool.sem_inc(S["seq_pool"], 1)
                    dg = bt[:, u % 2, n - P:n]
                    nc.gpsimd.affine_select(out=dg, in_=dg, compare_op=ALU.is_ge, fill=NEG, base=0,
                                            pattern=[[-1, P]], channel_multiplier=1
                                            ).then_inc(S["fx_bias_m"], 1)
            split_range(T_MERGE + 2, 24)
            split_range(T_WO + 2, 8)
            split_range(T_MEM + 2, 24)
            split_range(T_WOM + 2, 8)
            split_range(T_MLP + 2, 62)

        @block.scalar
        def _(act):
            def note():
                act.sem_inc(S["seq_act"], 1)

            def norm_squares(name):
                src, w = NB[name][0:2]
                r = NORM[name]
                for k in range(KT):
                    if 8 * r + k >= 2:
                        act.wait_ge(S["acc_done"], 8 * r + k - 1)
                    nc.scalar.activation(stage[:, k % 2, 0:w], src[:, k, :], ACT.Square
                                         ).then_inc(S["sq_ready"], 1)
                act.wait_ge(S["ss_ready"], r + 1)
                nc.scalar.activation(NB[name][5][:, 0:w], ps[:, 2 * BANK:2 * BANK + w], ACT.Sqrt,
                                     bias=eps[:, 0:1], scale=1.0 / D).then_inc(S["rms_ready"], 1)

            def norm_hi(name):
                r, f = NORM[name], FILL[name]
                w, hi = NB[name][1:3]
                for k in range(KT):
                    act.wait_ge(S["scaled"], 8 * r + k + 1)
                    if shift(name, k) is None:
                        nc.scalar.activation(hi[:, k, :], stage[:, k % 2, 0:w], ACT.Copy
                                             ).then_inc(S["hi_ready"], 1)
                    else:
                        nc.scalar.activation(hi[:, k, :], stage[:, k % 2, 0:w], ACT.Identity,
                                             bias=shift(name, k)).then_inc(S["hi_ready"], 1)

            def split_hi(hi):
                for k in range(KT):
                    nc.scalar.activation(hi[:, k, :], res[:, k, :], ACT.Copy).then_inc(S["hi_ready"], 1)

            act.dma_start(res[:, :, :], x_t).then_inc(S["x_in"], 16)
            act.wait_ge(S["small_in"], 48)
            nc.scalar.activation(cexp[:, :, :], cond[:, :, :], ACT.Exp, scale=-1.0).then_inc(S["c_exp"], 1)
            for h in range(8):
                for qa in range(2):
                    src = bass.AP(rpb_pad.tensor, h * 15 * 127 + (1 - qa) * 127 + 63,
                                  [[127, 14], [-1, GRID_W], [1, GRID_W]])
                    act.dma_start(band_dram[h, 64 * qa:64 * qa + 64].rearrange("q j c -> j q c"), src
                                  ).then_inc(S["toeplitz"], 16)
            src = bass.AP(rel_rows.tensor, P - 1, [[T + P - 1, 4], [-1, P], [1, T]])
            act.dma_start(strip_dram, src).then_inc(S["toeplitz"], 16)
            act.wait_ge(S["x_in"], 16)
            act.wait_ge(S["const_ready"], 1)
            norm_squares("x0")
            act.dma_start(ctxF[:, :, :], ctx_t).then_inc(S["ctx_in"], 16)
            nc.scalar.activation(perm[:, :], con[:, C_PERM:C_PERM + P], ACT.Copy).then_inc(S["perm_ready"], 1)
            norm_hi("x0")
            act.wait_ge(S["ctx_in"], 16)
            act.wait_ge(S["lo_ready"], 8 * FILL["x0"] + 8)
            norm_squares("ctx")
            norm_hi("ctx")
            with act.Fori(0, 4) as j:
                act.wait_ge(S["tile_done"], j + (T_CTX + 1))
                act.wait_ge(S["ck_done"], j + 1)
                nc.scalar.activation(kraw[:, :], bank(0, 0, C), ACT.Copy).then_inc(S["ck_ready"], 1)
                nc.scalar.activation(ksq[:, :], bank(0, 0, C), ACT.Square).then_inc(S["ck_sq"], 1)
                act.wait_ge(S["ck_ss"], j + 1)
                nc.scalar.activation(krs[:, :], bank(1, 0, C), ACT.Sqrt, bias=eps[:, 0:1],
                                     scale=1.0 / HD).then_inc(S["ck_rms"], 1)
            act.wait_ge(S["tile_done"], T_CTX + 8)
            act.dma_start(rope_sb[:, :, :], rope).then_inc(S["rope_in"], 16)
            act.dma_start(mask_sb[:, :, :], masks).then_inc(S["rope_in"], 16)

            act.wait_ge(S["toeplitz"], 16 * 17)
            with act.Fori(0, 4) as i:
                t0 = 4 * i + T_ATT
                act.wait_ge(S["pair_done"], i + 1)
                for a in range(2):
                    act.dma_start(band_u[a][:, :, :], band_dram[bass.ds(2 * i + a, 1)].rearrange(
                        "o p j c -> (o p) j c")).then_inc(S[f"band_in{a}"], 16)
                for n, (full, sq, b0) in enumerate(((tA, tB, 0), (tC, tD, 2))):
                    act.wait_ge(S["tile_done"], t0 + n + 1)
                    nc.scalar.activation(full, ps[:, b0 * BANK:(b0 + 2) * BANK], ACT.Copy
                                         ).then_inc(S["qk_raw"], 1)
                    nc.scalar.activation(sq, ps[:, b0 * BANK:(b0 + 2) * BANK], ACT.Square
                                         ).then_inc(S["qk_sq"], 1)
                nc.scalar.activation(kc_hi[:, :], kcF[:, bass.ds(i, 1), :].rearrange("p o c -> p (o c)"),
                                     ACT.Copy).then_inc(S["c_hi"], 1)
                nc.scalar.activation(vc_hi[:, :, :], vcF[:, :, bass.ds(P * i, P)],
                                     ACT.Copy).then_inc(S["c_hi"], 1)
                act.wait_ge(S["qk_ss"], 2 * i + 1)
                nc.scalar.activation(tB, ps[:, 0:2 * BANK], ACT.Sqrt, bias=eps[:, 0:1],
                                     scale=1.0 / HD).then_inc(S["qk_rms"], 1)
                act.wait_ge(S["qk_normed"], 2 * i + 1)
                nc.scalar.activation(qp_hi[:, :], tA, ACT.Copy).then_inc(S["qk_plain_hi"], 1)
                act.wait_ge(S["tile_done"], t0 + 3)
                nc.scalar.activation(v_hi[:, :, :], ps[:, 4 * BANK:6 * BANK].rearrange("p (t d) -> p t d", d=P),
                                     ACT.Copy).then_inc(S["v_hi"], 1)
                act.wait_ge(S["qk_ss"], 2 * i + 2)
                nc.scalar.activation(tD, ps[:, 2 * BANK:4 * BANK], ACT.Sqrt, bias=eps[:, 0:1],
                                     scale=1.0 / HD).then_inc(S["qk_rms"], 1)
                act.wait_ge(S["qk_normed"], 2 * i + 2)
                nc.scalar.activation(kr_hi[:, :], tC, ACT.Copy).then_inc(S["qk_plain_hi"], 1)
                act.wait_ge(S["qk_roped"], 2 * i + 1)
                nc.scalar.activation(qr_hi[:, :], tA, ACT.Copy).then_inc(S["qk_hi"], 1)
                act.wait_ge(S["tile_done"], t0 + 4)
                nc.scalar.activation(tB, ps[:, 6 * BANK:8 * BANK], ACT.Exp, scale=-1.0).then_inc(S["za_exp"], 1)
                act.wait_ge(S["qk_roped"], 2 * i + 2)
                nc.scalar.activation(kr_hi[:, :], tC, ACT.Copy).then_inc(S["qk_hi"], 1)

                def exp_unit(u):
                    a, qt = divmod(u, NT)
                    w = window(qt)[1] + C
                    act.wait_ge(S["na_logits"], 16 * i + (u + 1))
                    nc.scalar.activation(stage[:, u % 2, 0:w], stage[:, u % 2, 0:w], ACT.Exp,
                                         bias=nm[:, u % 2:u % 2 + 1], scale=-1.0,
                                         accum_out=rsum[:, u % 2:u % 2 + 1]).then_inc(S["na_probs"], 1)

                exp_unit(0)
                for u in range(16):
                    if u < 15:
                        exp_unit(u + 1)
                    w = 6 * P if window(u % NT)[1] == 512 else 7 * P
                    act.wait_ge(S["na_pt"], 16 * i + (u + 1))
                    if u > 0:
                        act.wait_ge(S["na_pv"], 16 * i + u)
                    nc.scalar.activation(pt_hi[:, 0:w], ps[:, 4 * BANK:4 * BANK + w], ACT.Copy
                                         ).then_inc(S["na_pt_hi"], 1)
            with act.Fori(0, 4) as i:
                t0 = 4 * i + T_CONV
                act.wait_ge(S["tile_done"], t0 + 1)
                act.wait_ge(S["conv_done"], i + 1)
                nc.scalar.activation(cv_a[:, :], ps[:, 0:2 * BANK], ACT.Copy).then_inc(S["cv_u"], 1)
                act.wait_ge(S["tile_done"], t0 + 4)
                nc.scalar.activation(cv_b[:, :], ps[:, 6 * BANK:8 * BANK], ACT.Exp, scale=-1.0
                                     ).then_inc(S["cv_exp"], 1)
            act.wait_ge(S["conv_done"], 5)
            act.wait_ge(S["tile_done"], T_OUT)
            split_hi(act_hi)

            def residual_loads(name, src):
                L = LINEAR[name]
                with act.Fori(0, 4) as i:
                    for s in range(2):
                        act.wait_ge(S["lin_evac"], 2 * i + (10 * L + s + 1))
                        act.dma_start(stage[:, s, :], src[:, bass.ds(2 * i + s, 1), :].rearrange("p o t -> p (o t)")
                                      ).then_inc(S[f"xres_in{s}"], 16)

            residual_loads("out", x_t)
            act.wait_ge(S["lin_evac"], 10)
            act.dma_start(wfl[:, :, :], w_fl).then_inc(S["wfl_in"], 16)
            act.dma_start(lamv[:, :, :], bcast(lam4, 4 * HD).rearrange("p (a d) -> p a d", a=4)
                          ).then_inc(S["lam_in"], 16)
            act.dma_start(spill[0], res[:, :, :]).then_inc(S["spilled"], 16)
            norm_squares("x1")
            act.wait_ge(S["wfl_in"], 16)
            nc.scalar.activation(wfl_hi[:, :, :], wfl[:, :, :], ACT.Copy).then_inc(S["fl_exp"], 1)
            norm_hi("x1")
            act.wait_ge(S["fl_z"], 3)
            nc.scalar.activation(ef[:, :, :], ef[:, :, :], ACT.Exp, scale=-1.0).then_inc(S["fl_exp"], 1)
            act.wait_ge(S["fl_exp"], 2)
            nc.scalar.activation(ef[:, :, :], ef[:, :, :], ACT.Ln, bias=one[:, 0:1]).then_inc(S["fl_ln"], 1)
            act.wait_ge(S["lam_step"], 2)
            nc.scalar.activation(lam2[:, :], lam2[:, :], ACT.Exp).then_inc(S["lam_exp"], 1)
            act.wait_ge(S["fl_negc"], 1)
            act.dma_start(negc_dram, negc[:, :]).then_inc(S["fl_out"], 16)
            act.wait_ge(S["fl_out"], 16)
            act.wait_ge(S["lam_step"], 4)
            with act.Fori(0, 4) as i:
                t0 = 6 * i + T_MIX
                act.wait_ge(S["df_done"], i + 1)
                act.dma_start(strip[:, :], strip_dram[bass.ds(i, 1)].rearrange("o p c -> (o p) c")
                              ).then_inc(S["strip_in"], 16)
                act.wait_ge(S["fx_done"], i + 1)
                for a in range(2):
                    row = negc_dram[bass.ds(2 * i + a, 1), :]
                    act.dma_start(nck[a][:, :], row.to_broadcast([P, T])).then_inc(S["fx_ck_in"], 16)

                def operands(base, count):
                    for n, (hi, sc) in enumerate(((q_hi, 0.125), (k_hi, 1.0), (va_hi, 1.0))):
                        act.wait_ge(S["tile_done"], t0 + base + n + 1)
                        src = ps[:, 2 * n * BANK:(2 * n + 2) * BANK]
                        if n == 2:
                            nc.scalar.activation(hi[:, :, :], src.rearrange("p (t d) -> p t d", d=P), ACT.Copy,
                                                 scale=sc).then_inc(S[count], 1)
                        else:
                            nc.scalar.activation(hi[:, :], src, ACT.Copy, scale=sc).then_inc(S[count], 1)

                operands(0, "df_hi")

                def exps(u):
                    n = P * (u + 1)
                    for m, buf in enumerate((stage, pb)):
                        c = 2 * (u % 2) + m
                        act.wait_ge(S["df_logits"], 16 * i + (2 * u + m + 1))
                        nc.scalar.activation(buf[:, u % 2, 0:n], buf[:, u % 2, 0:n], ACT.Exp,
                                             bias=nm[:, c:c + 1], scale=-1.0,
                                             accum_out=rsum[:, c:c + 1]).then_inc(S["df_probs"], 1)

                exps(0)
                for u in range(NT):
                    n = P * (u + 1)
                    if u + 1 < NT:
                        exps(u + 1)
                    act.wait_ge(S["df_pt"], 8 * i + (u + 1))
                    if u > 0:
                        act.wait_ge(S["df_pv"], 8 * i + u)
                    nc.scalar.activation(p8_hi[:, 0:n], ps[:, 4 * BANK:4 * BANK + n], ACT.Copy
                                         ).then_inc(S["df_pt_hi"], 1)
                    act.wait_ge(S["df_pv"], 8 * i + (u + 1))
                    nc.scalar.activation(o2[:, u, :], bank(6 + u % 2, 0, P), ACT.Copy).then_inc(S["df_out"], 1)
                    if u > 0:
                        act.wait_ge(S["df_out"], 16 * i + 2 * u)
                    nc.scalar.activation(osq[:, :], bank(6 + u % 2, 0, P), ACT.Square,
                                         accum_out=ms8[:, u:u + 1]).then_inc(S["df_out"], 1)
                act.wait_ge(S["df_out"], 16 * i + 16)
                nc.scalar.activation(ms8[:, :], ms8[:, :], ACT.Sqrt, bias=eps[:, 0:1], scale=1.0 / P
                                     ).then_inc(S["df_ms"], 1)
                operands(3, "fx_hi")

                def exp_fox(u):
                    n = P * (u % NT + 1)
                    act.wait_ge(S["fx_logits"], 16 * i + (u + 1))
                    nc.scalar.activation(stage[:, u % 2, 0:n], stage[:, u % 2, 0:n], ACT.Exp,
                                         bias=nm[:, u % 2:u % 2 + 1], scale=-1.0,
                                         accum_out=rsum[:, u % 2:u % 2 + 1]).then_inc(S["fx_probs"], 1)

                exp_fox(0)
                for u in range(2 * NT):
                    n = P * (u % NT + 1)
                    if u < 2 * NT - 1:
                        exp_fox(u + 1)
                    act.wait_ge(S["fx_pt"], 16 * i + (u + 1))
                    if u > 0:
                        act.wait_ge(S["fx_pv"], 16 * i + u)
                    nc.scalar.activation(p8_hi[:, 0:n], ps[:, 4 * BANK:4 * BANK + n], ACT.Copy
                                         ).then_inc(S["fx_pt_hi"], 1)
            act.wait_ge(S["fx_done"], 5)
            act.wait_ge(S["df_done"], 5)
            split_hi(y_hi)
            with act.Fori(0, 4) as i:
                for s in range(2):
                    t0 = 6 * i + (T_MERGE + 3 * s)
                    act.wait_ge(S["mg_done"], 2 * i + (s + 1))
                    for n, g in enumerate((g_a, g_b)):
                        act.wait_ge(S["tile_done"], t0 + n + 1)
                        nc.scalar.activation(g[:, :], ps[:, (4 + 2 * n) * BANK:(6 + 2 * n) * BANK], ACT.Exp,
                                             scale=-1.0).then_inc(S["mg_exp"], 1)
            act.wait_ge(S["mg_done"], 9)
            split_hi(act_hi)
            act.wait_ge(S["spilled"], 16)
            residual_loads("wo", spill[0])
            act.wait_ge(S["lin_evac"], 20)
            act.dma_start(memF[:, :, :], mem_t).then_inc(S["mem_in"], 16)
            act.dma_start(spill[1], res[:, :, :]).then_inc(S["spilled"], 16)
            act.wait_ge(S["mem_in"], 16)
            norm_squares("mem")
            norm_hi("mem")
            act.wait_ge(S["lo_ready"], 8 * FILL["mem"] + 8)
            norm_squares("x2")
            norm_hi("x2")
            act.wait_ge(S["spilled"], 32)
            with act.Fori(0, 4) as i:
                t0 = 6 * i + T_MEM
                for c in range(2):
                    act.wait_ge(S["tile_done"], t0 + c + 1)
                    nc.scalar.activation(mq_hi[:, c, :], ps[:, 2 * c * BANK:(2 * c + 2) * BANK], ACT.Copy,
                                         scale=0.0625).then_inc(S["mm_hi"], 1)
                for c in range(2):
                    act.wait_ge(S["tile_done"], t0 + c + 3)
                    nc.scalar.activation(mk_hi[:, c, :], bank(4 + c, 0, C), ACT.Copy).then_inc(S["mm_hi"], 1)
                act.wait_ge(S["tile_done"], t0 + 6)
                nc.scalar.activation(mv_hi[:, :, :], bank(6).rearrange("p (t d) -> p t d", d=C), ACT.Copy
                                     ).then_inc(S["mm_hi"], 1)

                def exp_mem(u):
                    act.wait_ge(S["mm_max"], 8 * i + (u + 1))
                    if u >= 2:
                        act.wait_ge(S["mm_pt"], 8 * i + (u - 1))
                    nc.scalar.activation(mp[:, u % 2, :], bank(u % 2, 0, C), ACT.Exp, bias=nm[:, u % 2:u % 2 + 1],
                                         accum_out=rsum[:, u % 2:u % 2 + 1]).then_inc(S["mm_probs"], 1)

                exp_mem(0)
                for u in range(NT):
                    if u + 1 < NT:
                        exp_mem(u + 1)
                    act.wait_ge(S["mm_pt"], 8 * i + (u + 1))
                    if u >= 2:
                        act.wait_ge(S["mm_pv"], 8 * i + (u - 1))
                    nc.scalar.activation(mpt_hi[:, u % 2, :], bank(2 + u % 2, 0, C), ACT.Copy
                                         ).then_inc(S["mm_pt_hi"], 1)
                act.wait_ge(S["mm_ot"], i + 1)
                note()
                nc.scalar.activation(res[:, bass.ds(2 * i, 2), :],
                                     ps[:, 0:4 * BANK].rearrange("p (c t) -> p c t", c=2), ACT.Copy
                                     ).then_inc(S["mm_done"], 1)
            act.wait_ge(S["mm_done"], 4)
            split_hi(act_hi)
            residual_loads("wom", spill[1])
            act.wait_ge(S["lin_evac"], 30)
            norm_squares("x3")
            norm_hi("x3")
            with act.Fori(0, 4) as b:
                with act.Fori(0, 4) as i:
                    for s in range(2):
                        n1 = 8 * b + 2 * i + s
                        act.wait_ge(S["tile_done"], 16 * b + 2 * i + (T_MLP + s + 1))
                        act.wait_ge(S["a_lo"], n1 + 1)
                        nc.scalar.activation(stage[:, s, :], ps[:, 2 * s * BANK:(2 * s + 2) * BANK], ACT.Relu
                                             ).then_inc(S["a_relu"], 1)
                        act.wait_ge(S["a_sq"], n1 + 1)
                        note()
                        nc.scalar.activation(a_hi[:, bass.ds(2 * i + s, 1), :].rearrange("p o t -> p (o t)"),
                                             stage[:, s, :], ACT.Copy).then_inc(S["a_hi"], 1)
            act.wait_ge(S["mlp_acc"], 34)
            norm_squares("final")

        @block.vector
        def _(dve):
            def note():
                dve.sem_inc(S["seq_dve"], 1)

            def norm_sum(name):
                src, w = NB[name][0:2]
                ac, r = NB[name][4], NORM[name]
                for k in range(KT):
                    dve.wait_ge(S["sq_ready"], 8 * r + k + 1)
                    if k == 0:
                        nc.vector.tensor_copy(ac[:, 0:w], stage[:, 0, 0:w]).then_inc(S["acc_done"], 1)
                    else:
                        dve.wait_ge(S["acc_done"], 8 * r + k)
                        nc.vector.tensor_tensor(ac[:, 0:w], ac[:, 0:w], stage[:, k % 2, 0:w], ALU.add
                                                ).then_inc(S["acc_done"], 1)
                dve.wait_ge(S["rms_ready"], r + 1)
                nc.vector.reciprocal(NB[name][5][:, 0:w], NB[name][5][:, 0:w]).then_inc(S["rstd_ready"], 1)
                dve.wait_ge(S["rstd_ready"], r + 1)

            def norm_scale(name):
                src, w, hi, lo, _, rstd = NB[name]
                r, f = NORM[name], FILL[name]

                def low(k):
                    dve.wait_ge(S["hi_ready"], 8 * f + k + 1)
                    sh = shift(name, k)
                    if sh is None:
                        nc.vector.tensor_tensor(lo[:, k, :], stage[:, k % 2, 0:w], hi[:, k, :].bitcast(F),
                                                ALU.subtract).then_inc(S["lo_ready"], 1)
                    else:
                        nc.vector.scalar_tensor_tensor(out=lo[:, k, :], in0=stage[:, k % 2, 0:w], scalar=sh,
                                                       in1=hi[:, k, :].bitcast(F), op0=ALU.add,
                                                       op1=ALU.subtract).then_inc(S["lo_ready"], 1)

                for k in range(KT):
                    if k >= 2:
                        dve.wait_ge(S["lo_ready"], 8 * f + k - 1)
                    nc.vector.scalar_tensor_tensor(out=stage[:, k % 2, 0:w], in0=src[:, k, :], scalar=gain(name, k),
                                                   in1=rstd[:, 0:w], op0=ALU.mult, op1=ALU.mult
                                                   ).then_inc(S["scaled"], 1)
                    if k >= 1:
                        low(k - 1)
                low(KT - 1)

            def split_lo(name, hi, lo):
                f = FILL[name]
                for k in range(KT):
                    dve.wait_ge(S["hi_ready"], 8 * f + k + 1)
                    nc.vector.tensor_tensor(lo[:, k, :], res[:, k, :], hi[:, k, :].bitcast(F), ALU.subtract
                                            ).then_inc(S["lo_ready"], 1)

            nc.vector.memset(eps[:, :], EPS).then_inc(S["const_ready"], 1)
            nc.vector.memset(one[:, :], 1.0)
            dve.wait_ge(S["small_in"], 48)
            nc.vector.tensor_scalar(out=qg8[:, :], in0=vec[:, V_QG:V_QG + 1], scalar1=0.125, scalar2=None,
                                    op0=ALU.mult).then_inc(S["const_ready"], 1)
            nc.vector.tensor_scalar(out=subg[:, :], in0=vec[:, V_SUB:V_SUB + 1], scalar1=1.0 - LAMBDA_INIT,
                                    scalar2=None, op0=ALU.mult).then_inc(S["const_ready"], 1)
            dve.wait_ge(S["c_exp"], 1)
            nc.vector.tensor_scalar(out=cexp[:, :, :], in0=cexp[:, :, :], scalar1=1.0, scalar2=None,
                                    op0=ALU.add).then_inc(S["c_step"], 1)
            dve.wait_ge(S["c_step"], 1)
            nc.vector.reciprocal(cexp[:, :, :], cexp[:, :, :]).then_inc(S["c_step"], 1)
            dve.wait_ge(S["c_step"], 2)
            nc.vector.tensor_tensor(cond[:, :, :], cond[:, :, :], cexp[:, :, :], ALU.mult).then_inc(S["c_step"], 1)
            dve.wait_ge(S["ada_used"], 24)
            nc.vector.tensor_tensor(mod[:, :, :], ps[:, 0:48].rearrange("p (m j) -> p m j", j=2),
                                    vec[:, V_BADA:V_BADA + 24].rearrange("p (m o) -> p m o", o=1)
                                    .to_broadcast([P, 24, 2]), ALU.add).then_inc(S["ada_step"], 1)
            dve.wait_ge(S["ada_step"], 1)
            nc.vector.scalar_tensor_tensor(out=gs[:, :, :], in0=mod[:, 8:16, :], scalar=1.0,
                                           in1=vec[:, V_NORM:V_NORM + 8].rearrange("p (m o) -> p m o", o=1)
                                           .to_broadcast([P, 8, 2]), op0=ALU.add, op1=ALU.mult
                                           ).then_inc(S["ada_step"], 1)
            dve.wait_ge(S["ada_step"], 2)
            norm_sum("x0")
            norm_scale("x0")
            norm_sum("ctx")
            norm_scale("ctx")
            dve.drain().then_inc(S["ck_done"], 1)
            with dve.Fori(0, 4) as j:
                dve.wait_ge(S["ck_rms"], j + 1)
                nc.vector.reciprocal(krs[:, :], krs[:, :]).then_inc(S["ck_rstd"], 1)
                dve.wait_ge(S["ck_rstd"], j + 1)
                nc.vector.scalar_tensor_tensor(out=kcF[:, bass.ds(j, 1), :].rearrange("p o c -> p (o c)"),
                                               in0=kraw[:, :], scalar=vec[:, V_KG:V_KG + 1], in1=krs[:, :],
                                               op0=ALU.mult, op1=ALU.mult).then_inc(S["ck_done"], 1)
            dve.drain().then_inc(S["cv_done"], 1)
            with dve.Fori(0, 4) as j:
                dve.wait_ge(S["tile_done"], j + (T_CTX + 5))
                nc.vector.tensor_copy(vcF[:, :, bass.ds(P * j, P)],
                                      bank(0, 0, C).rearrange("p (t d) -> p t d", d=P)).then_inc(S["cv_done"], 1)
            dve.wait_ge(S["rope_in"], 32)
            dve.drain().then_inc(S["pair_done"], 1)
            with dve.Fori(0, 4) as i:
                t0 = 4 * i + T_ATT

                def normed(n, full, sq, g):
                    dve.wait_ge(S["qk_rms"], 2 * i + (n + 1))
                    nc.vector.reciprocal(sq, sq).then_inc(S["qk_rstd"], 1)
                    dve.wait_ge(S["qk_rstd"], 2 * i + (n + 1))
                    nc.vector.scalar_tensor_tensor(out=full, in0=full, scalar=g, in1=sq, op0=ALU.mult,
                                                   op1=ALU.mult).then_inc(S["qk_normed"], 1)

                def plain_lo(n, full, hi, lo):
                    dve.wait_ge(S["qk_plain_hi"], 2 * i + (n + 1))
                    nc.vector.tensor_tensor(lo[:, :], full, hi[:, :].bitcast(F), ALU.subtract
                                            ).then_inc(S["qk_plain_lo"], 1)

                def roped(n, full, b0):
                    dve.wait_ge(S["qk_perm"], 2 * i + (n + 1))
                    nc.vector.tensor_tensor(stage[:, n, :], ps[:, b0 * BANK:(b0 + 2) * BANK], rope_sb[:, 1, :],
                                            ALU.mult).then_inc(S["qk_sin"], 1)
                    dve.wait_ge(S["qk_sin"], 2 * i + (n + 1))
                    dve.wait_ge(S["qk_cos"], 2 * i + (n + 1))
                    nc.vector.tensor_tensor(full, full, stage[:, n, :], ALU.add).then_inc(S["qk_roped"], 1)

                def rot_lo(n, full, hi, lo):
                    dve.wait_ge(S["qk_hi"], 2 * i + (n + 1))
                    nc.vector.tensor_tensor(lo[:, :], full, hi[:, :].bitcast(F), ALU.subtract
                                            ).then_inc(S["qk_lo"], 1)

                dve.wait_ge(S["c_hi"], 2 * i + 2)
                nc.vector.tensor_tensor(kc_lo[:, :], kcF[:, bass.ds(i, 1), :].rearrange("p o c -> p (o c)"),
                                        kc_hi[:, :].bitcast(F), ALU.subtract).then_inc(S["c_lo"], 1)
                nc.vector.tensor_tensor(vc_lo[:, :, :], vcF[:, :, bass.ds(P * i, P)],
                                        vc_hi[:, :, :].bitcast(F), ALU.subtract).then_inc(S["c_lo"], 1)
                normed(0, tA, tB, qg8[:, 0:1])
                plain_lo(0, tA, qp_hi, qp_lo)
                dve.wait_ge(S["v_hi"], i + 1)
                nc.vector.tensor_tensor(v_lo[:, :, :], ps[:, 4 * BANK:6 * BANK].rearrange("p (t d) -> p t d", d=P),
                                        v_hi[:, :, :].bitcast(F), ALU.subtract).then_inc(S["v_lo"], 1)
                normed(1, tC, tD, vec[:, V_KG:V_KG + 1])
                plain_lo(1, tC, kr_hi, kr_lo)
                roped(0, tA, 0)
                rot_lo(0, tA, qr_hi, qr_lo)
                roped(1, tC, 2)
                rot_lo(1, tC, kr_hi, kr_lo)
                dve.wait_ge(S["za_exp"], i + 1)
                nc.vector.tensor_scalar(out=tB, in0=tB, scalar1=1.0, scalar2=None, op0=ALU.add
                                        ).then_inc(S["za_step"], 1)
                dve.wait_ge(S["za_step"], 3 * i + 1)
                nc.vector.reciprocal(tB, tB).then_inc(S["za_step"], 1)
                dve.wait_ge(S["za_step"], 3 * i + 2)
                nc.vector.tensor_tensor(tB, ps[:, 6 * BANK:8 * BANK], tB, ALU.mult).then_inc(S["za_step"], 1)

                def logits(u):
                    a, qt = divmod(u, NT)
                    key0, nl, row0 = window(qt)
                    b0 = 2 * (u % 2) * BANK
                    g = 16 * i + u
                    dve.wait_ge(S["na_scores"], g + 1)
                    if u >= 2:
                        dve.wait_ge(S["na_pt"], g - 1)
                    elif u == 0:
                        dve.wait_ge(S["qk_roped"], 2 * i + 2)
                    if qt == 0:
                        dve.wait_ge(S["band_step"], 4 * i + 2 * a + 2)
                    nc.vector.tensor_scalar(out=stage[:, u % 2, nl:nl + C], in0=ps[:, b0 + nl:b0 + nl + C],
                                            scalar1=-1.0, scalar2=None, op0=ALU.mult, op1=ALU.min,
                                            accum_out=cm[:, u % 2:u % 2 + 1]).then_inc(S["na_cmax"], 1)
                    dve.wait_ge(S["na_cmax"], g + 1)
                    note()
                    if row0 is None:
                        band = band_m[a]
                    else:
                        band = band_u[a][:, row0:row0 + 8, :].rearrange("p r c -> p (r c)")
                    nc.vector.tensor_tensor_reduce(out=stage[:, u % 2, 0:nl], in0=ps[:, b0:b0 + nl], in1=band,
                                                   scale=-1.0, scalar=cm[:, u % 2:u % 2 + 1], op0=ALU.add,
                                                   op1=ALU.min, accum_out=nm[:, u % 2:u % 2 + 1]
                                                   ).then_inc(S["na_logits"], 1)

                logits(0)
                logits(1)
                for u in range(16):
                    a, qt = divmod(u, NT)
                    g = 16 * i + u
                    w = 6 * P if window(qt)[1] == 512 else 7 * P
                    dve.wait_ge(S["na_pt_hi"], g + 1)
                    nc.vector.tensor_tensor(pt_lo[:, 0:w], ps[:, 4 * BANK:4 * BANK + w], pt_hi[:, 0:w].bitcast(F),
                                            ALU.subtract).then_inc(S["na_pt_lo"], 1)
                    nc.vector.reciprocal(rinv[:, u % 2:u % 2 + 1], rsum[:, u % 2:u % 2 + 1]
                                         ).then_inc(S["na_inv"], 1)
                    if u + 2 < 16:
                        logits(u + 2)
                    dve.wait_ge(S["na_inv"], g + 1)
                    dve.wait_ge(S["na_pv"], g + 1)
                    nc.vector.tensor_scalar(out=o1[:, qt, a * HD:(a + 1) * HD], in0=bank(6 + u % 2, 0, HD),
                                            scalar1=rinv[:, u % 2:u % 2 + 1], scalar2=None, op0=ALU.mult
                                            ).then_inc(S["na_out"], 1)
                dve.wait_ge(S["na_ot"], i + 1)
                nc.vector.tensor_tensor(res[:, bass.ds(i, 1), :].rearrange("p o t -> p (o t)"),
                                        ps[:, 0:2 * BANK], tB, ALU.mult).then_inc(S["pair_done"], 1)
            dve.drain().then_inc(S["conv_done"], 1)
            with dve.Fori(0, 4) as i:
                t0 = 4 * i + T_CONV
                x_ = stage[:, 0, :]
                dve.wait_ge(S["cv_u"], i + 1)
                dve.wait_ge(S["tile_done"], t0 + 2)
                nc.vector.tensor_tensor(x_, ps[:, 2 * BANK:4 * BANK], cv_a[:, :], ALU.mult
                                        ).then_inc(S["cv_gated"], 1)
                dve.wait_ge(S["cv_gated"], i + 1)
                cw = [vec[:, bass.ds(V_CW + 4 * t + i, 1)] for t in range(3)]
                nc.vector.tensor_scalar(out=cv_y[:, :], in0=x_, scalar1=cw[1],
                                        scalar2=vec[:, bass.ds(V_CB + i, 1)], op0=ALU.mult, op1=ALU.add
                                        ).then_inc(S["cv_step"], 1)
                dve.wait_ge(S["cv_step"], 7 * i + 1)
                nc.vector.scalar_tensor_tensor(out=cv_y[:, 1:T], in0=stage[:, 0, 0:T - 1], scalar=cw[0],
                                               in1=cv_y[:, 1:T], op0=ALU.mult, op1=ALU.add
                                               ).then_inc(S["cv_step"], 1)
                dve.wait_ge(S["cv_step"], 7 * i + 2)
                nc.vector.scalar_tensor_tensor(out=cv_y[:, 0:T - 1], in0=stage[:, 0, 1:T], scalar=cw[2],
                                               in1=cv_y[:, 0:T - 1], op0=ALU.mult, op1=ALU.add
                                               ).then_inc(S["cv_step"], 1)
                dve.wait_ge(S["cv_step"], 7 * i + 3)
                dve.wait_ge(S["tile_done"], t0 + 3)
                nc.vector.tensor_tensor(cv_y[:, :], ps[:, 4 * BANK:6 * BANK], cv_y[:, :], ALU.mult
                                        ).then_inc(S["cv_step"], 1)
                dve.wait_ge(S["cv_exp"], i + 1)
                nc.vector.tensor_scalar(out=cv_b[:, :], in0=cv_b[:, :], scalar1=1.0, scalar2=None, op0=ALU.add
                                        ).then_inc(S["cv_step"], 1)
                dve.wait_ge(S["cv_step"], 7 * i + 5)
                nc.vector.reciprocal(cv_b[:, :], cv_b[:, :]).then_inc(S["cv_step"], 1)
                dve.wait_ge(S["cv_step"], 7 * i + 6)
                nc.vector.tensor_tensor(cv_b[:, :], ps[:, 6 * BANK:8 * BANK], cv_b[:, :], ALU.mult
                                        ).then_inc(S["cv_step"], 1)
                dve.wait_ge(S["cv_step"], 7 * i + 7)
                nc.vector.tensor_tensor(res[:, bass.ds(4 + i, 1), :].rearrange("p o t -> p (o t)"), cv_b[:, :],
                                        cv_y[:, :], ALU.mult).then_inc(S["conv_done"], 1)
            split_lo("mix", act_hi, act_lo)

            def residual(name, T0, gated):
                L = LINEAR[name]
                dve.drain().then_inc(S["lin_evac"], 2)
                with dve.Fori(0, 4) as i:
                    for s in range(2):
                        dve.wait_ge(S["tile_done"], 2 * i + (T0 + s + 1))
                        dve.wait_ge(S[f"xres_in{s}"], 16 * i + (64 * L + 16))
                        out = res[:, bass.ds(2 * i + s, 1), :].rearrange("p o t -> p (o t)")
                        src = ps[:, 2 * s * BANK:(2 * s + 2) * BANK]
                        if gated:
                            gate = mod[:, bass.ds(16 + 2 * i + s, 1), 0:1].rearrange("p a b -> p (a b)")
                            nc.vector.scalar_tensor_tensor(out=out, in0=src, scalar=gate, in1=stage[:, s, :],
                                                           op0=ALU.mult, op1=ALU.add).then_inc(S["lin_evac"], 1)
                        else:
                            nc.vector.tensor_tensor(out, src, stage[:, s, :], ALU.add).then_inc(S["lin_evac"], 1)

            residual("out", T_OUT, True)
            dve.wait_ge(S["lin_evac"], 10)
            norm_sum("x1")
            dve.wait_ge(S["fl_exp"], 1)
            nc.vector.tensor_tensor(wfl_lo[:, :, :], wfl[:, :, :], wfl_hi[:, :, :].bitcast(F), ALU.subtract
                                    ).then_inc(S["fl_z"], 1)
            norm_scale("x1")
            dve.wait_ge(S["fl_proj"], 1)
            nc.vector.tensor_tensor(zf[:, :, :], ps[:, 0:64].rearrange("p (t h) -> p t h", h=8),
                                    vec[:, V_BF:V_BF + 8].rearrange("p (o h) -> p o h", o=1)
                                    .to_broadcast([P, NT, 8]), ALU.add).then_inc(S["fl_z"], 1)
            dve.wait_ge(S["fl_z"], 2)
            nc.vector.scalar_tensor_tensor(out=ef[:, :, :], in0=zf[:, :, :], scalar=-1.0, in1=zf[:, :, :],
                                           op0=ALU.mult, op1=ALU.max).then_inc(S["fl_z"], 1)
            dve.wait_ge(S["fl_ln"], 1)
            nc.vector.scalar_tensor_tensor(out=logf[:, :, :], in0=zf[:, :, :], scalar=0.0, in1=ef[:, :, :],
                                           op0=ALU.min, op1=ALU.subtract).then_inc(S["fl_logf"], 1)
            dve.wait_ge(S["lam_in"], 16)
            for j in range(2):
                if j:
                    dve.wait_ge(S["lam_step"], 1)
                nc.vector.tensor_tensor_reduce(out=lamp[:, :], in0=lamv[:, 2 * j, :], in1=lamv[:, 2 * j + 1, :],
                                               scale=1.0, scalar=0.0, op0=ALU.mult, op1=ALU.add,
                                               accum_out=lam2[:, j:j + 1]).then_inc(S["lam_step"], 1)
            dve.wait_ge(S["lam_exp"], 1)
            nc.vector.tensor_scalar(out=nlam[:, :], in0=lam2[:, 1:2], scalar1=-LAMBDA_INIT, scalar2=None,
                                    op0=ALU.add).then_inc(S["lam_step"], 1)
            dve.wait_ge(S["lam_step"], 3)
            nc.vector.tensor_tensor(nlam[:, :], nlam[:, :], lam2[:, 0:1], ALU.subtract).then_inc(S["lam_step"], 1)
            dve.wait_ge(S["fl_cum"], 1)
            nc.vector.tensor_copy(cumq[:, :, :], bank(1, 0, 64).rearrange("p (t h) -> p t h", h=8)
                                  ).then_inc(S["fl_cumq"], 1)
            dve.wait_ge(S["fl_cum"], 2)
            nc.vector.tensor_scalar(out=negc[:, :], in0=ps[0:8, 2 * BANK:4 * BANK], scalar1=-1.0, scalar2=None,
                                    op0=ALU.mult).then_inc(S["fl_negc"], 1)
            dve.wait_ge(S["lam_step"], 4)
            dve.wait_ge(S["fl_out"], 16)
            dve.wait_ge(S["spilled"], 16)
            dve.drain().then_inc(S["df_done"], 1)
            dve.drain().then_inc(S["fx_done"], 1)
            with dve.Fori(0, 4) as i:
                t0 = 6 * i + T_MIX

                def low_parts(hi_sem, lo_sem):
                    for n, (hi, lo, sc) in enumerate(((q_hi, q_lo, 0.125), (k_hi, k_lo, 1.0), (va_hi, va_lo, 1.0))):
                        dve.wait_ge(S[hi_sem], 3 * i + (n + 1))
                        src = ps[:, 2 * n * BANK:(2 * n + 2) * BANK]
                        if n == 0:
                            nc.vector.scalar_tensor_tensor(out=lo[:, :], in0=src, scalar=sc,
                                                           in1=hi[:, :].bitcast(F), op0=ALU.mult,
                                                           op1=ALU.subtract).then_inc(S[lo_sem], 1)
                        elif n == 1:
                            nc.vector.tensor_tensor(lo[:, :], src, hi[:, :].bitcast(F), ALU.subtract
                                                    ).then_inc(S[lo_sem], 1)
                        else:
                            nc.vector.tensor_tensor(lo[:, :, :], src.rearrange("p (t d) -> p t d", d=P),
                                                    hi[:, :, :].bitcast(F), ALU.subtract).then_inc(S[lo_sem], 1)

                low_parts("df_hi", "df_lo")
                dve.wait_ge(S["strip_in"], 16 * i + 16)

                def logits(u):
                    n = P * (u + 1)
                    for m, buf in enumerate((stage, pb)):
                        c = 2 * (u % 2) + m
                        dve.wait_ge(S["df_scores"], 16 * i + (2 * u + m + 1))
                        if u >= 2:
                            dve.wait_ge(S["df_pt"], 8 * i + (u - 1))
                        note()
                        nc.vector.tensor_tensor_reduce(out=buf[:, u % 2, 0:n], in0=ps[:, 2 * m * BANK:2 * m * BANK + n],
                                                       in1=strip[:, T - n:T], scale=-1.0, scalar=BIG,
                                                       op0=ALU.add, op1=ALU.min, accum_out=nm[:, c:c + 1]
                                                       ).then_inc(S["df_logits"], 1)

                logits(0)
                for u in range(NT):
                    n = P * (u + 1)
                    g = 8 * i + u
                    c = 2 * (u % 2)
                    dve.wait_ge(S["df_probs"], 16 * i + (2 * u + 2))
                    if u >= 2:
                        dve.wait_ge(S["df_comb"], g - 1)
                    nc.vector.reciprocal(rinv[:, c:c + 2], rsum[:, c:c + 2]).then_inc(S["df_inv"], 1)
                    dve.wait_ge(S["df_inv"], 16 * i + (2 * u + 1))
                    nc.vector.tensor_scalar(out=rinv[:, c + 1:c + 2], in0=rinv[:, c + 1:c + 2], scalar1=nlam[:, 0:1],
                                            scalar2=None, op0=ALU.mult).then_inc(S["df_inv"], 1)
                    dve.wait_ge(S["df_scaled"], g + 1)
                    nc.vector.scalar_tensor_tensor(out=stage[:, u % 2, 0:n], in0=stage[:, u % 2, 0:n],
                                                   scalar=rinv[:, c:c + 1], in1=pb[:, u % 2, 0:n], op0=ALU.mult,
                                                   op1=ALU.add).then_inc(S["df_comb"], 1)
                    if u + 1 < NT:
                        logits(u + 1)
                    dve.wait_ge(S["df_pt_hi"], g + 1)
                    nc.vector.tensor_tensor(p8_lo[:, 0:n], ps[:, 4 * BANK:4 * BANK + n], p8_hi[:, 0:n].bitcast(F),
                                            ALU.subtract).then_inc(S["df_pt_lo"], 1)
                dve.wait_ge(S["df_ms"], i + 1)
                nc.vector.reciprocal(ms8[:, :], ms8[:, :]).then_inc(S["df_rstd"], 1)
                dve.wait_ge(S["df_rstd"], i + 1)
                nc.vector.tensor_tensor(o2[:, :, :], o2[:, :, :],
                                        ms8[:, :].rearrange("p (t o) -> p t o", o=1).to_broadcast([P, NT, P]),
                                        ALU.mult).then_inc(S["df_normed"], 1)
                dve.wait_ge(S["df_ot"], i + 1)
                nc.vector.tensor_scalar(out=res[:, bass.ds(i, 1), :].rearrange("p o t -> p (o t)"),
                                        in0=ps[:, 6 * BANK:8 * BANK], scalar1=subg[:, 0:1], scalar2=None,
                                        op0=ALU.mult).then_inc(S["df_done"], 1)
                low_parts("fx_hi", "fx_lo")

                def fox_logits(u):
                    n = P * (u % NT + 1)
                    g = 16 * i + u
                    b0 = 2 * (u % 2) * BANK
                    dve.wait_ge(S["fx_scores"], g + 1)
                    dve.wait_ge(S["fx_bias_m"], g + 1)
                    if u >= 2:
                        dve.wait_ge(S["fx_pt"], g - 1)
                    note()
                    nc.vector.tensor_tensor_reduce(out=stage[:, u % 2, 0:n], in0=ps[:, b0:b0 + n],
                                                   in1=bt[:, u % 2, 0:n], scale=-1.0, scalar=BIG, op0=ALU.add,
                                                   op1=ALU.min, accum_out=nm[:, u % 2:u % 2 + 1]
                                                   ).then_inc(S["fx_logits"], 1)

                fox_logits(0)
                fox_logits(1)
                for u in range(2 * NT):
                    a, qt = divmod(u, NT)
                    n = P * (qt + 1)
                    g = 16 * i + u
                    dve.wait_ge(S["fx_pt_hi"], g + 1)
                    nc.vector.tensor_tensor(p8_lo[:, 0:n], ps[:, 4 * BANK:4 * BANK + n], p8_hi[:, 0:n].bitcast(F),
                                            ALU.subtract).then_inc(S["fx_pt_lo"], 1)
                    nc.vector.reciprocal(rinv[:, u % 2:u % 2 + 1], rsum[:, u % 2:u % 2 + 1]
                                         ).then_inc(S["fx_inv"], 1)
                    if u + 2 < 2 * NT:
                        fox_logits(u + 2)
                    dve.wait_ge(S["fx_inv"], g + 1)
                    dve.wait_ge(S["fx_pv"], g + 1)
                    nc.vector.tensor_scalar(out=o2[:, qt, a * HD:(a + 1) * HD], in0=bank(6 + u % 2, 0, HD),
                                            scalar1=rinv[:, u % 2:u % 2 + 1], scalar2=None, op0=ALU.mult
                                            ).then_inc(S["fx_out"], 1)
                dve.wait_ge(S["fx_ot"], i + 1)
                nc.vector.tensor_copy(res[:, bass.ds(4 + i, 1), :].rearrange("p o t -> p (o t)"),
                                      ps[:, 0:2 * BANK]).then_inc(S["fx_done"], 1)
            split_lo("y", y_hi, y_lo)
            dve.drain().then_inc(S["mg_done"], 1)
            with dve.Fori(0, 4) as i:
                for s in range(2):
                    m = 2 * i + s
                    t0 = 6 * i + (T_MERGE + 3 * s)
                    for n, g in enumerate((g_a, g_b)):
                        dve.wait_ge(S["mg_exp"], 2 * m + (n + 1))
                        nc.vector.tensor_scalar(out=g[:, :], in0=g[:, :], scalar1=1.0, scalar2=None, op0=ALU.add
                                                ).then_inc(S["mg_step"], 1)
                        dve.wait_ge(S["mg_step"], 6 * m + (2 * n + 1))
                        nc.vector.reciprocal(g[:, :], g[:, :]).then_inc(S["mg_step"], 1)
                    dve.wait_ge(S["tile_done"], t0 + 3)
                    for n, g in enumerate((g_a, g_b)):
                        dve.wait_ge(S["mg_step"], 6 * m + (3 + n))
                        if n:
                            dve.wait_ge(S["mg_step"], 6 * m + 4)
                        nc.vector.tensor_tensor(g[:, :], ps[:, 2 * n * BANK:(2 * n + 2) * BANK], g[:, :], ALU.mult
                                                ).then_inc(S["mg_step"], 1)
                    dve.wait_ge(S["mg_step"], 6 * m + 6)
                    nc.vector.tensor_tensor(res[:, bass.ds(m, 1), :].rearrange("p o t -> p (o t)"), g_a[:, :],
                                            g_b[:, :], ALU.add).then_inc(S["mg_done"], 1)
            split_lo("merged", act_hi, act_lo)
            residual("wo", T_WO, False)
            dve.wait_ge(S["lin_evac"], 20)
            norm_sum("mem")
            norm_scale("mem")
            norm_sum("x2")
            norm_scale("x2")
            dve.drain().then_inc(S["mm_out"], 1)
            with dve.Fori(0, 4) as i:
                t0 = 6 * i + T_MEM
                for c in range(2):
                    dve.wait_ge(S["mm_hi"], 5 * i + (c + 1))
                    nc.vector.scalar_tensor_tensor(out=mq_lo[:, c, :], in0=ps[:, 2 * c * BANK:(2 * c + 2) * BANK],
                                                   scalar=0.0625, in1=mq_hi[:, c, :].bitcast(F), op0=ALU.mult,
                                                   op1=ALU.subtract).then_inc(S["mm_lo"], 1)
                for c in range(2):
                    dve.wait_ge(S["mm_hi"], 5 * i + (c + 3))
                    nc.vector.tensor_tensor(mk_lo[:, c, :], bank(4 + c, 0, C), mk_hi[:, c, :].bitcast(F),
                                            ALU.subtract).then_inc(S["mm_lo"], 1)
                dve.wait_ge(S["mm_hi"], 5 * i + 5)
                nc.vector.tensor_tensor(mv_lo[:, :, :], bank(6).rearrange("p (t d) -> p t d", d=C),
                                        mv_hi[:, :, :].bitcast(F), ALU.subtract).then_inc(S["mm_lo"], 1)

                def row_max(u):
                    dve.wait_ge(S["mm_scores"], 8 * i + (u + 1))
                    if u >= 2:
                        dve.wait_ge(S["mm_probs"], 8 * i + (u - 1))
                    nc.vector.tensor_reduce(out=nm[:, u % 2:u % 2 + 1], in_=bank(u % 2, 0, C), axis=AX.X,
                                            op=ALU.max, negate=True).then_inc(S["mm_max"], 1)

                row_max(0)
                row_max(1)
                for u in range(NT):
                    g = 8 * i + u
                    dve.wait_ge(S["mm_pt_hi"], g + 1)
                    nc.vector.tensor_tensor(mpt_lo[:, u % 2, :], bank(2 + u % 2, 0, C),
                                            mpt_hi[:, u % 2, :].bitcast(F), ALU.subtract
                                            ).then_inc(S["mm_pt_lo"], 1)
                    nc.vector.reciprocal(rinv[:, u % 2:u % 2 + 1], rsum[:, u % 2:u % 2 + 1]
                                         ).then_inc(S["mm_inv"], 1)
                    if u + 2 < NT:
                        row_max(u + 2)
                    dve.wait_ge(S["mm_inv"], g + 1)
                    dve.wait_ge(S["mm_pv"], g + 1)
                    nc.vector.tensor_scalar(out=mo[:, u, :], in0=bank(4 + u % 2, 0, C),
                                            scalar1=rinv[:, u % 2:u % 2 + 1], scalar2=None, op0=ALU.mult
                                            ).then_inc(S["mm_out"], 1)
            split_lo("memo", act_hi, act_lo)
            residual("wom", T_WOM, False)
            dve.wait_ge(S["lin_evac"], 30)
            norm_sum("x3")
            norm_scale("x3")
            dve.drain().then_inc(S["a_lo"], 2)
            dve.drain().then_inc(S["mlp_acc"], 2)
            with dve.Fori(0, 4) as b:
                with dve.Fori(0, 4) as i:
                    for s in range(2):
                        n1 = 8 * b + 2 * i + s
                        dve.wait_ge(S["a_relu"], n1 + 1)
                        nc.vector.tensor_tensor(stage[:, s, :], stage[:, s, :], stage[:, s, :], ALU.mult
                                                ).then_inc(S["a_sq"], 1)
                        dve.wait_ge(S["a_hi"], n1 + 1)
                        nc.vector.tensor_tensor(a_lo[:, bass.ds(2 * i + s, 1), :].rearrange("p o t -> p (o t)"),
                                                stage[:, s, :],
                                                a_hi[:, bass.ds(2 * i + s, 1), :].rearrange("p o t -> p (o t)")
                                                .bitcast(F), ALU.subtract).then_inc(S["a_lo"], 1)
                with dve.Fori(0, 4) as i:
                    for s in range(2):
                        dve.wait_ge(S["tile_done"], 16 * b + 2 * i + (T_MLP + 8 + s + 1))
                        out = res[:, bass.ds(2 * i + s, 1), :].rearrange("p o t -> p (o t)")
                        dve.wait_ge(S["mlp_acc"], 8 * b + 2)
                        nc.vector.tensor_tensor(out, ps[:, (4 + 2 * s) * BANK:(6 + 2 * s) * BANK], out, ALU.add
                                                ).then_inc(S["mlp_acc"], 1)
            dve.wait_ge(S["mlp_acc"], 34)
            norm_sum("final")
            for k in range(KT):
                nc.vector.scalar_tensor_tensor(out=res[:, k, :], in0=res[:, k, :], scalar=gain("final", k),
                                               in1=rs3[:, :], op0=ALU.mult, op1=ALU.mult).then_inc(S["y_ready"], 1)

        @block.tensor
        def _(pe):
            def mm3(out, wh, wl, xh, xl, start, stop):
                nc.tensor.matmul(out, wh, xh, start=start, stop=False)
                nc.tensor.matmul(out, wh, xl, start=False, stop=False)
                return nc.tensor.matmul(out, wl, xh, start=False, stop=stop)

            def project(s, b0, xh, xl, width, ks=range(KT)):
                for c in range(0, width, BANK):
                    n = min(BANK, width - c)
                    for k in ks:
                        last = mm3(ps[:, b0 * BANK + c:b0 * BANK + c + n], w_hi[:, s, k, :], w_lo[:, s, k, :],
                                   xh[:, k, c:c + n], xl[:, k, c:c + n], k == ks[0], k == ks[-1])
                return last

            def project_tok(s, out_of, xh, xl, nt):
                for t in range(nt):
                    for k in range(KT):
                        last = mm3(out_of(t), xh[:, k, t * P:(t + 1) * P], xl[:, k, t * P:(t + 1) * P],
                                   w_hi[:, s, k, :], w_lo[:, s, k, :], k == 0, k == KT - 1)
                return last

            def tile_ready(idx):
                pe.wait_ge(S["w_split"], idx + 1)

            def sum_squares(name):
                w, ac, r = NB[name][1], NB[name][4], NORM[name]
                pe.wait_ge(S["acc_done"], 8 * r + 8)
                if r:
                    pe.wait_ge(S["rms_ready"], r)
                for c in range(0, w, BANK):
                    n = min(BANK, w - c)
                    last = nc.tensor.matmul(ps[:, 2 * BANK + c:2 * BANK + c + n], ones, ac[:, c:c + n],
                                            start=True, stop=True)
                last.then_inc(S["ss_ready"], 1)

            pe.wait_ge(S["c_step"], 3)
            for t in range(24):
                n = t // 3
                pe.wait_ge(S[f"ada_in{n % 4}"], 16 * (n // 4) + 16)
                for k in range(KT):
                    last = nc.tensor.matmul(ps[:, 2 * t:2 * t + 2], ada[:, t % ADA_R, k, :], cond[:, k, :],
                                            start=(k == 0), stop=(k == KT - 1))
                last.then_inc(S["ada_used"], 1)
            sum_squares("x0")
            sum_squares("ctx")
            pe.wait_ge(S["lo_ready"], 8 * FILL["ctx"] + 8)
            with pe.Fori(0, 2) as i:
                for s in range(2):
                    j = 2 * i + s
                    tile_ready(2 * i + (T_CTX + s))
                    pe.wait_ge(S["ck_done"], j + 1)
                    project(s, 0, hc_hi, hc_lo, C).then_inc(S["tile_done"], 1)
                    pe.wait_ge(S["ck_sq"], j + 1)
                    nc.tensor.matmul(bank(1, 0, C), bd64, ksq[:, :], start=True, stop=True
                                     ).then_inc(S["ck_ss"], 1)
            pe.wait_ge(S["ck_done"], 5)
            with pe.Fori(0, 2) as i:
                for s in range(2):
                    tile_ready(2 * i + (T_CTX + 4 + s))
                    pe.wait_ge(S["cv_done"], 2 * i + (s + 1))
                    project_tok(s, lambda t: bank(0, t * P, (t + 1) * P), hc_hi, hc_lo, CT
                                ).then_inc(S["tile_done"], 1)
            with pe.Fori(0, 4) as i:
                t0 = 4 * i + T_ATT
                tile_ready(t0)
                pe.wait_ge(S["pair_done"], i + 1)
                project(0, 0, act_hi, act_lo, T).then_inc(S["tile_done"], 1)
                tile_ready(t0 + 1)
                project(1, 2, act_hi, act_lo, T).then_inc(S["tile_done"], 1)

                def head_ss(n, sq, b0):
                    pe.wait_ge(S["qk_sq"], 2 * i + (n + 1))
                    for c in range(2):
                        last = nc.tensor.matmul(bank(b0 + c), bd64, sq[:, c * BANK:(c + 1) * BANK],
                                                start=True, stop=True)
                    last.then_inc(S["qk_ss"], 1)

                def half_turn(n, hi, lo, b0):
                    pe.wait_ge(S["qk_plain_lo"], 2 * i + (n + 1))
                    for c in range(2):
                        nc.tensor.matmul(bank(b0 + c), perm[:, :], hi[:, c * BANK:(c + 1) * BANK],
                                         start=True, stop=False)
                        last = nc.tensor.matmul(bank(b0 + c), perm[:, :], lo[:, c * BANK:(c + 1) * BANK],
                                                start=False, stop=True)
                    last.then_inc(S["qk_perm"], 1)

                head_ss(0, tB, 0)
                tile_ready(t0 + 2)
                project_tok(0, lambda t: bank(4 + t // 4, (t % 4) * P, (t % 4 + 1) * P), act_hi, act_lo, NT
                            ).then_inc(S["tile_done"], 1)
                head_ss(1, tD, 2)
                half_turn(0, qp_hi, qp_lo, 0)
                tile_ready(t0 + 3)
                project(1, 6, act_hi, act_lo, T).then_inc(S["tile_done"], 1)
                half_turn(1, kr_hi, kr_lo, 2)

                def scores(u):
                    a, qt = divmod(u, NT)
                    key0, nl, _ = window(qt)
                    b0 = 2 * (u % 2) * BANK
                    h = slice(a * HD, (a + 1) * HD)
                    q = slice(qt * P, (qt + 1) * P)
                    if u == 0:
                        pe.wait_ge(S["qk_lo"], 2 * i + 2)
                        pe.wait_ge(S["c_lo"], 2 * i + 2)
                    if u >= 2:
                        pe.wait_ge(S["na_logits"], 16 * i + (u - 1))
                    for c in range(0, nl, BANK):
                        n = min(BANK, nl - c)
                        mm3(ps[:, b0 + c:b0 + c + n], qr_hi[h, q], qr_lo[h, q],
                            kr_hi[h, key0 + c:key0 + c + n], kr_lo[h, key0 + c:key0 + c + n], True, True)
                    mm3(ps[:, b0 + nl:b0 + nl + C], qp_hi[h, q], qp_lo[h, q], kc_hi[h, :], kc_lo[h, :],
                        True, True).then_inc(S["na_scores"], 1)

                scores(0)
                scores(1)
                for u in range(16):
                    a, qt = divmod(u, NT)
                    key0, nl, _ = window(qt)
                    g = 16 * i + u
                    lat = [(c, min(P, nl - c)) for c in range(0, nl, P)]
                    blocks = lat + [(nl, P), (nl + P, P)]
                    pe.wait_ge(S["na_probs"], g + 1)
                    if u > 0:
                        pe.wait_ge(S["na_pt_lo"], g)
                    else:
                        pe.wait_ge(S["v_lo"], i + 1)
                    for j, (c, n) in enumerate(blocks):
                        last = nc.tensor.transpose(ps[:, 4 * BANK + j * P:4 * BANK + (j + 1) * P],
                                                   stage[:, u % 2, c:c + P], ident)
                    last.then_inc(S["na_pt"], 1)
                    if u + 2 < 16:
                        scores(u + 2)
                    pe.wait_ge(S["na_pt_lo"], g + 1)
                    if u >= 2:
                        pe.wait_ge(S["na_out"], g - 1)
                    elif u == 0:
                        pe.wait_ge(S["za_step"], 3 * i + 3)
                    hv = slice(a * HD, (a + 1) * HD)
                    for j, (c, n) in enumerate(blocks):
                        if j < len(lat):
                            vh, vl = v_hi[0:n, key0 // P + j, hv], v_lo[0:n, key0 // P + j, hv]
                        else:
                            vh, vl = vc_hi[:, j - len(lat), hv], vc_lo[:, j - len(lat), hv]
                        last = mm3(bank(6 + u % 2, 0, HD), pt_hi[0:n, j * P:(j + 1) * P],
                                   pt_lo[0:n, j * P:(j + 1) * P], vh, vl, j == 0, j == len(blocks) - 1)
                    last.then_inc(S["na_pv"], 1)
                pe.wait_ge(S["na_out"], 16 * i + 16)
                for t in range(NT):
                    last = nc.tensor.transpose(ps[:, t * P:(t + 1) * P], o1[:, t, :], ident)
                last.then_inc(S["na_ot"], 1)
            with pe.Fori(0, 4) as i:
                pe.wait_ge(S["conv_done"], i + 1)
                for n in range(4):
                    tile_ready(4 * i + (T_CONV + n))
                    project(n % 2, 2 * n, act_hi, act_lo, T).then_inc(S["tile_done"], 1)

            def linear(name, T0):
                L = LINEAR[name]
                with pe.Fori(0, 4) as i:
                    for s in range(2):
                        tile_ready(2 * i + (T0 + s))
                        pe.wait_ge(S["lin_evac"], 2 * i + (10 * L + s + 1))
                        project(s, 2 * s, act_hi, act_lo, T).then_inc(S["tile_done"], 1)

            pe.wait_ge(S["lo_ready"], 8 * FILL["mix"] + 8)
            linear("out", T_OUT)
            sum_squares("x1")
            pe.wait_ge(S["lo_ready"], 8 * FILL["x1"] + 8)
            for t in range(NT):
                for k in range(KT):
                    last = mm3(ps[:, 8 * t:8 * t + 8], act_hi[:, k, t * P:(t + 1) * P],
                               act_lo[:, k, t * P:(t + 1) * P], wfl_hi[:, k, :], wfl_lo[:, k, :],
                               k == 0, k == KT - 1)
            last.then_inc(S["fl_proj"], 1)
            pe.wait_ge(S["fl_logf"], 1)
            for t in range(NT):
                for j in range(t + 1):
                    last = nc.tensor.matmul(bank(1, 8 * t, 8 * t + 8), tri if j == t else ones, logf[:, j, :],
                                            start=(j == 0), stop=(j == t))
            last.then_inc(S["fl_cum"], 1)
            for t in range(NT):
                for j in range(t + 1):
                    last = nc.tensor.matmul(ps[0:8, 2 * BANK + t * P:2 * BANK + (t + 1) * P], logf[:, j, :],
                                            tri if j == t else ones, start=(j == 0), stop=(j == t))
            last.then_inc(S["fl_cum"], 1)
            pe.wait_ge(S["fl_negc"], 1)
            with pe.Fori(0, 4) as i:
                t0 = 6 * i + T_MIX

                def operands(base):
                    for n in range(3):
                        s = (base + n) % 2
                        tile_ready(t0 + base + n)
                        if n < 2:
                            last = project(s, 2 * n, act_hi, act_lo, T)
                        else:
                            last = project_tok(s, lambda t: bank(4 + t // 4, (t % 4) * P, (t % 4 + 1) * P),
                                               act_hi, act_lo, NT)
                        last.then_inc(S["tile_done"], 1)

                pe.wait_ge(S["fx_done"], i + 1)
                operands(0)

                def scores(u):
                    n = P * (u + 1)
                    q = slice(u * P, (u + 1) * P)
                    for m in range(2):
                        h = slice(m * HD, (m + 1) * HD)
                        if u == 0:
                            pe.wait_ge(S["df_lo"], 3 * i + 3)
                        else:
                            pe.wait_ge(S["df_logits"], 16 * i + (2 * u - 1 + m))
                        for c in range(0, n, BANK):
                            w = min(BANK, n - c)
                            last = mm3(ps[:, 2 * m * BANK + c:2 * m * BANK + c + w], q_hi[h, q], q_lo[h, q],
                                       k_hi[h, c:c + w], k_lo[h, c:c + w], True, True)
                        last.then_inc(S["df_scores"], 1)

                scores(0)
                for u in range(NT):
                    g = 8 * i + u
                    if u + 1 < NT:
                        scores(u + 1)
                    pe.wait_ge(S["df_comb"], g + 1)
                    if u > 0:
                        pe.wait_ge(S["df_pt_lo"], g)
                    for j in range(u + 1):
                        last = nc.tensor.transpose(ps[:, 4 * BANK + j * P:4 * BANK + (j + 1) * P],
                                                   stage[:, u % 2, j * P:(j + 1) * P], ident)
                    last.then_inc(S["df_pt"], 1)
                    pe.wait_ge(S["df_pt_lo"], g + 1)
                    if u >= 2:
                        pe.wait_ge(S["df_out"], 16 * i + (2 * u - 2))
                    for j in range(u + 1):
                        last = mm3(bank(6 + u % 2, 0, P), p8_hi[:, j * P:(j + 1) * P], p8_lo[:, j * P:(j + 1) * P],
                                   va_hi[:, j, :], va_lo[:, j, :], j == 0, j == u)
                    last.then_inc(S["df_pv"], 1)
                operands(3)
                pe.wait_ge(S["df_normed"], i + 1)
                for t in range(NT):
                    last = nc.tensor.transpose(ps[:, 6 * BANK + t * P:6 * BANK + (t + 1) * P], o2[:, t, :], ident)
                last.then_inc(S["df_ot"], 1)

                def fox_scores(u):
                    a, qt = divmod(u, NT)
                    n = P * (qt + 1)
                    b0 = 2 * (u % 2) * BANK
                    h = slice(a * HD, (a + 1) * HD)
                    q = slice(qt * P, (qt + 1) * P)
                    if u == 0:
                        pe.wait_ge(S["fx_lo"], 3 * i + 3)
                    if u >= 2:
                        pe.wait_ge(S["fx_logits"], 16 * i + (u - 1))
                    for c in range(0, n, BANK):
                        w = min(BANK, n - c)
                        last = mm3(ps[:, b0 + c:b0 + c + w], q_hi[h, q], q_lo[h, q], k_hi[h, c:c + w],
                                   k_lo[h, c:c + w], True, True)
                    last.then_inc(S["fx_scores"], 1)

                fox_scores(0)
                fox_scores(1)
                for u in range(2 * NT):
                    a, qt = divmod(u, NT)
                    g = 16 * i + u
                    pe.wait_ge(S["fx_probs"], g + 1)
                    if u > 0:
                        pe.wait_ge(S["fx_pt_lo"], g)
                    for j in range(qt + 1):
                        last = nc.tensor.transpose(ps[:, 4 * BANK + j * P:4 * BANK + (j + 1) * P],
                                                   stage[:, u % 2, j * P:(j + 1) * P], ident)
                    last.then_inc(S["fx_pt"], 1)
                    if u + 2 < 2 * NT:
                        fox_scores(u + 2)
                    pe.wait_ge(S["fx_pt_lo"], g + 1)
                    if u >= 2:
                        pe.wait_ge(S["fx_out"], g - 1)
                    else:
                        pe.wait_ge(S["df_done"], i + 2)
                    hv = slice(a * HD, (a + 1) * HD)
                    for j in range(qt + 1):
                        last = mm3(bank(6 + u % 2, 0, HD), p8_hi[:, j * P:(j + 1) * P], p8_lo[:, j * P:(j + 1) * P],
                                   va_hi[:, j, hv], va_lo[:, j, hv], j == 0, j == qt)
                    last.then_inc(S["fx_pv"], 1)
                pe.wait_ge(S["fx_out"], 16 * i + 16)
                for t in range(NT):
                    last = nc.tensor.transpose(ps[:, t * P:(t + 1) * P], o2[:, t, :], ident)
                last.then_inc(S["fx_ot"], 1)
            pe.wait_ge(S["mg_done"], 1)
            with pe.Fori(0, 4) as i:
                for s in range(2):
                    t0 = 6 * i + (T_MERGE + 3 * s)
                    for n in range(2):
                        tile_ready(t0 + n)
                        if s == 1:
                            pe.wait_ge(S["mg_exp"], 4 * i + (n + 1))
                        else:
                            pe.wait_ge(S["mg_done"], 2 * i + 1)
                        project((3 * s + n) % 2, 4 + 2 * n, act_hi, act_lo, T).then_inc(S["tile_done"], 1)
                    tile_ready(t0 + 2)
                    pe.wait_ge(S["mg_done"], 2 * i + (s + 1))
                    pe.wait_ge(S["lo_ready"], 8 * FILL["y"] + 8)
                    w = (3 * s + 2) % 2
                    project(w, 0, y_hi, y_lo, T, range(0, 4))
                    project(w, 2, y_hi, y_lo, T, range(4, 8)).then_inc(S["tile_done"], 1)
            pe.wait_ge(S["lo_ready"], 8 * FILL["merged"] + 8)
            linear("wo", T_WO)
            sum_squares("mem")
            sum_squares("x2")
            pe.wait_ge(S["lo_ready"], 8 * FILL["x2"] + 8)
            with pe.Fori(0, 4) as i:
                t0 = 6 * i + T_MEM
                pe.wait_ge(S["mm_out"], 8 * i + 1)
                for c in range(2):
                    tile_ready(t0 + c)
                    project(c, 2 * c, act_hi, act_lo, T).then_inc(S["tile_done"], 1)
                for c in range(2):
                    tile_ready(t0 + 2 + c)
                    project(c, 4 + c, m_hi, m_lo, C).then_inc(S["tile_done"], 1)
                for c in range(2):
                    tile_ready(t0 + 4 + c)
                    project_tok(c, lambda t: bank(6, t * C + c * P, t * C + (c + 1) * P), m_hi, m_lo, CT
                                ).then_inc(S["tile_done"], 1)

                def scores(u):
                    if u == 0:
                        pe.wait_ge(S["mm_lo"], 5 * i + 5)
                    if u >= 2:
                        pe.wait_ge(S["mm_probs"], 8 * i + (u - 1))
                    q = slice(u * P, (u + 1) * P)
                    for c in range(2):
                        last = mm3(bank(u % 2, 0, C), mq_hi[:, c, q], mq_lo[:, c, q], mk_hi[:, c, :], mk_lo[:, c, :],
                                   c == 0, c == 1)
                    last.then_inc(S["mm_scores"], 1)

                scores(0)
                scores(1)
                for u in range(NT):
                    g = 8 * i + u
                    pe.wait_ge(S["mm_probs"], g + 1)
                    if u >= 2:
                        pe.wait_ge(S["mm_pt_lo"], g - 1)
                    for j in range(2):
                        last = nc.tensor.transpose(bank(2 + u % 2, j * P, (j + 1) * P), mp[:, u % 2, j * P:(j + 1) * P],
                                                   ident)
                    last.then_inc(S["mm_pt"], 1)
                    if u + 2 < NT:
                        scores(u + 2)
                    pe.wait_ge(S["mm_pt_lo"], g + 1)
                    if u >= 2:
                        pe.wait_ge(S["mm_out"], g)
                    for j in range(2):
                        last = mm3(bank(4 + u % 2, 0, C), mpt_hi[:, u % 2, j * P:(j + 1) * P],
                                   mpt_lo[:, u % 2, j * P:(j + 1) * P], mv_hi[:, j, :], mv_lo[:, j, :], j == 0, j == 1)
                    last.then_inc(S["mm_pv"], 1)
                pe.wait_ge(S["mm_out"], 8 * i + 9)
                for c in range(2):
                    for t in range(NT):
                        last = nc.tensor.transpose(ps[:, 2 * c * BANK + t * P:2 * c * BANK + (t + 1) * P],
                                                   mo[:, t, c * P:(c + 1) * P], ident)
                last.then_inc(S["mm_ot"], 1)
                pe.wait_ge(S["mm_done"], i + 1)
            pe.wait_ge(S["lo_ready"], 8 * FILL["memo"] + 8)
            linear("wom", T_WOM)
            sum_squares("x3")
            pe.wait_ge(S["lo_ready"], 8 * FILL["x3"] + 8)
            with pe.Fori(0, 4) as b:
                with pe.Fori(0, 4) as i:
                    for s in range(2):
                        tile_ready(16 * b + 2 * i + (T_MLP + s))
                        pe.wait_ge(S["a_lo"], 8 * b + 2 * i + (s + 1))
                        project(s, 2 * s, act_hi, act_lo, T).then_inc(S["tile_done"], 1)
                pe.wait_ge(S["a_lo"], 8 * b + 10)
                pe.sem_inc(S["seq_pe"], 1)
                with pe.Fori(0, 4) as i:
                    for s in range(2):
                        tile_ready(16 * b + 2 * i + (T_MLP + 8 + s))
                        pe.wait_ge(S["mlp_acc"], 8 * b + 2 * i + (s + 1))
                        project(s, 4 + 2 * s, a_hi, a_lo, T).then_inc(S["tile_done"], 1)
            sum_squares("final")


def _tiles(w):
    n = w.shape[1] // P
    return w.reshape(KT, P, n, P).transpose(2, 1, 0, 3).reshape(n, P, KT * P)


def _cols(v):
    return v.reshape(-1, P).T


def _feature_major(a):
    return np.ascontiguousarray(a.T.reshape(KT, P, -1).transpose(1, 0, 2))


def _constants():
    ident = np.eye(P)
    tri = np.triu(np.ones((P, P)))
    ones = np.ones((P, P))
    bd = np.kron(np.eye(2), np.ones((HD, HD)))
    perm = np.zeros((P, P))
    for h in range(2):
        for ax in range(2):
            for f in range(16):
                lo, hi = h * 64 + ax * 32 + f, h * 64 + ax * 32 + 16 + f
                perm[hi, lo] = -1.0
                perm[lo, hi] = 1.0
    return np.concatenate([ident, tri, ones, bd, perm], 1).astype(np.float32)


def _rope():
    nf = HD // 4
    inv = (np.float32(10000.0) ** (-np.arange(nf, dtype=np.float32) / nf)).astype(np.float32)
    pos = np.arange(T)
    out = np.zeros((P, 2, T), np.float32)
    for p in range(P):
        ax, f = (p % HD) // 32, p % 16
        coord = (pos // GRID_W if ax == 0 else pos % GRID_W).astype(np.float32)
        ang = (coord * inv[f]).astype(np.float32)
        out[p, 0], out[p, 1] = np.cos(ang), np.sin(ang)
    return out


def _masks():
    q = np.arange(GRID_W)
    start = np.clip(q - 8, 0, GRID_W - 16)
    ok = (q[None, :] >= start[:, None]) & (q[None, :] < start[:, None] + 16)
    col = np.where(ok, 0.0, NEG)
    out = np.zeros((P, 10, GRID_W), np.float32)
    for a in range(2):
        for r in range(9):
            row_ok = r <= 7 if a == 0 else 1 <= r <= 8
            out[a * 64:(a + 1) * 64, r] = col if row_ok else NEG
        out[a * 64:(a + 1) * 64, 9] = col
    return out


def _buckets(n):
    d = np.arange(n)
    large = 16 + (np.log(np.maximum(d, 1) / 16.0) / math.log(8.0) * 16).astype(np.int64)
    return np.where(d < 16, d, np.minimum(large, 31))


def _place_rpb(rpb):
    out = np.zeros((8, 15, 127), rpb.dtype)
    out[:, :, 48:79] = rpb
    return out


def _place_rel(rel_bias):
    out = np.full((4, T + P - 1), NEG, rel_bias.dtype)
    out[:, :T] = rel_bias[_buckets(T)[::-1]].T
    return out


_OUT = "out_0_dram"


def kernel(**inputs):
    import concourse.bacc as bacc
    from concourse.bass_utils import run_bass_kernel_spmd

    a = {k: np.asarray(v) for k, v in inputs.items()}
    x_t, ctx_t, mem_t = (_feature_major(a[n][0]) for n in ("x", "ctx", "mem_2"))
    cond_t = np.stack([_cols(a["c"][0]), _cols(a["c_ctx"])], axis=-1)
    w_in, w_in2 = _tiles(a["w_in"][0]), a["w_in_2"][0]
    stream = [w_in[4:12]]
    for i in range(4):
        stream += [w_in[[i, 4 + i, 8 + i, 12 + i]]]
    for i in range(4):
        stream += [w_in[[16 + i, 24 + i, 20 + i, 28 + i]]]
    stream += [_tiles(a["w_out"][0])]
    w2a, w2g = _tiles(w_in2[:, :3072]), _tiles(w_in2[:, 3080:])
    for i in range(4):
        stream += [w2a[[i, 4 + i, 8 + i, 12 + i, 16 + i, 20 + i]]]
    dx = _tiles(np.concatenate([a["w_diff_out_2"][0], a["w_fox_out_2"][0]], 0))
    for m in range(8):
        stream += [w2g[[m, 8 + m]], dx[m:m + 1]]
    stream += [_tiles(a["w_o_2"][0])]
    wq, wkv = _tiles(a["w_q_mem_2"][0]), _tiles(a["w_kv_mem_2"][0])
    for i in range(4):
        stream += [wq[2 * i:2 * i + 2], wkv[2 * i:2 * i + 2], wkv[8 + 2 * i:10 + 2 * i]]
    stream += [_tiles(a["w_o_mem_2"][0])]
    w1, w2 = _tiles(a["w1_2"][0]), a["w2_2"][0]
    for b in range(4):
        stream += [w1[8 * b:8 * b + 8], _tiles(w2[1024 * b:1024 * b + 1024])]
    w_stream = np.concatenate(stream, 0)
    assert w_stream.shape[0] == N_TILES

    small = np.concatenate(
        [_cols(a["norm_g"][0]), _cols(a["g_mix_2"][0]), _cols(a["g_mem_q_2"][0]), _cols(a["g_mem_kv_2"][0]),
         _cols(a["g_mlp_2"][0]), _cols(a["g_final_2"]), _cols(a["b_ada"][0]),
         np.tile(a["q_norm_g"][0], 2)[:, None], np.tile(a["k_norm_g"][0], 2)[:, None],
         _cols(a["conv_w"][0].reshape(-1)), _cols(a["conv_b"][0]), a["g_subln_2"][0][:, None],
         np.tile(a["b_forget_2"][0][None], (P, 1))], 1)
    assert small.shape == (P, V_COLS)
    lam4 = np.stack([a[f"lambda_{n}_2"][0] for n in ("q1", "k1", "q2", "k2")]).reshape(1, -1)
    w_fl = np.ascontiguousarray(w_in2[:, 3072:3080].reshape(KT, P, 8).transpose(1, 0, 2))
    ins = dict(x_t=x_t, ctx_t=ctx_t, mem_t=mem_t, cond_t=cond_t, small=small, lam4=lam4,
               consts=_constants(), rope=_rope(), masks=_masks(),
               rpb_pad=_place_rpb(a["rpb"][0]), rel_rows=_place_rel(a["rel_bias_2"]), w_fl=w_fl,
               w_ada=_tiles(a["w_ada"][0]), w_stream=w_stream)

    nc = bacc.Bacc("TRN2", target_bir_lowering=False, num_devices=1)
    arrays, aps = {}, {}
    for name, v in ins.items():
        v = np.ascontiguousarray(v)
        arrays[f"in_{name}_dram"] = v
        aps[name] = nc.dram_tensor(f"in_{name}_dram", v.shape, mybir.dt.from_np(v.dtype),
                                   kind="ExternalInput").ap()
    y_t = nc.dram_tensor(_OUT, (P, KT, T), F, kind="ExternalOutput").ap()
    program(nc, y_t=y_t, **aps)
    r = run_bass_kernel_spmd(nc, [arrays], core_ids=[0])
    y = r.results[0][_OUT]
    return np.ascontiguousarray(y.transpose(2, 1, 0).reshape(1, T, D))
```

```python
import math
from contextlib import ExitStack

import numpy as np

import concourse.bass as bass
from concourse import mybir

F = mybir.dt.float32
R = mybir.dt.float32r
ALU = mybir.AluOpType
ACT = mybir.ActivationFunctionType
AX = mybir.AxisListType

P = 128
D = 1024
T = 1024
C = 256
KT = D // P
NT = T // P
CT = C // P
BANK = 512
HD = 64
GRID_W = 64
NEG = -1.0e30
EPS = 1e-6
BIG = 3.0e38
LAMBDA_INIT = 0.8 - 0.6 * math.exp(-0.3 * 0)

T_CTX = 0
T_ATT = T_CTX + 8
T_OUT = T_ATT + 32
T_MIX = T_OUT + 8
T_MERGE = T_MIX + 40
T_WO = T_MERGE + 8
T_MEM = T_WO + 8
T_WOM = T_MEM + 24
T_MLP = T_WOM + 8
N_TILES = T_MLP + 64

FILL = {n: i for i, n in enumerate(
    ["x0", "ctx", "mix", "x1", "y", "merged", "mem", "x2", "memo", "x3"])}
NORM = {n: i for i, n in enumerate(["x0", "ctx", "x1", "mem", "x2", "x3", "final"])}
LINEAR = {"out": 0, "wo": 1, "wom": 2}

V_NORM, V_MIXG, V_MEMQ, V_MEMKV, V_MLPG, V_FIN, V_BADA = 0, 8, 16, 24, 32, 40, 48
V_QG, V_KG, V_CW, V_CB, V_SUB, V_BF = 72, 73, 74, 86, 90, 91
V_COLS = V_BF + 8
C_ID, C_TRI, C_ONE, C_BD, C_PERM = 0, 128, 256, 384, 512
C_COLS = 640

SEMS = """small_in ada_in0 ada_in1 ada_in2 ada_in3 ada_used x_in rows_in rope_in fl_in toeplitz
raw_in0 raw_in1 w_hi w_split tile_done c_sig c_silu ada_step const_ready sq_ready
acc_done ss_ready rms_ready rstd_ready rstd_spread scaled hi_ready lo_ready ck_sq ck_ss ck_rms ck_rstd
ck_done cv_done mask_in qk_sq qk_ss qk_rms qk_rstd qk_spread qk_normed qk_plain_hi qk_plain_lo qk_perm qk_sin
qk_cos qk_roped qk_hi qk_lo v_raw v_turned v_hi v_lo za_sig za_done c_hi c_lo tile_in0 tile_in1 band_step na_scores
na_cmax na_logits na_probs na_pt na_pt_hi na_pt_lo na_pv na_inv na_out na_ot pair_done cv_u cv_sig
cv_half cv_step conv_done conv_out lin_evac xres_in0 xres_in1 spilled fl_proj fl_z fl_exp fl_ln fl_logf
fl_cum fl_cumq fl_negc fl_out lam_step lam_exp df_hi df_lo strip_in df_scores df_logits df_probs
df_inv df_comb df_pt df_pt_hi df_pt_lo df_pv df_out df_ms df_rstd df_normed df_ot df_done
fx_hi fx_lo fx_ck_in fx_cq fx_bias fx_bias_m fx_scores fx_logits fx_probs fx_pt fx_pt_hi fx_pt_lo
fx_pv fx_inv fx_out fx_ot fx_done gate_half gate_copied gate_out0 gate_out1 mg_sig mg_step mm_hi mm_lo mm_scores mm_max mm_probs mm_pt
mm_pt_hi mm_pt_lo mm_pv mm_inv mm_out mm_ot mm_done a_relu a_sq a_hi a_lo mlp_acc y_ready y_out
issued""".split()


def program(nc, x_t, ctx_t, mem_t, cond_t, small, lam4, consts, rope, masks, rpb_pad, rel_rows,
            w_fl, w_ada, w_stream, y_t):
    ctx = ExitStack()
    with ctx:
        S = {n: ctx.enter_context(nc.semaphore(n)) for n in SEMS}

        def alloc(stack, name, shape, dt=F):
            return stack.enter_context(nc.sbuf_tensor(name, shape, dt))

        vec = alloc(ctx, "vec", [P, V_COLS])
        con = alloc(ctx, "con", [P, C_COLS])
        mod = alloc(ctx, "mod", [P, 24, 2])
        gs = alloc(ctx, "gs", [P, KT, 2])
        eps = alloc(ctx, "eps", [P, 1])
        one = alloc(ctx, "one", [P, 1])
        qg8 = alloc(ctx, "qg8", [P, 1])
        subg = alloc(ctx, "subg", [P, 1])
        rt = alloc(ctx, "rt", [P, NT])
        hr = alloc(ctx, "hr", [P, 2, 2 * NT])
        nm = alloc(ctx, "nm", [P, 4])
        cm = alloc(ctx, "cm", [P, 2])
        rsum = alloc(ctx, "rsum", [P, 4])
        rinv = alloc(ctx, "rinv", [P, 4])
        act_hi = alloc(ctx, "act_hi", [P, KT, T], R)
        act_lo = alloc(ctx, "act_lo", [P, KT, T], R)
        res = alloc(ctx, "res", [P, KT, T])
        raw = alloc(ctx, "raw", [P, 2, KT, P])
        w_hi = alloc(ctx, "w_hi", [P, 2, KT, P], R)
        w_lo = alloc(ctx, "w_lo", [P, 2, KT, P], R)
        stage = alloc(ctx, "stage", [P, 2, T])
        ps = ctx.enter_context(nc.psum_tensor("ps", [P, 8 * BANK], F))

        ident = con[:, C_ID:C_ID + P]
        tri = con[:, C_TRI:C_TRI + P]
        ones = con[:, C_ONE:C_ONE + P]
        bd64 = con[:, C_BD:C_BD + P]

        st = ExitStack()
        ADA_R = 12
        ada = alloc(st, "ada", [P, ADA_R, KT, P])
        cond = alloc(st, "cond", [P, KT, 2])
        cexp = alloc(st, "cexp", [P, KT, 2])
        st.close()

        st1 = ExitStack()
        kcF = alloc(st1, "kcF", [P, 4, C])
        vcF = alloc(st1, "vcF", [P, CT, 512])
        perm = alloc(st1, "perm", [P, P], R)
        st = ExitStack()
        hc_hi = alloc(st, "hc_hi", [P, KT, C], R)
        hc_lo = alloc(st, "hc_lo", [P, KT, C], R)
        ctxF = alloc(st, "ctxF", [P, KT, C])
        ksq = alloc(st, "ksq", [P, C])
        krs = alloc(st, "krs", [P, C])
        kraw = alloc(st, "kraw", [P, C])
        accc = alloc(st, "accc", [P, C])
        acc0b = alloc(st, "acc0b", [P, T])
        st.close()
        qp_hi = alloc(st1, "qp_hi", [P, T], R)
        qp_lo = alloc(st1, "qp_lo", [P, T], R)
        qr_hi = alloc(st1, "qr_hi", [P, T], R)
        qr_lo = alloc(st1, "qr_lo", [P, T], R)
        kr_hi = alloc(st1, "kr_hi", [P, T], R)
        kr_lo = alloc(st1, "kr_lo", [P, T], R)
        v_hi = alloc(st1, "v_hi", [P, NT, P], R)
        v_lo = alloc(st1, "v_lo", [P, NT, P], R)
        kc_hi = alloc(st1, "kc_hi", [P, C], R)
        kc_lo = alloc(st1, "kc_lo", [P, C], R)
        vc_hi = alloc(st1, "vc_hi", [P, CT, P], R)
        vc_lo = alloc(st1, "vc_lo", [P, CT, P], R)
        pt_hi = alloc(st1, "pt_hi", [P, 7 * P], R)
        pt_lo = alloc(st1, "pt_lo", [P, 7 * P], R)
        band_u = [alloc(st1, f"band_u{a}", [P, 14, GRID_W]) for a in range(2)]
        rope_sb = alloc(st1, "rope_sb", [P, 2, T])
        mask_sb = alloc(st1, "mask_sb", [P, 10, GRID_W])
        st1.close()
        tA, tB, tC, tD = (res[:, j, :] for j in (4, 5, 6, 7))
        band_m = [tC[:, 0:576], tA[:, 0:576]]
        o1 = tD.rearrange("p (t d) -> p t d", d=P)

        cv_x, cv_y = rope_sb[:, 0, :], rope_sb[:, 1, :]

        st4 = ExitStack()
        acc = alloc(st4, "acc", [P, T])
        q_hi = alloc(st4, "q_hi", [P, T], R)
        q_lo = alloc(st4, "q_lo", [P, T], R)
        k_hi = alloc(st4, "k_hi", [P, T], R)
        k_lo = alloc(st4, "k_lo", [P, T], R)
        va_hi = alloc(st4, "va_hi", [P, NT, P], R)
        va_lo = alloc(st4, "va_lo", [P, NT, P], R)
        strip = alloc(st4, "strip", [P, T])
        pb = alloc(st4, "pb", [P, 2, T])
        p8_hi = alloc(st4, "p8_hi", [P, T], R)
        p8_lo = alloc(st4, "p8_lo", [P, T], R)
        o2 = alloc(st4, "o2", [P, NT, P])
        cumq = alloc(st4, "cumq", [P, NT, 8])
        cq2 = alloc(st4, "cq2", [P, NT, 2])
        nlam = alloc(st4, "nlam", [P, 1])
        ms8 = alloc(st4, "ms8", [P, NT])
        osq = alloc(st4, "osq", [P, P])
        gate_sb = alloc(st4, "gate_sb", [P, 2, BANK])
        st = ExitStack()
        wfl = alloc(st, "wfl", [P, KT, 8])
        wfl_hi = alloc(st, "wfl_hi", [P, KT, 8], R)
        wfl_lo = alloc(st, "wfl_lo", [P, KT, 8], R)
        zf = alloc(st, "zf", [P, NT, 8])
        ef = alloc(st, "ef", [P, NT, 8])
        logf = alloc(st, "logf", [P, NT, 8])
        negc = alloc(st, "negc", [8, T])
        lamv = alloc(st, "lamv", [P, 4, HD])
        lamp = alloc(st, "lamp", [P, HD])
        lam2 = alloc(st, "lam2", [P, 2])
        st.close()
        bt = alloc(st4, "bt", [P, 2, T])
        nck = [alloc(st4, f"nck{a}", [P, T]) for a in range(2)]
        st4.close()

        st = ExitStack()
        y_hi = alloc(st, "y_hi", [P, KT, T], R)
        y_lo = alloc(st, "y_lo", [P, KT, T], R)
        gate_g = [alloc(st, "gate_g", [P, 2, T]), stage]
        st.close()

        st = ExitStack()
        acc2 = alloc(st, "acc2", [P, T])
        memF = alloc(st, "memF", [P, KT, C])
        m_hi = alloc(st, "m_hi", [P, KT, C], R)
        m_lo = alloc(st, "m_lo", [P, KT, C], R)
        mq_hi = alloc(st, "mq_hi", [P, 2, T], R)
        mq_lo = alloc(st, "mq_lo", [P, 2, T], R)
        mk_hi = alloc(st, "mk_hi", [P, 2, C], R)
        mk_lo = alloc(st, "mk_lo", [P, 2, C], R)
        mv_hi = alloc(st, "mv_hi", [P, 2, C], R)
        mv_lo = alloc(st, "mv_lo", [P, 2, C], R)
        mp = alloc(st, "mp", [P, 2, C])
        mpt_hi = alloc(st, "mpt_hi", [P, 2, C], R)
        mpt_lo = alloc(st, "mpt_lo", [P, 2, C], R)
        mo = alloc(st, "mo", [P, NT, C])
        st.close()

        st = ExitStack()
        acc3 = alloc(st, "acc3", [P, T])
        a_hi = alloc(st, "a_hi", [P, KT, T], R)
        a_lo = alloc(st, "a_lo", [P, KT, T], R)
        st.close()

        negc_dram = nc.dram_tensor("negc_dram", [8, T], F).ap()
        band_dram = nc.dram_tensor("band_dram", [8, P, 14, GRID_W], F).ap()
        conv_dram = nc.dram_tensor("conv_dram", [P, 4, T], F).ap()
        strip_dram = nc.dram_tensor("strip_dram", [4, P, T], F).ap()
        gate_dram = nc.dram_tensor("gate_dram", [P, 16, T], F).ap()
        spill = [nc.dram_tensor(f"spill{j}", [P, KT, T], F).ap() for j in range(2)]

        NB = {"x0": (res, T, act_hi, act_lo, acc0b), "ctx": (ctxF, C, hc_hi, hc_lo, accc),
              "x1": (res, T, act_hi, act_lo, acc), "mem": (memF, C, m_hi, m_lo, acc2),
              "x2": (res, T, act_hi, act_lo, acc2), "x3": (res, T, act_hi, act_lo, acc3),
              "final": (res, T, None, None, acc3)}
        GAIN = {"x1": V_MIXG, "mem": V_MEMKV, "x2": V_MEMQ, "x3": V_MLPG, "final": V_FIN}

        def gain(name, k):
            if name in ("x0", "ctx"):
                j = 0 if name == "x0" else 1
                return gs[:, k, j:j + 1]
            return vec[:, GAIN[name] + k:GAIN[name] + k + 1]

        def shift(name, k):
            if name in ("x0", "ctx"):
                j = 0 if name == "x0" else 1
                return mod[:, k, j:j + 1]
            return None

        def bank(b, c0=0, c1=BANK):
            return ps[:, b * BANK + c0:b * BANK + c1]

        na_o = ps[:, 6 * BANK - HD:6 * BANK]

        def bcast(src, n):
            return bass.AP(src.tensor, src.offset, [[0, P], [1, n]])

        def window(qt):
            if qt < 2:
                return 0, 512, 6 - 2 * qt
            if qt >= 6:
                return 512, 512, 14 - 2 * qt
            return (qt - 2) * P, 576, None

        HALF_TAKEN = {2: [0], 5: [1], 7: [2], 10: [3], 13: [4], 15: [5]}

        block = ctx.enter_context(nc.Block())

        @block.sync
        def _(sp):
            sp.dma_start(vec[:, :], small).then_inc(S["small_in"], 16)
            sp.dma_start(con[:, :], consts).then_inc(S["small_in"], 16)
            sp.dma_start(cond[:, :, :], cond_t).then_inc(S["small_in"], 16)
            for n in range(8):
                if n >= 4:
                    sp.wait_ge(S["ada_used"], 3 * (n - 4) + 3)
                j = 3 * n % ADA_R
                sp.dma_start(ada[:, j:j + 3, :, :],
                             w_ada[3 * n:3 * n + 3].rearrange("t p (k c) -> p t k c", k=KT)
                             ).then_inc(S[f"ada_in{n % 4}"], 16)
            for s in range(2):
                sp.dma_start(raw[:, s, :, :],
                             w_stream[s].rearrange("p (k c) -> p k c", k=KT)
                             ).then_inc(S[f"raw_in{s}"], 16)
            with sp.Fori(1, N_TILES // 2) as h:
                for s in range(2):
                    sp.wait_ge(S["w_split"], 2 * h + s - 1)
                    sp.dma_start(raw[:, s, :, :],
                                 w_stream[bass.ds(2 * h + s, 1)].rearrange("o p (k c) -> (o p) k c", k=KT)
                                 ).then_inc(S[f"raw_in{s}"], 16)
            for k in range(KT):
                sp.wait_ge(S["y_ready"], k + 1)
                sp.dma_start(y_t[:, k, :], res[:, k, :]).then_inc(S["y_out"], 16)
            sp.wait_ge(S["y_out"], 16 * KT)

        @block.gpsimd
        def _(pool):
            def split(h, s, free=True):
                pool.wait_ge(S[f"raw_in{s}"], 16 * h + 16)
                if free:
                    pool.wait_ge(S["tile_done"], 2 * h + s - 1)
                pool.sem_inc(S["issued"], 1)
                nc.gpsimd.tensor_copy(w_hi[:, s, :, :], raw[:, s, :, :]).then_inc(S["w_hi"], 1)
                pool.wait_ge(S["w_hi"], 2 * h + s + 1)
                nc.gpsimd.tensor_tensor(w_lo[:, s, :, :], raw[:, s, :, :], w_hi[:, s, :, :].bitcast(F),
                                        ALU.subtract).then_inc(S["w_split"], 1)

            def split_range(first, n):
                with pool.Fori(first // 2, (first + n) // 2) as h:
                    split(h, 0)
                    split(h, 1)

            split(0, 0, free=False)
            split(0, 1, free=False)
            split_range(T_CTX + 2, 8)
            pool.wait_ge(S["mask_in"], 16)
            with pool.Fori(0, 4) as i:
                h0 = 4 * i + (T_ATT // 2)
                split(h0 + 1, 0)
                split(h0 + 1, 1)
                split(h0 + 2, 0)
                pool.wait_ge(S["rope_in"], 16 * i + 16)
                pool.wait_ge(S["qk_plain_lo"], 2 * i + 1)
                nc.gpsimd.tensor_tensor(tA, tA, rope_sb[:, 0, :], ALU.mult).then_inc(S["qk_cos"], 1)
                pool.wait_ge(S["qk_plain_lo"], 2 * i + 2)
                nc.gpsimd.tensor_tensor(tC, tC, rope_sb[:, 0, :], ALU.mult).then_inc(S["qk_cos"], 1)
                split(h0 + 2, 1)
                pool.wait_ge(S["qk_lo"], 2 * i + 2)
                for a in range(2):
                    pool.wait_ge(S[f"tile_in{a}"], 16 * i + 16)
                    pool.sem_inc(S["issued"], 1)
                    nc.gpsimd.tensor_tensor(band_m[a].rearrange("p (r c) -> p r c", c=GRID_W),
                                            band_u[a][:, 2:11, :], mask_sb[:, 0:9, :],
                                            ALU.add).then_inc(S["band_step"], 1)
                    pool.wait_ge(S["band_step"], 4 * i + 2 * a + 1)
                    nc.gpsimd.tensor_tensor(band_u[a][:, :, :], band_u[a][:, :, :],
                                            mask_sb[:, 9:10, :].to_broadcast([P, 14, GRID_W]),
                                            ALU.add).then_inc(S["band_step"], 1)
                for n in range(3, 5):
                    split(h0 + n, 0)
                    split(h0 + n, 1)
            split_range(T_OUT + 2, 8)
            with pool.Fori(0, 4) as i:
                h0 = 5 * i + (T_MIX // 2)
                for n in range(1, 5):
                    split(h0 + n, 0)
                    split(h0 + n, 1)
                pool.wait_ge(S["fl_cumq"], 1)
                pool.wait_ge(S["fx_done"], i + 1)
                pool.sem_inc(S["issued"], 1)
                nc.gpsimd.tensor_copy(cq2[:, :, :], cumq[:, :, bass.ds(2 * i, 2)]).then_inc(S["fx_cq"], 1)
                pool.wait_ge(S["fx_cq"], i + 1)
                for u in range(2 * NT):
                    a, qt = divmod(u, NT)
                    n = P * (qt + 1)
                    g = 16 * i + u
                    b = bt[:, u % 2, 0:n]
                    if qt == 0:
                        pool.wait_ge(S["fx_ck_in"], 32 * i + 32)
                    if u >= 2:
                        pool.wait_ge(S["fx_logits"], g - 1)
                    pool.sem_inc(S["issued"], 1)
                    nc.gpsimd.tensor_scalar(out=b, in0=nck[a][:, 0:n], scalar1=cq2[:, qt, a:a + 1],
                                            scalar2=None, op0=ALU.add).then_inc(S["fx_bias"], 1)
                    pool.wait_ge(S["fx_bias"], g + 1)
                    pool.sem_inc(S["issued"], 1)
                    dg = bt[:, u % 2, n - P:n]
                    nc.gpsimd.affine_select(out=dg, in_=dg, compare_op=ALU.is_ge, fill=NEG, base=0,
                                            pattern=[[-1, P]], channel_multiplier=1
                                            ).then_inc(S["fx_bias_m"], 1)
                    if u == 9:
                        split(h0 + 5, 0)
                split(h0 + 5, 1)
            split_range(T_MERGE + 2, 8)
            split_range(T_WO + 2, 8)
            split_range(T_MEM + 2, 24)
            split_range(T_WOM + 2, 8)
            split_range(T_MLP + 2, 62)

        @block.scalar
        def _(act):
            def note():
                act.sem_inc(S["issued"], 1)

            def norm_squares(name):
                src, w = NB[name][0:2]
                r = NORM[name]
                for k in range(KT):
                    if 8 * r + k >= 2:
                        act.wait_ge(S["acc_done"], 8 * r + k - 1)
                    nc.scalar.activation(stage[:, k % 2, 0:w], src[:, k, :], ACT.Square
                                         ).then_inc(S["sq_ready"], 1)
                act.wait_ge(S["ss_ready"], r + 1)
                nc.scalar.activation(rt[:, 0:w // P], bank(2, 0, w // P), ACT.Sqrt,
                                     bias=eps[:, 0:1], scale=1.0 / D).then_inc(S["rms_ready"], 1)

            def norm_hi(name):
                r, f = NORM[name], FILL[name]
                w, hi = NB[name][1:3]
                for k in range(KT):
                    act.wait_ge(S["scaled"], 8 * r + k + 1)
                    if shift(name, k) is None:
                        nc.scalar.activation(hi[:, k, :], stage[:, k % 2, 0:w], ACT.Copy
                                             ).then_inc(S["hi_ready"], 1)
                    else:
                        nc.scalar.activation(hi[:, k, :], stage[:, k % 2, 0:w], ACT.Identity,
                                             bias=shift(name, k)).then_inc(S["hi_ready"], 1)

            def split_hi(hi, loaded=None):
                for k in range(KT):
                    if loaded is not None and k == 4:
                        act.wait_ge(loaded, 32)
                    nc.scalar.activation(hi[:, k, :], res[:, k, :], ACT.Copy).then_inc(S["hi_ready"], 1)

            act.dma_start(res[:, :, :], x_t).then_inc(S["x_in"], 16)
            act.wait_ge(S["small_in"], 48)
            nc.scalar.activation(cexp[:, :, :], cond[:, :, :], ACT.Sigmoid).then_inc(S["c_sig"], 1)
            for h in range(8):
                for qa in range(2):
                    src = bass.AP(rpb_pad.tensor, h * 15 * 127 + (1 - qa) * 127 + 63,
                                  [[127, 14], [-1, GRID_W], [1, GRID_W]])
                    act.dma_start(band_dram[h, 64 * qa:64 * qa + 64].rearrange("q j c -> j q c"), src
                                  ).then_inc(S["toeplitz"], 16)
            src = bass.AP(rel_rows.tensor, P - 1, [[T + P - 1, 4], [-1, P], [1, T]])
            act.dma_start(strip_dram, src).then_inc(S["toeplitz"], 16)
            act.wait_ge(S["x_in"], 16)
            act.wait_ge(S["const_ready"], 1)
            norm_squares("x0")
            act.dma_start(ctxF[:, :, :], ctx_t).then_inc(S["rows_in"], 16)
            nc.scalar.activation(perm[:, :], con[:, C_PERM:C_PERM + P], ACT.Copy)
            norm_hi("x0")
            act.wait_ge(S["rows_in"], 16)
            act.wait_ge(S["lo_ready"], 8 * FILL["x0"] + 8)
            norm_squares("ctx")
            norm_hi("ctx")
            with act.Fori(0, 4) as j:
                act.wait_ge(S["tile_done"], j + (T_CTX + 1))
                act.wait_ge(S["ck_done"], j + 1)
                nc.scalar.activation(kraw[:, :], bank(0, 0, C), ACT.Copy)
                nc.scalar.activation(ksq[:, :], bank(0, 0, C), ACT.Square).then_inc(S["ck_sq"], 1)
                act.wait_ge(S["ck_ss"], j + 1)
                nc.scalar.activation(krs[:, :], bank(1, 0, C), ACT.Sqrt, bias=eps[:, 0:1],
                                     scale=1.0 / HD).then_inc(S["ck_rms"], 1)
            act.wait_ge(S["tile_done"], T_CTX + 8)
            act.dma_start(mask_sb[:, :, :], masks).then_inc(S["mask_in"], 16)

            act.wait_ge(S["toeplitz"], 16 * 17)
            with act.Fori(0, 4) as i:
                t0 = 8 * i + T_ATT
                act.wait_ge(S["conv_out"], 16 * i + 16)
                act.dma_start(rope_sb[:, :, :], rope).then_inc(S["rope_in"], 16)
                act.wait_ge(S["pair_done"], i + 1)
                for a in range(2):
                    act.dma_start(band_u[a][:, :, :], band_dram[bass.ds(2 * i + a, 1)].rearrange(
                        "o p j c -> (o p) j c")).then_inc(S[f"tile_in{a}"], 16)
                for n, (full, sq, b0) in enumerate(((tA, tB, 0), (tC, tD, 2))):
                    act.wait_ge(S["tile_done"], t0 + n + 1)
                    nc.scalar.activation(full, ps[:, b0 * BANK:(b0 + 2) * BANK], ACT.Copy
                                         )
                    nc.scalar.activation(sq, ps[:, b0 * BANK:(b0 + 2) * BANK], ACT.Square
                                         ).then_inc(S["qk_sq"], 1)
                nc.scalar.activation(kc_hi[:, :], kcF[:, bass.ds(i, 1), :].rearrange("p o c -> p (o c)"),
                                     ACT.Copy).then_inc(S["c_hi"], 1)
                nc.scalar.activation(vc_hi[:, :, :], vcF[:, :, bass.ds(P * i, P)],
                                     ACT.Copy).then_inc(S["c_hi"], 1)
                act.wait_ge(S["qk_ss"], 2 * i + 1)
                nc.scalar.activation(hr[:, 0, :], bank(0, 0, 2 * NT), ACT.Sqrt, bias=eps[:, 0:1],
                                     scale=1.0 / HD).then_inc(S["qk_rms"], 1)
                act.wait_ge(S["tile_done"], t0 + 3)
                nc.scalar.activation(stage[:, 1, :], ps[:, 4 * BANK:6 * BANK], ACT.Copy).then_inc(S["v_raw"], 1)
                act.wait_ge(S["qk_normed"], 2 * i + 1)
                nc.scalar.activation(qp_hi[:, :], tA, ACT.Copy).then_inc(S["qk_plain_hi"], 1)
                act.wait_ge(S["qk_ss"], 2 * i + 2)
                nc.scalar.activation(hr[:, 1, :], bank(2, 0, 2 * NT), ACT.Sqrt, bias=eps[:, 0:1],
                                     scale=1.0 / HD).then_inc(S["qk_rms"], 1)
                act.wait_ge(S["v_turned"], i + 1)
                nc.scalar.activation(v_hi[:, :, :], ps[:, 4 * BANK:6 * BANK].rearrange("p (t d) -> p t d", d=P),
                                     ACT.Copy).then_inc(S["v_hi"], 1)
                act.wait_ge(S["qk_normed"], 2 * i + 2)
                nc.scalar.activation(kr_hi[:, :], tC, ACT.Copy).then_inc(S["qk_plain_hi"], 1)
                act.wait_ge(S["qk_roped"], 2 * i + 1)
                nc.scalar.activation(qr_hi[:, :], tA, ACT.Copy).then_inc(S["qk_hi"], 1)
                act.wait_ge(S["tile_done"], t0 + 4)
                nc.scalar.activation(tB, ps[:, 6 * BANK:8 * BANK], ACT.Sigmoid).then_inc(S["za_sig"], 1)
                act.wait_ge(S["qk_roped"], 2 * i + 2)
                nc.scalar.activation(kr_hi[:, :], tC, ACT.Copy).then_inc(S["qk_hi"], 1)
                act.wait_ge(S["tile_done"], t0 + 5)
                nc.scalar.activation(cv_x, ps[:, 4 * BANK:6 * BANK], ACT.Copy).then_inc(S["cv_u"], 1)

                def exp_unit(u):
                    a, qt = divmod(u, NT)
                    w = window(qt)[1] + C
                    act.wait_ge(S["na_logits"], 16 * i + (u + 1))
                    nc.scalar.activation(stage[:, u % 2, 0:w], stage[:, u % 2, 0:w], ACT.Exp,
                                         bias=nm[:, u % 2:u % 2 + 1], scale=-1.0,
                                         accum_out=rsum[:, u % 2:u % 2 + 1]).then_inc(S["na_probs"], 1)

                exp_unit(0)
                for u in range(16):
                    if u < 15:
                        exp_unit(u + 1)
                    w = 6 * P if window(u % NT)[1] == 512 else 7 * P
                    act.wait_ge(S["na_pt"], 16 * i + (u + 1))
                    if u > 0:
                        act.wait_ge(S["na_pv"], 16 * i + u)
                    nc.scalar.activation(pt_hi[:, 0:w], ps[:, 4 * BANK:4 * BANK + w], ACT.Copy
                                         ).then_inc(S["na_pt_hi"], 1)
                    for h in HALF_TAKEN.get(u, []):
                        if h >= 4:
                            act.wait_ge(S["cv_half"], 6 * i + (h + 1))
                            act.wait_ge(S["cv_step"], 9 * i + 5)
                            half = slice((h % 2) * BANK, (h % 2 + 1) * BANK)
                            nc.scalar.activation(cv_x[:, half], bank(6 + h % 2), ACT.Sigmoid
                                                 ).then_inc(S["cv_sig"], 1)
                act.wait_ge(S["conv_done"], i + 2)
                act.dma_start(conv_dram[:, bass.ds(i, 1), :].rearrange("p o t -> p (o t)"), cv_y
                              ).then_inc(S["conv_out"], 16)
            act.wait_ge(S["pair_done"], 5)
            act.wait_ge(S["conv_out"], 80)
            act.dma_start(res[:, 4:8, :], conv_dram).then_inc(S["rows_in"], 16)
            act.wait_ge(S["tile_done"], T_OUT)
            split_hi(act_hi, S["rows_in"])

            def residual_loads(name, src):
                L = LINEAR[name]
                with act.Fori(0, 4) as i:
                    for s in range(2):
                        act.wait_ge(S["lin_evac"], 2 * i + (10 * L + s + 1))
                        act.dma_start(stage[:, s, :], src[:, bass.ds(2 * i + s, 1), :].rearrange("p o t -> p (o t)")
                                      ).then_inc(S[f"xres_in{s}"], 16)

            residual_loads("out", x_t)
            act.wait_ge(S["lin_evac"], 10)
            act.dma_start(wfl[:, :, :], w_fl).then_inc(S["fl_in"], 16)
            act.dma_start(lamv[:, :, :], bcast(lam4, 4 * HD).rearrange("p (a d) -> p a d", a=4)
                          ).then_inc(S["fl_in"], 16)
            act.dma_start(spill[0], res[:, :, :]).then_inc(S["spilled"], 16)
            norm_squares("x1")
            act.wait_ge(S["fl_in"], 32)
            nc.scalar.activation(wfl_hi[:, :, :], wfl[:, :, :], ACT.Copy).then_inc(S["fl_exp"], 1)
            norm_hi("x1")
            act.wait_ge(S["fl_z"], 3)
            nc.scalar.activation(ef[:, :, :], ef[:, :, :], ACT.Exp, scale=-1.0).then_inc(S["fl_exp"], 1)
            act.wait_ge(S["fl_exp"], 2)
            nc.scalar.activation(ef[:, :, :], ef[:, :, :], ACT.Ln, bias=one[:, 0:1]).then_inc(S["fl_ln"], 1)
            act.wait_ge(S["lam_step"], 2)
            nc.scalar.activation(lam2[:, :], lam2[:, :], ACT.Exp).then_inc(S["lam_exp"], 1)
            act.wait_ge(S["fl_negc"], 1)
            act.dma_start(negc_dram, negc[:, :]).then_inc(S["fl_out"], 16)
            act.wait_ge(S["fl_out"], 16)
            act.wait_ge(S["lam_step"], 4)
            with act.Fori(0, 4) as i:
                t0 = 10 * i + T_MIX
                act.wait_ge(S["df_done"], i + 1)
                act.dma_start(strip[:, :], strip_dram[bass.ds(i, 1)].rearrange("o p c -> (o p) c")
                              ).then_inc(S["strip_in"], 16)
                act.wait_ge(S["fx_done"], i + 1)
                for a in range(2):
                    row = negc_dram[bass.ds(2 * i + a, 1), :]
                    act.dma_start(nck[a][:, :], row.to_broadcast([P, T])).then_inc(S["fx_ck_in"], 16)

                def operands(base, count):
                    act.wait_ge(S["tile_done"], t0 + base + 1)
                    nc.scalar.activation(stage[:, 1, :], ps[:, 4 * BANK:6 * BANK], ACT.Copy).then_inc(S["v_raw"], 1)
                    act.wait_ge(S["tile_done"], t0 + base + 2)
                    nc.scalar.activation(q_hi[:, :], ps[:, 0:2 * BANK], ACT.Copy, scale=0.125).then_inc(S[count], 1)
                    act.wait_ge(S["v_turned"], 2 * i + (5 + base // 5))
                    nc.scalar.activation(va_hi[:, :, :], ps[:, 4 * BANK:6 * BANK].rearrange("p (t d) -> p t d", d=P),
                                         ACT.Copy).then_inc(S[count], 1)
                    act.wait_ge(S["tile_done"], t0 + base + 3)
                    nc.scalar.activation(k_hi[:, :], ps[:, 2 * BANK:4 * BANK], ACT.Copy).then_inc(S[count], 1)

                def gate_half(h):
                    out = S[f"gate_out{h % 2}"]
                    act.wait_ge(S["gate_half"], 8 * i + (h + 1))
                    act.wait_ge(out, 64 * i + 16 * (h // 2 + 1))
                    nc.scalar.activation(gate_sb[:, h % 2, :], bank(7), ACT.Copy).then_inc(S["gate_copied"], 1)
                    act.wait_ge(S["gate_copied"], 8 * i + (h + 2))
                    dst = gate_dram[:, bass.ds(4 * i + h // 2, 1), (h % 2) * BANK:(h % 2 + 1) * BANK]
                    act.dma_start(dst.rearrange("p o t -> p (o t)"), gate_sb[:, h % 2, :]).then_inc(out, 16)

                operands(0, "df_hi")

                def exps(u):
                    n = P * (u + 1)
                    for m, buf in enumerate((stage, pb)):
                        c = 2 * (u % 2) + m
                        act.wait_ge(S["df_logits"], 16 * i + (2 * u + m + 1))
                        nc.scalar.activation(buf[:, u % 2, 0:n], buf[:, u % 2, 0:n], ACT.Exp,
                                             bias=nm[:, c:c + 1], scale=-1.0,
                                             accum_out=rsum[:, c:c + 1]).then_inc(S["df_probs"], 1)

                exps(0)
                for u in range(NT):
                    n = P * (u + 1)
                    if u + 1 < NT:
                        exps(u + 1)
                    act.wait_ge(S["df_pt"], 8 * i + (u + 1))
                    if u > 0:
                        act.wait_ge(S["df_pv"], 8 * i + u)
                    nc.scalar.activation(p8_hi[:, 0:n], ps[:, 4 * BANK:4 * BANK + n], ACT.Copy
                                         ).then_inc(S["df_pt_hi"], 1)
                    if u % 2 == 1:
                        gate_half(u // 2)
                    act.wait_ge(S["df_pv"], 8 * i + (u + 1))
                    r1 = rinv[:, 2 * (u % 2):2 * (u % 2) + 1]
                    nc.scalar.activation(o2[:, u, :], bank(6, 0, P), ACT.Copy, scale=r1).then_inc(S["df_out"], 1)
                    if u > 0:
                        act.wait_ge(S["df_out"], 16 * i + 2 * u)
                    nc.scalar.activation(osq[:, :], bank(6, 0, P), ACT.Square, scale=r1,
                                         accum_out=ms8[:, u:u + 1]).then_inc(S["df_out"], 1)
                act.wait_ge(S["df_out"], 16 * i + 16)
                nc.scalar.activation(ms8[:, :], ms8[:, :], ACT.Sqrt, bias=eps[:, 0:1], scale=1.0 / P
                                     ).then_inc(S["df_ms"], 1)
                operands(5, "fx_hi")

                def exp_fox(u):
                    n = P * (u % NT + 1)
                    act.wait_ge(S["fx_logits"], 16 * i + (u + 1))
                    nc.scalar.activation(stage[:, u % 2, 0:n], stage[:, u % 2, 0:n], ACT.Exp,
                                         bias=nm[:, u % 2:u % 2 + 1], scale=-1.0,
                                         accum_out=rsum[:, u % 2:u % 2 + 1]).then_inc(S["fx_probs"], 1)

                exp_fox(0)
                for u in range(2 * NT):
                    n = P * (u % NT + 1)
                    if u < 2 * NT - 1:
                        exp_fox(u + 1)
                    act.wait_ge(S["fx_pt"], 16 * i + (u + 1))
                    if u > 0:
                        act.wait_ge(S["fx_pv"], 16 * i + u)
                    nc.scalar.activation(p8_hi[:, 0:n], ps[:, 4 * BANK:4 * BANK + n], ACT.Copy
                                         ).then_inc(S["fx_pt_hi"], 1)
                    if u % 4 == 3:
                        gate_half(4 + u // 4)
            act.wait_ge(S["fx_done"], 5)
            act.wait_ge(S["df_done"], 5)
            for p in range(2):
                act.wait_ge(S[f"gate_out{p}"], 16 * 17)
            split_hi(y_hi)
            def load_gates(s, first, m=0):
                if not first:
                    act.wait_ge(S["lo_ready"], m + (8 * FILL["merged"] + s - 1))
                act.dma_start(gate_g[s][:, :, :], gate_dram[:, bass.ds(2 * m + 2 * s, 2), :]
                              if not first else gate_dram[:, 2 * s:2 * s + 2, :]).then_inc(S[f"tile_in{s}"], 16)

            def sigmoids(s, m):
                act.wait_ge(S[f"tile_in{s}"], 8 * m + 80)
                nc.scalar.activation(gate_g[s][:, :, :], gate_g[s][:, :, :], ACT.Sigmoid).then_inc(S["mg_sig"], 1)

            def merged_hi(s, m):
                act.wait_ge(S["mg_step"], 3 * m + 3 * (s + 1))
                act.sem_inc(S["issued"], 1)
                nc.scalar.activation(act_hi[:, bass.ds(m + s, 1), :].rearrange("p o t -> p (o t)"),
                                     gate_g[s][:, 0, :], ACT.Copy).then_inc(S["hi_ready"], 1)

            load_gates(0, True)
            load_gates(1, True)
            sigmoids(0, 0)
            with act.Fori(0, 3) as i:
                sigmoids(1, 2 * i)
                merged_hi(0, 2 * i)
                load_gates(0, False, 2 * i + 2)
                merged_hi(1, 2 * i)
                load_gates(1, False, 2 * i + 2)
                sigmoids(0, 2 * i + 2)
            sigmoids(1, 6)
            merged_hi(0, 6)
            merged_hi(1, 6)
            act.wait_ge(S["spilled"], 16)
            residual_loads("wo", spill[0])
            act.wait_ge(S["lin_evac"], 20)
            act.dma_start(memF[:, :, :], mem_t).then_inc(S["rows_in"], 16)
            act.dma_start(spill[1], res[:, :, :]).then_inc(S["spilled"], 16)
            act.wait_ge(S["rows_in"], 48)
            norm_squares("mem")
            norm_hi("mem")
            act.wait_ge(S["lo_ready"], 8 * FILL["mem"] + 8)
            norm_squares("x2")
            norm_hi("x2")
            act.wait_ge(S["spilled"], 32)
            with act.Fori(0, 4) as i:
                t0 = 6 * i + T_MEM
                for c in range(2):
                    act.wait_ge(S["tile_done"], t0 + c + 1)
                    nc.scalar.activation(mq_hi[:, c, :], ps[:, 2 * c * BANK:(2 * c + 2) * BANK], ACT.Copy,
                                         scale=0.0625).then_inc(S["mm_hi"], 1)
                for c in range(2):
                    act.wait_ge(S["tile_done"], t0 + c + 3)
                    nc.scalar.activation(mk_hi[:, c, :], bank(4 + c, 0, C), ACT.Copy).then_inc(S["mm_hi"], 1)
                act.wait_ge(S["tile_done"], t0 + 6)
                nc.scalar.activation(mv_hi[:, :, :], bank(6).rearrange("p (t d) -> p t d", d=C), ACT.Copy
                                     ).then_inc(S["mm_hi"], 1)

                def exp_mem(u):
                    act.wait_ge(S["mm_max"], 8 * i + (u + 1))
                    if u >= 2:
                        act.wait_ge(S["mm_pt"], 8 * i + (u - 1))
                    nc.scalar.activation(mp[:, u % 2, :], bank(u % 2, 0, C), ACT.Exp, bias=nm[:, u % 2:u % 2 + 1],
                                         accum_out=rsum[:, u % 2:u % 2 + 1]).then_inc(S["mm_probs"], 1)

                exp_mem(0)
                for u in range(NT):
                    if u + 1 < NT:
                        exp_mem(u + 1)
                    act.wait_ge(S["mm_pt"], 8 * i + (u + 1))
                    if u >= 2:
                        act.wait_ge(S["mm_pv"], 8 * i + (u - 1))
                    nc.scalar.activation(mpt_hi[:, u % 2, :], bank(2 + u % 2, 0, C), ACT.Copy
                                         ).then_inc(S["mm_pt_hi"], 1)
                act.wait_ge(S["mm_ot"], i + 1)
                note()
                nc.scalar.activation(res[:, bass.ds(2 * i, 2), :],
                                     ps[:, 0:4 * BANK].rearrange("p (c t) -> p c t", c=2), ACT.Copy
                                     ).then_inc(S["mm_done"], 1)
            act.wait_ge(S["mm_done"], 4)
            split_hi(act_hi)
            residual_loads("wom", spill[1])
            act.wait_ge(S["lin_evac"], 30)
            norm_squares("x3")
            norm_hi("x3")
            with act.Fori(0, 4) as b:
                with act.Fori(0, 4) as i:
                    for s in range(2):
                        n1 = 8 * b + 2 * i + s
                        act.wait_ge(S["tile_done"], 16 * b + 2 * i + (T_MLP + s + 1))
                        act.wait_ge(S["a_lo"], n1 + 1)
                        nc.scalar.activation(stage[:, s, :], ps[:, 2 * s * BANK:(2 * s + 2) * BANK], ACT.Relu
                                             ).then_inc(S["a_relu"], 1)
                        act.wait_ge(S["a_sq"], n1 + 1)
                        note()
                        nc.scalar.activation(a_hi[:, bass.ds(2 * i + s, 1), :].rearrange("p o t -> p (o t)"),
                                             stage[:, s, :], ACT.Copy).then_inc(S["a_hi"], 1)
            act.wait_ge(S["mlp_acc"], 34)
            norm_squares("final")

        @block.vector
        def _(dve):
            def note():
                dve.sem_inc(S["issued"], 1)

            def norm_sum(name):
                src, w = NB[name][0:2]
                ac, r = NB[name][4], NORM[name]
                for k in range(KT):
                    dve.wait_ge(S["sq_ready"], 8 * r + k + 1)
                    if k == 0:
                        nc.vector.tensor_copy(ac[:, 0:w], stage[:, 0, 0:w]).then_inc(S["acc_done"], 1)
                    else:
                        dve.wait_ge(S["acc_done"], 8 * r + k)
                        nc.vector.tensor_tensor(ac[:, 0:w], ac[:, 0:w], stage[:, k % 2, 0:w], ALU.add
                                                ).then_inc(S["acc_done"], 1)
                dve.wait_ge(S["rms_ready"], r + 1)
                nc.vector.reciprocal(rt[:, 0:w // P], rt[:, 0:w // P]).then_inc(S["rstd_ready"], 1)
                dve.wait_ge(S["rstd_spread"], r + 1)

            def norm_scale(name):
                src, w, hi, lo, _ = NB[name]
                r, f = NORM[name], FILL[name]

                def low(k):
                    dve.wait_ge(S["hi_ready"], 8 * f + k + 1)
                    sh = shift(name, k)
                    if sh is None:
                        nc.vector.tensor_tensor(lo[:, k, :], stage[:, k % 2, 0:w], hi[:, k, :].bitcast(F),
                                                ALU.subtract).then_inc(S["lo_ready"], 1)
                    else:
                        nc.vector.scalar_tensor_tensor(out=lo[:, k, :], in0=stage[:, k % 2, 0:w], scalar=sh,
                                                       in1=hi[:, k, :].bitcast(F), op0=ALU.add,
                                                       op1=ALU.subtract).then_inc(S["lo_ready"], 1)

                for k in range(KT):
                    if k >= 2:
                        dve.wait_ge(S["lo_ready"], 8 * f + k - 1)
                    nc.vector.scalar_tensor_tensor(out=stage[:, k % 2, 0:w], in0=src[:, k, :], scalar=gain(name, k),
                                                   in1=ps[:, 2 * BANK:2 * BANK + w], op0=ALU.mult, op1=ALU.mult
                                                   ).then_inc(S["scaled"], 1)
                    if k >= 1:
                        low(k - 1)
                low(KT - 1)

            def split_lo(name, hi, lo):
                f = FILL[name]
                for k in range(KT):
                    dve.wait_ge(S["hi_ready"], 8 * f + k + 1)
                    nc.vector.tensor_tensor(lo[:, k, :], res[:, k, :], hi[:, k, :].bitcast(F), ALU.subtract
                                            ).then_inc(S["lo_ready"], 1)

            nc.vector.memset(eps[:, :], EPS).then_inc(S["const_ready"], 1)
            nc.vector.memset(one[:, :], 1.0)
            dve.wait_ge(S["small_in"], 48)
            nc.vector.tensor_scalar(out=qg8[:, :], in0=vec[:, V_QG:V_QG + 1], scalar1=0.125, scalar2=None,
                                    op0=ALU.mult).then_inc(S["const_ready"], 1)
            nc.vector.tensor_scalar(out=subg[:, :], in0=vec[:, V_SUB:V_SUB + 1], scalar1=1.0 - LAMBDA_INIT,
                                    scalar2=None, op0=ALU.mult).then_inc(S["const_ready"], 1)
            dve.wait_ge(S["c_sig"], 1)
            nc.vector.tensor_tensor(cond[:, :, :], cond[:, :, :], cexp[:, :, :], ALU.mult).then_inc(S["c_silu"], 1)
            dve.wait_ge(S["ada_used"], 24)
            nc.vector.tensor_tensor(mod[:, :, :], ps[:, 0:48].rearrange("p (m j) -> p m j", j=2),
                                    vec[:, V_BADA:V_BADA + 24].rearrange("p (m o) -> p m o", o=1)
                                    .to_broadcast([P, 24, 2]), ALU.add).then_inc(S["ada_step"], 1)
            dve.wait_ge(S["ada_step"], 1)
            nc.vector.scalar_tensor_tensor(out=gs[:, :, :], in0=mod[:, 8:16, :], scalar=1.0,
                                           in1=vec[:, V_NORM:V_NORM + 8].rearrange("p (m o) -> p m o", o=1)
                                           .to_broadcast([P, 8, 2]), op0=ALU.add, op1=ALU.mult
                                           ).then_inc(S["ada_step"], 1)
            dve.wait_ge(S["ada_step"], 2)
            norm_sum("x0")
            norm_scale("x0")
            norm_sum("ctx")
            norm_scale("ctx")
            dve.drain().then_inc(S["ck_done"], 1)
            with dve.Fori(0, 4) as j:
                dve.wait_ge(S["ck_rms"], j + 1)
                nc.vector.reciprocal(krs[:, :], krs[:, :]).then_inc(S["ck_rstd"], 1)
                dve.wait_ge(S["ck_rstd"], j + 1)
                nc.vector.scalar_tensor_tensor(out=kcF[:, bass.ds(j, 1), :].rearrange("p o c -> p (o c)"),
                                               in0=kraw[:, :], scalar=vec[:, V_KG:V_KG + 1], in1=krs[:, :],
                                               op0=ALU.mult, op1=ALU.mult).then_inc(S["ck_done"], 1)
            dve.drain().then_inc(S["cv_done"], 1)
            with dve.Fori(0, 4) as j:
                dve.wait_ge(S["tile_done"], j + (T_CTX + 5))
                nc.vector.tensor_copy(vcF[:, :, bass.ds(P * j, P)],
                                      bank(0, 0, C).rearrange("p (t d) -> p t d", d=P)).then_inc(S["cv_done"], 1)
            dve.drain().then_inc(S["pair_done"], 1)
            dve.drain().then_inc(S["conv_done"], 1)
            dve.drain().then_inc(S["conv_out"], 16)
            with dve.Fori(0, 4) as i:
                def normed(n, full, sq, g):
                    b0 = 2 * n
                    dve.wait_ge(S["qk_rms"], 2 * i + (n + 1))
                    nc.vector.reciprocal(hr[:, n, :], hr[:, n, :]).then_inc(S["qk_rstd"], 1)
                    dve.wait_ge(S["qk_rstd"], 4 * i + (2 * n + 1))
                    nc.vector.tensor_copy(sq.rearrange("p (t d) -> p t d", d=HD),
                                          hr[:, n, :].rearrange("p (t o) -> p t o", o=1)
                                          .to_broadcast([P, 2 * NT, HD])).then_inc(S["qk_rstd"], 1)
                    dve.wait_ge(S["qk_spread"], 2 * i + (n + 1))
                    nc.vector.scalar_tensor_tensor(out=full, in0=full, scalar=g,
                                                   in1=ps[:, b0 * BANK:(b0 + 2) * BANK], op0=ALU.mult,
                                                   op1=ALU.mult).then_inc(S["qk_normed"], 1)

                def plain_lo(n, full, hi, lo):
                    dve.wait_ge(S["qk_plain_hi"], 2 * i + (n + 1))
                    nc.vector.tensor_tensor(lo[:, :], full, hi[:, :].bitcast(F), ALU.subtract
                                            ).then_inc(S["qk_plain_lo"], 1)

                def roped(n, full, b0):
                    dve.wait_ge(S["qk_perm"], 2 * i + (n + 1))
                    if n == 0:
                        dve.wait_ge(S["rope_in"], 16 * i + 16)
                    nc.vector.tensor_tensor(stage[:, n, :], ps[:, b0 * BANK:(b0 + 2) * BANK], rope_sb[:, 1, :],
                                            ALU.mult).then_inc(S["qk_sin"], 1)
                    dve.wait_ge(S["qk_sin"], 2 * i + (n + 1))
                    dve.wait_ge(S["qk_cos"], 2 * i + (n + 1))
                    nc.vector.tensor_tensor(full, full, stage[:, n, :], ALU.add).then_inc(S["qk_roped"], 1)

                def rot_lo(n, full, hi, lo):
                    dve.wait_ge(S["qk_hi"], 2 * i + (n + 1))
                    nc.vector.tensor_tensor(lo[:, :], full, hi[:, :].bitcast(F), ALU.subtract
                                            ).then_inc(S["qk_lo"], 1)

                dve.wait_ge(S["c_hi"], 2 * i + 2)
                nc.vector.tensor_tensor(kc_lo[:, :], kcF[:, bass.ds(i, 1), :].rearrange("p o c -> p (o c)"),
                                        kc_hi[:, :].bitcast(F), ALU.subtract).then_inc(S["c_lo"], 1)
                nc.vector.tensor_tensor(vc_lo[:, :, :], vcF[:, :, bass.ds(P * i, P)],
                                        vc_hi[:, :, :].bitcast(F), ALU.subtract).then_inc(S["c_lo"], 1)
                normed(0, tA, tB, qg8[:, 0:1])
                plain_lo(0, tA, qp_hi, qp_lo)
                normed(1, tC, tD, vec[:, V_KG:V_KG + 1])
                dve.wait_ge(S["v_hi"], i + 1)
                nc.vector.tensor_tensor(v_lo[:, :, :], ps[:, 4 * BANK:6 * BANK].rearrange("p (t d) -> p t d", d=P),
                                        v_hi[:, :, :].bitcast(F), ALU.subtract).then_inc(S["v_lo"], 1)
                plain_lo(1, tC, kr_hi, kr_lo)
                roped(0, tA, 0)
                rot_lo(0, tA, qr_hi, qr_lo)
                roped(1, tC, 2)
                rot_lo(1, tC, kr_hi, kr_lo)
                dve.wait_ge(S["za_sig"], i + 1)
                nc.vector.tensor_tensor(tB, ps[:, 6 * BANK:8 * BANK], tB, ALU.mult).then_inc(S["za_done"], 1)

                def logits(u):
                    a, qt = divmod(u, NT)
                    key0, nl, row0 = window(qt)
                    b0 = 2 * (u % 2) * BANK
                    g = 16 * i + u
                    dve.wait_ge(S["na_scores"], g + 1)
                    if u >= 2:
                        dve.wait_ge(S["na_pt"], g - 1)
                    elif u == 0:
                        dve.wait_ge(S["qk_roped"], 2 * i + 2)
                    if qt == 0:
                        dve.wait_ge(S["band_step"], 4 * i + 2 * a + 2)
                    nc.vector.tensor_scalar(out=stage[:, u % 2, nl:nl + C], in0=ps[:, b0 + nl:b0 + nl + C],
                                            scalar1=-1.0, scalar2=None, op0=ALU.mult, op1=ALU.min,
                                            accum_out=cm[:, u % 2:u % 2 + 1]).then_inc(S["na_cmax"], 1)
                    dve.wait_ge(S["na_cmax"], g + 1)
                    note()
                    if row0 is None:
                        band = band_m[a]
                    else:
                        band = band_u[a][:, row0:row0 + 8, :].rearrange("p r c -> p (r c)")
                    nc.vector.tensor_tensor_reduce(out=stage[:, u % 2, 0:nl], in0=ps[:, b0:b0 + nl], in1=band,
                                                   scale=-1.0, scalar=cm[:, u % 2:u % 2 + 1], op0=ALU.add,
                                                   op1=ALU.min, accum_out=nm[:, u % 2:u % 2 + 1]
                                                   ).then_inc(S["na_logits"], 1)

                def conv_half(h):
                    half = slice((h % 2) * BANK, (h % 2 + 1) * BANK)
                    src, x_, y_ = bank(6 + h % 2), cv_x[:, half], cv_y[:, half]
                    dve.wait_ge(S["cv_half"], 6 * i + (h + 1))
                    if h < 2:
                        dve.wait_ge(S["cv_u"], i + 1)
                        nc.vector.tensor_tensor(x_, src, x_, ALU.mult).then_inc(S["cv_step"], 1)
                    elif h < 4:
                        dve.wait_ge(S["cv_step"], 9 * i + 5)
                        nc.vector.tensor_tensor(y_, src, y_, ALU.mult).then_inc(S["cv_step"], 1)
                    else:
                        dve.wait_ge(S["cv_sig"], 2 * i + (h - 3))
                        nc.vector.tensor_tensor(x_, src, x_, ALU.mult).then_inc(S["cv_step"], 1)

                def conv_tap(n):
                    tap = vec[:, bass.ds(V_CW + 4 * n + i, 1)]
                    if n == 1:
                        dve.wait_ge(S["cv_step"], 9 * i + 2)
                        nc.vector.tensor_scalar(out=cv_y, in0=cv_x, scalar1=tap,
                                                scalar2=vec[:, bass.ds(V_CB + i, 1)], op0=ALU.mult, op1=ALU.add
                                                ).then_inc(S["cv_step"], 1)
                        return
                    dve.wait_ge(S["cv_step"], 9 * i + (3 if n == 0 else 4))
                    x_, y_ = (cv_x[:, 0:T - 1], cv_y[:, 1:T]) if n == 0 else (cv_x[:, 1:T], cv_y[:, 0:T - 1])
                    nc.vector.scalar_tensor_tensor(out=y_, in0=x_, scalar=tap, in1=y_, op0=ALU.mult, op1=ALU.add
                                                   ).then_inc(S["cv_step"], 1)

                TAPS = {5: [1], 6: [0, 2]}

                logits(0)
                logits(1)
                for u in range(16):
                    a, qt = divmod(u, NT)
                    g = 16 * i + u
                    w = 6 * P if window(qt)[1] == 512 else 7 * P
                    dve.wait_ge(S["na_pt_hi"], g + 1)
                    nc.vector.tensor_tensor(pt_lo[:, 0:w], ps[:, 4 * BANK:4 * BANK + w], pt_hi[:, 0:w].bitcast(F),
                                            ALU.subtract).then_inc(S["na_pt_lo"], 1)
                    nc.vector.reciprocal(rinv[:, u % 2:u % 2 + 1], rsum[:, u % 2:u % 2 + 1]
                                         ).then_inc(S["na_inv"], 1)
                    if u + 2 < 16:
                        logits(u + 2)
                    for h in HALF_TAKEN.get(u, []):
                        conv_half(h)
                    for n in TAPS.get(u, []):
                        conv_tap(n)
                    dve.wait_ge(S["na_inv"], g + 1)
                    dve.wait_ge(S["na_pv"], g + 1)
                    nc.vector.tensor_scalar(out=o1[:, qt, a * HD:(a + 1) * HD], in0=na_o,
                                            scalar1=rinv[:, u % 2:u % 2 + 1], scalar2=None, op0=ALU.mult
                                            ).then_inc(S["na_out"], 1)
                dve.wait_ge(S["cv_step"], 9 * i + 9)
                nc.vector.tensor_tensor(cv_y, cv_x, cv_y, ALU.mult).then_inc(S["conv_done"], 1)
                dve.wait_ge(S["na_ot"], i + 1)
                nc.vector.tensor_tensor(res[:, bass.ds(i, 1), :].rearrange("p o t -> p (o t)"),
                                        ps[:, 0:2 * BANK], tB, ALU.mult).then_inc(S["pair_done"], 1)
            split_lo("mix", act_hi, act_lo)

            def residual(name, T0, gated):
                L = LINEAR[name]
                dve.drain().then_inc(S["lin_evac"], 2)
                with dve.Fori(0, 4) as i:
                    for s in range(2):
                        dve.wait_ge(S["tile_done"], 2 * i + (T0 + s + 1))
                        dve.wait_ge(S[f"xres_in{s}"], 16 * i + (64 * L + 16))
                        out = res[:, bass.ds(2 * i + s, 1), :].rearrange("p o t -> p (o t)")
                        src = ps[:, 2 * s * BANK:(2 * s + 2) * BANK]
                        if gated:
                            gate = mod[:, bass.ds(16 + 2 * i + s, 1), 0:1].rearrange("p a b -> p (a b)")
                            nc.vector.scalar_tensor_tensor(out=out, in0=src, scalar=gate, in1=stage[:, s, :],
                                                           op0=ALU.mult, op1=ALU.add).then_inc(S["lin_evac"], 1)
                        else:
                            nc.vector.tensor_tensor(out, src, stage[:, s, :], ALU.add).then_inc(S["lin_evac"], 1)

            residual("out", T_OUT, True)
            dve.wait_ge(S["lin_evac"], 10)
            norm_sum("x1")
            dve.wait_ge(S["fl_exp"], 1)
            nc.vector.tensor_tensor(wfl_lo[:, :, :], wfl[:, :, :], wfl_hi[:, :, :].bitcast(F), ALU.subtract
                                    ).then_inc(S["fl_z"], 1)
            norm_scale("x1")
            dve.wait_ge(S["fl_proj"], 1)
            nc.vector.tensor_tensor(zf[:, :, :], ps[:, 0:64].rearrange("p (t h) -> p t h", h=8),
                                    vec[:, V_BF:V_BF + 8].rearrange("p (o h) -> p o h", o=1)
                                    .to_broadcast([P, NT, 8]), ALU.add).then_inc(S["fl_z"], 1)
            dve.wait_ge(S["fl_z"], 2)
            nc.vector.scalar_tensor_tensor(out=ef[:, :, :], in0=zf[:, :, :], scalar=-1.0, in1=zf[:, :, :],
                                           op0=ALU.mult, op1=ALU.max).then_inc(S["fl_z"], 1)
            dve.wait_ge(S["fl_ln"], 1)
            nc.vector.scalar_tensor_tensor(out=logf[:, :, :], in0=zf[:, :, :], scalar=0.0, in1=ef[:, :, :],
                                           op0=ALU.min, op1=ALU.subtract).then_inc(S["fl_logf"], 1)
            dve.wait_ge(S["fl_in"], 32)
            for j in range(2):
                if j:
                    dve.wait_ge(S["lam_step"], 1)
                nc.vector.tensor_tensor_reduce(out=lamp[:, :], in0=lamv[:, 2 * j, :], in1=lamv[:, 2 * j + 1, :],
                                               scale=1.0, scalar=0.0, op0=ALU.mult, op1=ALU.add,
                                               accum_out=lam2[:, j:j + 1]).then_inc(S["lam_step"], 1)
            dve.wait_ge(S["lam_exp"], 1)
            nc.vector.tensor_scalar(out=nlam[:, :], in0=lam2[:, 1:2], scalar1=-LAMBDA_INIT, scalar2=None,
                                    op0=ALU.add).then_inc(S["lam_step"], 1)
            dve.wait_ge(S["lam_step"], 3)
            nc.vector.tensor_tensor(nlam[:, :], nlam[:, :], lam2[:, 0:1], ALU.subtract).then_inc(S["lam_step"], 1)
            dve.wait_ge(S["fl_cum"], 1)
            nc.vector.tensor_copy(cumq[:, :, :], bank(1, 0, 64).rearrange("p (t h) -> p t h", h=8)
                                  ).then_inc(S["fl_cumq"], 1)
            dve.wait_ge(S["fl_cum"], 2)
            nc.vector.tensor_scalar(out=negc[:, :], in0=ps[0:8, 2 * BANK:4 * BANK], scalar1=-1.0, scalar2=None,
                                    op0=ALU.mult).then_inc(S["fl_negc"], 1)
            dve.wait_ge(S["lam_step"], 4)
            dve.wait_ge(S["fl_out"], 16)
            dve.wait_ge(S["spilled"], 16)
            dve.drain().then_inc(S["df_done"], 1)
            dve.drain().then_inc(S["fx_done"], 1)
            dve.drain().then_inc(S["gate_out0"], 16)
            dve.drain().then_inc(S["gate_out1"], 16)
            dve.drain().then_inc(S["gate_copied"], 1)
            with dve.Fori(0, 4) as i:
                def low_parts(hi_sem, lo_sem):
                    dve.wait_ge(S[hi_sem], 3 * i + 1)
                    nc.vector.scalar_tensor_tensor(out=q_lo[:, :], in0=ps[:, 0:2 * BANK], scalar=0.125,
                                                   in1=q_hi[:, :].bitcast(F), op0=ALU.mult,
                                                   op1=ALU.subtract).then_inc(S[lo_sem], 1)
                    dve.wait_ge(S[hi_sem], 3 * i + 2)
                    nc.vector.tensor_tensor(va_lo[:, :, :], ps[:, 4 * BANK:6 * BANK].rearrange(
                        "p (t d) -> p t d", d=P), va_hi[:, :, :].bitcast(F), ALU.subtract).then_inc(S[lo_sem], 1)
                    dve.wait_ge(S[hi_sem], 3 * i + 3)
                    nc.vector.tensor_tensor(k_lo[:, :], ps[:, 2 * BANK:4 * BANK], k_hi[:, :].bitcast(F),
                                            ALU.subtract).then_inc(S[lo_sem], 1)

                low_parts("df_hi", "df_lo")
                dve.wait_ge(S["strip_in"], 16 * i + 16)

                def logits(u):
                    n = P * (u + 1)
                    for m, buf in enumerate((stage, pb)):
                        c = 2 * (u % 2) + m
                        dve.wait_ge(S["df_scores"], 16 * i + (2 * u + m + 1))
                        if u >= 2:
                            dve.wait_ge(S["df_pt"], 8 * i + (u - 1))
                        note()
                        nc.vector.tensor_tensor_reduce(out=buf[:, u % 2, 0:n], in0=ps[:, 2 * m * BANK:2 * m * BANK + n],
                                                       in1=strip[:, T - n:T], scale=-1.0, scalar=BIG,
                                                       op0=ALU.add, op1=ALU.min, accum_out=nm[:, c:c + 1]
                                                       ).then_inc(S["df_logits"], 1)

                logits(0)
                for u in range(NT):
                    n = P * (u + 1)
                    g = 8 * i + u
                    c = 2 * (u % 2)
                    dve.wait_ge(S["df_probs"], 16 * i + (2 * u + 2))
                    if u >= 2:
                        dve.wait_ge(S["df_out"], 16 * i + (2 * u - 2))
                    nc.vector.reciprocal(rinv[:, c:c + 2], rsum[:, c:c + 2]).then_inc(S["df_inv"], 1)
                    dve.wait_ge(S["df_inv"], 16 * i + (2 * u + 1))
                    nc.vector.tensor_scalar(out=rinv[:, c + 1:c + 2], in0=rinv[:, c + 1:c + 2], scalar1=nlam[:, 0:1],
                                            scalar2=rsum[:, c:c + 1], op0=ALU.mult, op1=ALU.mult
                                            ).then_inc(S["df_inv"], 1)
                    dve.wait_ge(S["df_inv"], 16 * i + (2 * u + 2))
                    nc.vector.scalar_tensor_tensor(out=stage[:, u % 2, 0:n], in0=pb[:, u % 2, 0:n],
                                                   scalar=rinv[:, c + 1:c + 2], in1=stage[:, u % 2, 0:n],
                                                   op0=ALU.mult, op1=ALU.add).then_inc(S["df_comb"], 1)
                    if u + 1 < NT:
                        logits(u + 1)
                    dve.wait_ge(S["df_pt_hi"], g + 1)
                    nc.vector.tensor_tensor(p8_lo[:, 0:n], ps[:, 4 * BANK:4 * BANK + n], p8_hi[:, 0:n].bitcast(F),
                                            ALU.subtract).then_inc(S["df_pt_lo"], 1)
                dve.wait_ge(S["df_ms"], i + 1)
                nc.vector.reciprocal(ms8[:, :], ms8[:, :]).then_inc(S["df_rstd"], 1)
                dve.wait_ge(S["df_rstd"], i + 1)
                nc.vector.tensor_tensor(o2[:, :, :], o2[:, :, :],
                                        ms8[:, :].rearrange("p (t o) -> p t o", o=1).to_broadcast([P, NT, P]),
                                        ALU.mult).then_inc(S["df_normed"], 1)
                low_parts("fx_hi", "fx_lo")
                dve.wait_ge(S["df_ot"], i + 1)
                nc.vector.tensor_scalar(out=res[:, bass.ds(i, 1), :].rearrange("p o t -> p (o t)"),
                                        in0=ps[:, 4 * BANK:6 * BANK], scalar1=subg[:, 0:1], scalar2=None,
                                        op0=ALU.mult).then_inc(S["df_done"], 1)

                def fox_logits(u):
                    n = P * (u % NT + 1)
                    g = 16 * i + u
                    b0 = 2 * (u % 2) * BANK
                    dve.wait_ge(S["fx_scores"], g + 1)
                    dve.wait_ge(S["fx_bias_m"], g + 1)
                    if u >= 2:
                        dve.wait_ge(S["fx_pt"], g - 1)
                    note()
                    nc.vector.tensor_tensor_reduce(out=stage[:, u % 2, 0:n], in0=ps[:, b0:b0 + n],
                                                   in1=bt[:, u % 2, 0:n], scale=-1.0, scalar=BIG, op0=ALU.add,
                                                   op1=ALU.min, accum_out=nm[:, u % 2:u % 2 + 1]
                                                   ).then_inc(S["fx_logits"], 1)

                fox_logits(0)
                fox_logits(1)
                for u in range(2 * NT):
                    a, qt = divmod(u, NT)
                    n = P * (qt + 1)
                    g = 16 * i + u
                    dve.wait_ge(S["fx_pt_hi"], g + 1)
                    nc.vector.tensor_tensor(p8_lo[:, 0:n], ps[:, 4 * BANK:4 * BANK + n], p8_hi[:, 0:n].bitcast(F),
                                            ALU.subtract).then_inc(S["fx_pt_lo"], 1)
                    nc.vector.reciprocal(rinv[:, u % 2:u % 2 + 1], rsum[:, u % 2:u % 2 + 1]
                                         ).then_inc(S["fx_inv"], 1)
                    if u + 2 < 2 * NT:
                        fox_logits(u + 2)
                    dve.wait_ge(S["fx_inv"], g + 1)
                    dve.wait_ge(S["fx_pv"], g + 1)
                    nc.vector.tensor_scalar(out=o2[:, qt, a * HD:(a + 1) * HD], in0=bank(6, 0, HD),
                                            scalar1=rinv[:, u % 2:u % 2 + 1], scalar2=None, op0=ALU.mult
                                            ).then_inc(S["fx_out"], 1)
                dve.wait_ge(S["fx_ot"], i + 1)
                nc.vector.tensor_copy(res[:, bass.ds(4 + i, 1), :].rearrange("p o t -> p (o t)"),
                                      ps[:, 0:2 * BANK]).then_inc(S["fx_done"], 1)
            split_lo("y", y_hi, y_lo)
            with dve.Fori(0, 4) as i:
                for s in range(2):
                    g = gate_g[s]
                    dve.wait_ge(S["mg_sig"], 2 * i + (s + 1))
                    dve.wait_ge(S["tile_done"], 2 * i + (T_MERGE + s + 1))
                    for n in range(2):
                        src = ps[:, (4 * s + 2 * n) * BANK:(4 * s + 2 * n + 2) * BANK]
                        nc.vector.tensor_tensor(g[:, n, :], src, g[:, n, :], ALU.mult).then_inc(S["mg_step"], 1)
                    dve.wait_ge(S["mg_step"], 6 * i + (3 * s + 2))
                    nc.vector.tensor_tensor(g[:, 0, :], g[:, 0, :], g[:, 1, :], ALU.add).then_inc(S["mg_step"], 1)
                    dve.wait_ge(S["hi_ready"], 2 * i + (8 * FILL["merged"] + s + 1))
                    note()
                    nc.vector.tensor_tensor(act_lo[:, bass.ds(2 * i + s, 1), :].rearrange("p o t -> p (o t)"),
                                            g[:, 0, :],
                                            act_hi[:, bass.ds(2 * i + s, 1), :].rearrange("p o t -> p (o t)")
                                            .bitcast(F), ALU.subtract).then_inc(S["lo_ready"], 1)
            residual("wo", T_WO, False)
            dve.wait_ge(S["lin_evac"], 20)
            norm_sum("mem")
            norm_scale("mem")
            norm_sum("x2")
            norm_scale("x2")
            dve.drain().then_inc(S["mm_out"], 1)
            with dve.Fori(0, 4) as i:
                t0 = 6 * i + T_MEM
                for c in range(2):
                    dve.wait_ge(S["mm_hi"], 5 * i + (c + 1))
                    nc.vector.scalar_tensor_tensor(out=mq_lo[:, c, :], in0=ps[:, 2 * c * BANK:(2 * c + 2) * BANK],
                                                   scalar=0.0625, in1=mq_hi[:, c, :].bitcast(F), op0=ALU.mult,
                                                   op1=ALU.subtract).then_inc(S["mm_lo"], 1)
                for c in range(2):
                    dve.wait_ge(S["mm_hi"], 5 * i + (c + 3))
                    nc.vector.tensor_tensor(mk_lo[:, c, :], bank(4 + c, 0, C), mk_hi[:, c, :].bitcast(F),
                                            ALU.subtract).then_inc(S["mm_lo"], 1)
                dve.wait_ge(S["mm_hi"], 5 * i + 5)
                nc.vector.tensor_tensor(mv_lo[:, :, :], bank(6).rearrange("p (t d) -> p t d", d=C),
                                        mv_hi[:, :, :].bitcast(F), ALU.subtract).then_inc(S["mm_lo"], 1)

                def row_max(u):
                    dve.wait_ge(S["mm_scores"], 8 * i + (u + 1))
                    if u >= 2:
                        dve.wait_ge(S["mm_probs"], 8 * i + (u - 1))
                    nc.vector.tensor_reduce(out=nm[:, u % 2:u % 2 + 1], in_=bank(u % 2, 0, C), axis=AX.X,
                                            op=ALU.max, negate=True).then_inc(S["mm_max"], 1)

                row_max(0)
                row_max(1)
                for u in range(NT):
                    g = 8 * i + u
                    dve.wait_ge(S["mm_pt_hi"], g + 1)
                    nc.vector.tensor_tensor(mpt_lo[:, u % 2, :], bank(2 + u % 2, 0, C),
                                            mpt_hi[:, u % 2, :].bitcast(F), ALU.subtract
                                            ).then_inc(S["mm_pt_lo"], 1)
                    nc.vector.reciprocal(rinv[:, u % 2:u % 2 + 1], rsum[:, u % 2:u % 2 + 1]
                                         ).then_inc(S["mm_inv"], 1)
                    if u + 2 < NT:
                        row_max(u + 2)
                    dve.wait_ge(S["mm_inv"], g + 1)
                    dve.wait_ge(S["mm_pv"], g + 1)
                    nc.vector.tensor_scalar(out=mo[:, u, :], in0=bank(4 + u % 2, 0, C),
                                            scalar1=rinv[:, u % 2:u % 2 + 1], scalar2=None, op0=ALU.mult
                                            ).then_inc(S["mm_out"], 1)
            split_lo("memo", act_hi, act_lo)
            residual("wom", T_WOM, False)
            dve.wait_ge(S["lin_evac"], 30)
            norm_sum("x3")
            norm_scale("x3")
            dve.drain().then_inc(S["a_lo"], 2)
            dve.drain().then_inc(S["mlp_acc"], 2)
            with dve.Fori(0, 4) as b:
                with dve.Fori(0, 4) as i:
                    for s in range(2):
                        n1 = 8 * b + 2 * i + s
                        dve.wait_ge(S["a_relu"], n1 + 1)
                        nc.vector.tensor_tensor(stage[:, s, :], stage[:, s, :], stage[:, s, :], ALU.mult
                                                ).then_inc(S["a_sq"], 1)
                        dve.wait_ge(S["a_hi"], n1 + 1)
                        nc.vector.tensor_tensor(a_lo[:, bass.ds(2 * i + s, 1), :].rearrange("p o t -> p (o t)"),
                                                stage[:, s, :],
                                                a_hi[:, bass.ds(2 * i + s, 1), :].rearrange("p o t -> p (o t)")
                                                .bitcast(F), ALU.subtract).then_inc(S["a_lo"], 1)
                with dve.Fori(0, 4) as i:
                    for s in range(2):
                        dve.wait_ge(S["tile_done"], 16 * b + 2 * i + (T_MLP + 8 + s + 1))
                        out = res[:, bass.ds(2 * i + s, 1), :].rearrange("p o t -> p (o t)")
                        dve.wait_ge(S["mlp_acc"], 8 * b + 2)
                        nc.vector.tensor_tensor(out, ps[:, (4 + 2 * s) * BANK:(6 + 2 * s) * BANK], out, ALU.add
                                                ).then_inc(S["mlp_acc"], 1)
            dve.wait_ge(S["mlp_acc"], 34)
            norm_sum("final")
            for k in range(KT):
                nc.vector.scalar_tensor_tensor(out=res[:, k, :], in0=res[:, k, :], scalar=gain("final", k),
                                               in1=ps[:, 2 * BANK:4 * BANK], op0=ALU.mult, op1=ALU.mult
                                               ).then_inc(S["y_ready"], 1)

        @block.tensor
        def _(pe):
            def mm3(out, wh, wl, xh, xl, start, stop):
                nc.tensor.matmul(out, wh, xh, start=start, stop=False)
                nc.tensor.matmul(out, wh, xl, start=False, stop=False)
                return nc.tensor.matmul(out, wl, xh, start=False, stop=stop)

            def project(s, b0, xh, xl, width, ks=range(KT), filled=None):
                for c in range(0, width, BANK):
                    n = min(BANK, width - c)
                    for k in ks:
                        if filled is not None and c == 0:
                            pe.wait_ge(S["lo_ready"], filled + k + 1)
                        last = mm3(ps[:, b0 * BANK + c:b0 * BANK + c + n], w_hi[:, s, k, :], w_lo[:, s, k, :],
                                   xh[:, k, c:c + n], xl[:, k, c:c + n], k == ks[0], k == ks[-1])
                return last

            def project_half(s, b0, c):
                x = slice(c * BANK, (c + 1) * BANK)
                for k in range(KT):
                    last = mm3(bank(b0 + c), w_hi[:, s, k, :], w_lo[:, s, k, :], act_hi[:, k, x], act_lo[:, k, x],
                               k == 0, k == KT - 1)
                return last

            def project_tok(s, out_of, xh, xl, nt):
                for t in range(nt):
                    for k in range(KT):
                        last = mm3(out_of(t), xh[:, k, t * P:(t + 1) * P], xl[:, k, t * P:(t + 1) * P],
                                   w_hi[:, s, k, :], w_lo[:, s, k, :], k == 0, k == KT - 1)
                return last

            def tile_ready(idx):
                pe.wait_ge(S["w_split"], idx + 1)

            def sum_squares(name):
                w, ac, r = NB[name][1], NB[name][4], NORM[name]
                pe.wait_ge(S["acc_done"], 8 * r + 8)
                if r:
                    pe.wait_ge(S["rms_ready"], r)
                for t in range(w // P):
                    last = nc.tensor.matmul(bank(2, t, t + 1), ac[:, t * P:(t + 1) * P], ones[:, 0:1],
                                            start=True, stop=True)
                last.then_inc(S["ss_ready"], 1)
                pe.wait_ge(S["rstd_ready"], r + 1)
                for t in range(w // P):
                    last = nc.tensor.matmul(ps[:, 2 * BANK + t * P:2 * BANK + (t + 1) * P],
                                            rt[:, t:t + 1].to_broadcast([P, P]), ident, start=True, stop=True)
                last.then_inc(S["rstd_spread"], 1)

            pe.wait_ge(S["c_silu"], 1)
            for t in range(24):
                n = t // 3
                pe.wait_ge(S[f"ada_in{n % 4}"], 16 * (n // 4) + 16)
                for k in range(KT):
                    last = nc.tensor.matmul(ps[:, 2 * t:2 * t + 2], ada[:, t % ADA_R, k, :], cond[:, k, :],
                                            start=(k == 0), stop=(k == KT - 1))
                last.then_inc(S["ada_used"], 1)
            sum_squares("x0")
            sum_squares("ctx")
            pe.wait_ge(S["lo_ready"], 8 * FILL["ctx"] + 8)
            with pe.Fori(0, 2) as i:
                for s in range(2):
                    j = 2 * i + s
                    tile_ready(2 * i + (T_CTX + s))
                    pe.wait_ge(S["ck_done"], j + 1)
                    project(s, 0, hc_hi, hc_lo, C).then_inc(S["tile_done"], 1)
                    pe.wait_ge(S["ck_sq"], j + 1)
                    nc.tensor.matmul(bank(1, 0, C), bd64, ksq[:, :], start=True, stop=True
                                     ).then_inc(S["ck_ss"], 1)
            pe.wait_ge(S["ck_done"], 5)
            with pe.Fori(0, 2) as i:
                for s in range(2):
                    tile_ready(2 * i + (T_CTX + 4 + s))
                    pe.wait_ge(S["cv_done"], 2 * i + (s + 1))
                    project_tok(s, lambda t: bank(0, t * P, (t + 1) * P), hc_hi, hc_lo, CT
                                ).then_inc(S["tile_done"], 1)
            with pe.Fori(0, 4) as i:
                t0 = 8 * i + T_ATT
                tile_ready(t0)
                pe.wait_ge(S["pair_done"], i + 1)
                project(0, 0, act_hi, act_lo, T).then_inc(S["tile_done"], 1)
                tile_ready(t0 + 1)
                project(1, 2, act_hi, act_lo, T).then_inc(S["tile_done"], 1)

                def head_ss(n, sq, b0):
                    pe.wait_ge(S["qk_sq"], 2 * i + (n + 1))
                    for t in range(NT):
                        last = nc.tensor.matmul(bank(b0, 2 * t, 2 * t + 2), sq[:, t * P:(t + 1) * P],
                                                bd64[:, 0:P:HD], start=True, stop=True)
                    last.then_inc(S["qk_ss"], 1)

                def head_spread(n, sq, b0):
                    pe.wait_ge(S["qk_rstd"], 4 * i + (2 * n + 2))
                    for t in range(NT):
                        last = nc.tensor.transpose(ps[:, b0 * BANK + t * P:b0 * BANK + (t + 1) * P],
                                                   sq[:, t * P:(t + 1) * P], ident)
                    last.then_inc(S["qk_spread"], 1)

                def half_turn(n, hi, lo, b0):
                    pe.wait_ge(S["qk_plain_lo"], 2 * i + (n + 1))
                    for c in range(2):
                        nc.tensor.matmul(bank(b0 + c), perm[:, :], hi[:, c * BANK:(c + 1) * BANK],
                                         start=True, stop=False)
                        last = nc.tensor.matmul(bank(b0 + c), perm[:, :], lo[:, c * BANK:(c + 1) * BANK],
                                                start=False, stop=True)
                    last.then_inc(S["qk_perm"], 1)

                head_ss(0, tB, 0)
                tile_ready(t0 + 2)
                project(0, 4, act_hi, act_lo, T).then_inc(S["tile_done"], 1)
                head_spread(0, tB, 0)
                head_ss(1, tD, 2)
                pe.wait_ge(S["v_raw"], i + 1)
                for t in range(NT):
                    last = nc.tensor.transpose(ps[:, 4 * BANK + t * P:4 * BANK + (t + 1) * P],
                                               stage[:, 1, t * P:(t + 1) * P], ident)
                last.then_inc(S["v_turned"], 1)
                tile_ready(t0 + 3)
                pe.wait_ge(S["conv_done"], i + 1)
                project_half(1, 6, 0)
                head_spread(1, tD, 2)
                half_turn(0, qp_hi, qp_lo, 0)
                project_half(1, 6, 1).then_inc(S["tile_done"], 1)
                half_turn(1, kr_hi, kr_lo, 2)
                tile_ready(t0 + 4)
                pe.wait_ge(S["v_lo"], i + 1)
                project(0, 4, act_hi, act_lo, T).then_inc(S["tile_done"], 1)

                def conv_steps(first, n_steps):
                    for step in range(first, first + n_steps):
                        n, c, k = step // 16, step // 8 % 2, step % 8
                        w, h = (n + 1) % 2, step // 8
                        if step % 16 == 0:
                            tile_ready(t0 + 5 + n)
                        if k == 0:
                            if h == 0:
                                pe.wait_ge(S["za_done"], i + 1)
                            elif h >= 2:
                                pe.wait_ge(S["cv_step"], 9 * i + (1, 2, 6, 7)[h - 2])
                        x = slice(c * BANK, (c + 1) * BANK)
                        last = mm3(bank(6 + c), w_hi[:, w, k, :], w_lo[:, w, k, :], act_hi[:, k, x], act_lo[:, k, x],
                                   k == 0, k == KT - 1)
                        if k == KT - 1:
                            last.then_inc(S["cv_half"], 1)
                            if c == 1:
                                pe.drain().then_inc(S["tile_done"], 1)

                def scores(u):
                    a, qt = divmod(u, NT)
                    key0, nl, _ = window(qt)
                    b0 = 2 * (u % 2) * BANK
                    h = slice(a * HD, (a + 1) * HD)
                    q = slice(qt * P, (qt + 1) * P)
                    if u == 0:
                        pe.wait_ge(S["qk_lo"], 2 * i + 2)
                        pe.wait_ge(S["c_lo"], 2 * i + 2)
                    if u >= 2:
                        pe.wait_ge(S["na_logits"], 16 * i + (u - 1))
                    for c in range(0, nl, BANK):
                        n = min(BANK, nl - c)
                        mm3(ps[:, b0 + c:b0 + c + n], qr_hi[h, q], qr_lo[h, q],
                            kr_hi[h, key0 + c:key0 + c + n], kr_lo[h, key0 + c:key0 + c + n], True, True)
                    mm3(ps[:, b0 + nl:b0 + nl + C], qp_hi[h, q], qp_lo[h, q], kc_hi[h, :], kc_lo[h, :],
                        True, True).then_inc(S["na_scores"], 1)

                scores(0)
                scores(1)
                conv_steps(0, 1)
                for u in range(16):
                    a, qt = divmod(u, NT)
                    key0, nl, _ = window(qt)
                    g = 16 * i + u
                    lat = [(c, min(P, nl - c)) for c in range(0, nl, P)]
                    blocks = lat + [(nl, P), (nl + P, P)]
                    pe.wait_ge(S["na_probs"], g + 1)
                    if u > 0:
                        pe.wait_ge(S["na_out"], g)
                    else:
                        pe.wait_ge(S["cv_u"], i + 1)
                    for j, (c, n) in enumerate(blocks):
                        last = nc.tensor.transpose(ps[:, 4 * BANK + j * P:4 * BANK + (j + 1) * P],
                                                   stage[:, u % 2, c:c + P], ident)
                    last.then_inc(S["na_pt"], 1)
                    if u + 2 < 16:
                        scores(u + 2)
                    conv_steps(3 * u + 1, 2)
                    pe.wait_ge(S["na_pt_lo"], g + 1)
                    hv = slice(a * HD, (a + 1) * HD)
                    for j, (c, n) in enumerate(blocks):
                        if j < len(lat):
                            vh, vl = v_hi[0:n, key0 // P + j, hv], v_lo[0:n, key0 // P + j, hv]
                        else:
                            vh, vl = vc_hi[:, j - len(lat), hv], vc_lo[:, j - len(lat), hv]
                        last = mm3(na_o, pt_hi[0:n, j * P:(j + 1) * P],
                                   pt_lo[0:n, j * P:(j + 1) * P], vh, vl, j == 0, j == len(blocks) - 1)
                    last.then_inc(S["na_pv"], 1)
                    if u < 15:
                        conv_steps(3 * u + 3, 1)
                pe.wait_ge(S["na_out"], 16 * i + 16)
                for t in range(NT):
                    last = nc.tensor.transpose(ps[:, t * P:(t + 1) * P], o1[:, t, :], ident)
                last.then_inc(S["na_ot"], 1)
            def linear(name, T0):
                L = LINEAR[name]
                with pe.Fori(0, 4) as i:
                    for s in range(2):
                        tile_ready(2 * i + (T0 + s))
                        pe.wait_ge(S["lin_evac"], 2 * i + (10 * L + s + 1))
                        project(s, 2 * s, act_hi, act_lo, T).then_inc(S["tile_done"], 1)

            pe.wait_ge(S["lo_ready"], 8 * FILL["mix"] + 8)
            linear("out", T_OUT)
            sum_squares("x1")
            pe.wait_ge(S["lo_ready"], 8 * FILL["x1"] + 8)
            for t in range(NT):
                for k in range(KT):
                    last = mm3(ps[:, 8 * t:8 * t + 8], act_hi[:, k, t * P:(t + 1) * P],
                               act_lo[:, k, t * P:(t + 1) * P], wfl_hi[:, k, :], wfl_lo[:, k, :],
                               k == 0, k == KT - 1)
            last.then_inc(S["fl_proj"], 1)
            pe.wait_ge(S["fl_logf"], 1)
            for t in range(NT):
                for j in range(t + 1):
                    last = nc.tensor.matmul(bank(1, 8 * t, 8 * t + 8), tri if j == t else ones, logf[:, j, :],
                                            start=(j == 0), stop=(j == t))
            last.then_inc(S["fl_cum"], 1)
            for t in range(NT):
                for j in range(t + 1):
                    last = nc.tensor.matmul(ps[0:8, 2 * BANK + t * P:2 * BANK + (t + 1) * P], logf[:, j, :],
                                            tri if j == t else ones, start=(j == 0), stop=(j == t))
            last.then_inc(S["fl_cum"], 1)
            pe.wait_ge(S["fl_negc"], 1)
            with pe.Fori(0, 4) as i:
                t0 = 10 * i + T_MIX

                def operands(base):
                    tile_ready(t0 + base)
                    project(base % 2, 4, act_hi, act_lo, T).then_inc(S["tile_done"], 1)
                    tile_ready(t0 + base + 1)
                    project((base + 1) % 2, 0, act_hi, act_lo, T).then_inc(S["tile_done"], 1)
                    pe.wait_ge(S["v_raw"], 2 * i + (5 + base // 5))
                    for t in range(NT):
                        last = nc.tensor.transpose(ps[:, 4 * BANK + t * P:4 * BANK + (t + 1) * P],
                                                   stage[:, 1, t * P:(t + 1) * P], ident)
                    last.then_inc(S["v_turned"], 1)
                    tile_ready(t0 + base + 2)
                    project(base % 2, 2, act_hi, act_lo, T).then_inc(S["tile_done"], 1)

                def gate_steps(first, n_steps):
                    for step in range(first, first + n_steps):
                        n, h, k = step // 16, step // 8, step % 8
                        tile = (3, 4, 8, 9)[n]
                        if step % 16 == 0:
                            tile_ready(t0 + tile)
                        if k == 0:
                            pe.wait_ge(S["gate_copied"], 8 * i + (h + 1))
                        x = slice((h % 2) * BANK, (h % 2 + 1) * BANK)
                        last = mm3(bank(7), w_hi[:, tile % 2, k, :], w_lo[:, tile % 2, k, :], act_hi[:, k, x],
                                   act_lo[:, k, x], k == 0, k == KT - 1)
                        if k == KT - 1:
                            last.then_inc(S["gate_half"], 1)
                            if h % 2 == 1:
                                pe.drain().then_inc(S["tile_done"], 1)

                pe.wait_ge(S["fx_done"], i + 1)
                operands(0)
                gate_steps(0, 2)

                def scores(u):
                    n = P * (u + 1)
                    q = slice(u * P, (u + 1) * P)
                    for m in range(2):
                        h = slice(m * HD, (m + 1) * HD)
                        if u == 0:
                            pe.wait_ge(S["df_lo"], 3 * i + 3)
                        else:
                            pe.wait_ge(S["df_logits"], 16 * i + (2 * u - 1 + m))
                        for c in range(0, n, BANK):
                            w = min(BANK, n - c)
                            last = mm3(ps[:, 2 * m * BANK + c:2 * m * BANK + c + w], q_hi[h, q], q_lo[h, q],
                                       k_hi[h, c:c + w], k_lo[h, c:c + w], True, True)
                        last.then_inc(S["df_scores"], 1)

                scores(0)
                for u in range(NT):
                    g = 8 * i + u
                    if u + 1 < NT:
                        scores(u + 1)
                    if u > 0:
                        gate_steps(4 * u, 2)
                    pe.wait_ge(S["df_comb"], g + 1)
                    if u > 0:
                        pe.wait_ge(S["df_pt_lo"], g)
                    for j in range(u + 1):
                        last = nc.tensor.transpose(ps[:, 4 * BANK + j * P:4 * BANK + (j + 1) * P],
                                                   stage[:, u % 2, j * P:(j + 1) * P], ident)
                    last.then_inc(S["df_pt"], 1)
                    gate_steps(4 * u + 2, 2)
                    pe.wait_ge(S["df_pt_lo"], g + 1)
                    if u >= 1:
                        pe.wait_ge(S["df_out"], 16 * i + 2 * u)
                    for j in range(u + 1):
                        last = mm3(bank(6, 0, P), p8_hi[:, j * P:(j + 1) * P], p8_lo[:, j * P:(j + 1) * P],
                                   va_hi[:, j, :], va_lo[:, j, :], j == 0, j == u)
                    last.then_inc(S["df_pv"], 1)
                operands(5)
                pe.wait_ge(S["df_normed"], i + 1)
                pe.wait_ge(S["fx_lo"], 3 * i + 2)
                for t in range(NT):
                    last = nc.tensor.transpose(ps[:, 4 * BANK + t * P:4 * BANK + (t + 1) * P], o2[:, t, :], ident)
                last.then_inc(S["df_ot"], 1)
                gate_steps(32, 2)

                def fox_scores(u):
                    a, qt = divmod(u, NT)
                    n = P * (qt + 1)
                    b0 = 2 * (u % 2) * BANK
                    h = slice(a * HD, (a + 1) * HD)
                    q = slice(qt * P, (qt + 1) * P)
                    if u == 0:
                        pe.wait_ge(S["fx_lo"], 3 * i + 3)
                    if u >= 2:
                        pe.wait_ge(S["fx_logits"], 16 * i + (u - 1))
                    for c in range(0, n, BANK):
                        w = min(BANK, n - c)
                        last = mm3(ps[:, b0 + c:b0 + c + w], q_hi[h, q], q_lo[h, q], k_hi[h, c:c + w],
                                   k_lo[h, c:c + w], True, True)
                    last.then_inc(S["fx_scores"], 1)

                fox_scores(0)
                fox_scores(1)
                for u in range(2 * NT):
                    a, qt = divmod(u, NT)
                    g = 16 * i + u
                    pe.wait_ge(S["fx_probs"], g + 1)
                    if u > 0:
                        pe.wait_ge(S["fx_pt_lo"], g)
                    else:
                        pe.wait_ge(S["df_done"], i + 2)
                    for j in range(qt + 1):
                        last = nc.tensor.transpose(ps[:, 4 * BANK + j * P:4 * BANK + (j + 1) * P],
                                                   stage[:, u % 2, j * P:(j + 1) * P], ident)
                    last.then_inc(S["fx_pt"], 1)
                    if u + 2 < 2 * NT:
                        fox_scores(u + 2)
                    if u > 0:
                        gate_steps(32 + 2 * u, 2)
                    pe.wait_ge(S["fx_pt_lo"], g + 1)
                    if u > 0:
                        pe.wait_ge(S["fx_out"], g)
                    hv = slice(a * HD, (a + 1) * HD)
                    for j in range(qt + 1):
                        last = mm3(bank(6, 0, HD), p8_hi[:, j * P:(j + 1) * P], p8_lo[:, j * P:(j + 1) * P],
                                   va_hi[:, j, hv], va_lo[:, j, hv], j == 0, j == qt)
                    last.then_inc(S["fx_pv"], 1)
                pe.wait_ge(S["fx_out"], 16 * i + 16)
                for t in range(NT):
                    last = nc.tensor.transpose(ps[:, t * P:(t + 1) * P], o2[:, t, :], ident)
                last.then_inc(S["fx_ot"], 1)
            with pe.Fori(0, 4) as i:
                for s in range(2):
                    tile_ready(2 * i + (T_MERGE + s))
                    pe.wait_ge(S["lo_ready"], 2 * i + (8 * FILL["merged"] + s - 1))
                    project(s, 4 * s, y_hi, y_lo, T, range(0, 4), 8 * FILL["y"])
                    project(s, 4 * s + 2, y_hi, y_lo, T, range(4, 8), 8 * FILL["y"]).then_inc(S["tile_done"], 1)
            pe.wait_ge(S["lo_ready"], 8 * FILL["merged"] + 8)
            linear("wo", T_WO)
            sum_squares("mem")
            sum_squares("x2")
            pe.wait_ge(S["lo_ready"], 8 * FILL["x2"] + 8)
            with pe.Fori(0, 4) as i:
                t0 = 6 * i + T_MEM
                pe.wait_ge(S["mm_out"], 8 * i + 1)
                for c in range(2):
                    tile_ready(t0 + c)
                    project(c, 2 * c, act_hi, act_lo, T).then_inc(S["tile_done"], 1)
                for c in range(2):
                    tile_ready(t0 + 2 + c)
                    project(c, 4 + c, m_hi, m_lo, C).then_inc(S["tile_done"], 1)
                for c in range(2):
                    tile_ready(t0 + 4 + c)
                    project_tok(c, lambda t: bank(6, t * C + c * P, t * C + (c + 1) * P), m_hi, m_lo, CT
                                ).then_inc(S["tile_done"], 1)

                def scores(u):
                    if u == 0:
                        pe.wait_ge(S["mm_lo"], 5 * i + 5)
                    if u >= 2:
                        pe.wait_ge(S["mm_probs"], 8 * i + (u - 1))
                    q = slice(u * P, (u + 1) * P)
                    for c in range(2):
                        last = mm3(bank(u % 2, 0, C), mq_hi[:, c, q], mq_lo[:, c, q], mk_hi[:, c, :], mk_lo[:, c, :],
                                   c == 0, c == 1)
                    last.then_inc(S["mm_scores"], 1)

                scores(0)
                scores(1)
                for u in range(NT):
                    g = 8 * i + u
                    pe.wait_ge(S["mm_probs"], g + 1)
                    if u >= 2:
                        pe.wait_ge(S["mm_pt_lo"], g - 1)
                    for j in range(2):
                        last = nc.tensor.transpose(bank(2 + u % 2, j * P, (j + 1) * P), mp[:, u % 2, j * P:(j + 1) * P],
                                                   ident)
                    last.then_inc(S["mm_pt"], 1)
                    if u + 2 < NT:
                        scores(u + 2)
                    pe.wait_ge(S["mm_pt_lo"], g + 1)
                    if u >= 2:
                        pe.wait_ge(S["mm_out"], g)
                    for j in range(2):
                        last = mm3(bank(4 + u % 2, 0, C), mpt_hi[:, u % 2, j * P:(j + 1) * P],
                                   mpt_lo[:, u % 2, j * P:(j + 1) * P], mv_hi[:, j, :], mv_lo[:, j, :], j == 0, j == 1)
                    last.then_inc(S["mm_pv"], 1)
                pe.wait_ge(S["mm_out"], 8 * i + 9)
                for c in range(2):
                    for t in range(NT):
                        last = nc.tensor.transpose(ps[:, 2 * c * BANK + t * P:2 * c * BANK + (t + 1) * P],
                                                   mo[:, t, c * P:(c + 1) * P], ident)
                last.then_inc(S["mm_ot"], 1)
                pe.wait_ge(S["mm_done"], i + 1)
            pe.wait_ge(S["lo_ready"], 8 * FILL["memo"] + 8)
            linear("wom", T_WOM)
            sum_squares("x3")
            pe.wait_ge(S["lo_ready"], 8 * FILL["x3"] + 8)
            with pe.Fori(0, 4) as b:
                with pe.Fori(0, 4) as i:
                    for s in range(2):
                        tile_ready(16 * b + 2 * i + (T_MLP + s))
                        pe.wait_ge(S["a_lo"], 8 * b + 2 * i + (s + 1))
                        project(s, 2 * s, act_hi, act_lo, T).then_inc(S["tile_done"], 1)
                pe.wait_ge(S["a_lo"], 8 * b + 10)
                pe.sem_inc(S["issued"], 1)
                with pe.Fori(0, 4) as i:
                    for s in range(2):
                        tile_ready(16 * b + 2 * i + (T_MLP + 8 + s))
                        pe.wait_ge(S["mlp_acc"], 8 * b + 2 * i + (s + 1))
                        project(s, 4 + 2 * s, a_hi, a_lo, T).then_inc(S["tile_done"], 1)
            sum_squares("final")


def _tiles(w):
    n = w.shape[1] // P
    return w.reshape(KT, P, n, P).transpose(2, 1, 0, 3).reshape(n, P, KT * P)


def _cols(v):
    return v.reshape(-1, P).T


def _feature_major(a):
    return np.ascontiguousarray(a.T.reshape(KT, P, -1).transpose(1, 0, 2))


def _constants():
    ident = np.eye(P)
    tri = np.triu(np.ones((P, P)))
    ones = np.ones((P, P))
    bd = np.kron(np.eye(2), np.ones((HD, HD)))
    perm = np.zeros((P, P))
    for h in range(2):
        for ax in range(2):
            for f in range(16):
                lo, hi = h * 64 + ax * 32 + f, h * 64 + ax * 32 + 16 + f
                perm[hi, lo] = -1.0
                perm[lo, hi] = 1.0
    return np.concatenate([ident, tri, ones, bd, perm], 1).astype(np.float32)


def _rope():
    nf = HD // 4
    inv = (np.float32(10000.0) ** (-np.arange(nf, dtype=np.float32) / nf)).astype(np.float32)
    pos = np.arange(T)
    out = np.zeros((P, 2, T), np.float32)
    for p in range(P):
        ax, f = (p % HD) // 32, p % 16
        coord = (pos // GRID_W if ax == 0 else pos % GRID_W).astype(np.float32)
        ang = (coord * inv[f]).astype(np.float32)
        out[p, 0], out[p, 1] = np.cos(ang), np.sin(ang)
    return out


def _masks():
    q = np.arange(GRID_W)
    start = np.clip(q - 8, 0, GRID_W - 16)
    ok = (q[None, :] >= start[:, None]) & (q[None, :] < start[:, None] + 16)
    col = np.where(ok, 0.0, NEG)
    out = np.zeros((P, 10, GRID_W), np.float32)
    for a in range(2):
        for r in range(9):
            row_ok = r <= 7 if a == 0 else 1 <= r <= 8
            out[a * 64:(a + 1) * 64, r] = col if row_ok else NEG
        out[a * 64:(a + 1) * 64, 9] = col
    return out


def _buckets(n):
    d = np.arange(n)
    large = 16 + (np.log(np.maximum(d, 1) / 16.0) / math.log(8.0) * 16).astype(np.int64)
    return np.where(d < 16, d, np.minimum(large, 31))


def _place_rpb(rpb):
    out = np.zeros((8, 15, 127), rpb.dtype)
    out[:, :, 48:79] = rpb
    return out


def _place_rel(rel_bias):
    out = np.full((4, T + P - 1), NEG, rel_bias.dtype)
    out[:, :T] = rel_bias[_buckets(T)[::-1]].T
    return out


_OUT = "out_0_dram"


def kernel(**inputs):
    import concourse.bacc as bacc
    from concourse.bass_utils import run_bass_kernel_spmd

    a = {k: np.asarray(v) for k, v in inputs.items()}
    x_t, ctx_t, mem_t = (_feature_major(a[n][0]) for n in ("x", "ctx", "mem_2"))
    cond_t = np.stack([_cols(a["c"][0]), _cols(a["c_ctx"])], axis=-1)
    w_in, w_in2 = _tiles(a["w_in"][0]), a["w_in_2"][0]
    stream = [w_in[4:12]]
    for i in range(4):
        stream += [w_in[[i, 4 + i, 8 + i, 12 + i]]]
        stream += [w_in[[16 + i, 24 + i, 20 + i, 28 + i]]]
    stream += [_tiles(a["w_out"][0])]
    w2a, w2g = _tiles(w_in2[:, :3072]), _tiles(w_in2[:, 3080:])
    for i in range(4):
        stream += [w2a[[8 + i, i, 4 + i]], w2g[[2 * i, 8 + 2 * i]]]
        stream += [w2a[[20 + i, 12 + i, 16 + i]], w2g[[2 * i + 1, 9 + 2 * i]]]
    stream += [_tiles(np.concatenate([a["w_diff_out_2"][0], a["w_fox_out_2"][0]], 0))]
    stream += [_tiles(a["w_o_2"][0])]
    wq, wkv = _tiles(a["w_q_mem_2"][0]), _tiles(a["w_kv_mem_2"][0])
    for i in range(4):
        stream += [wq[2 * i:2 * i + 2], wkv[2 * i:2 * i + 2], wkv[8 + 2 * i:10 + 2 * i]]
    stream += [_tiles(a["w_o_mem_2"][0])]
    w1, w2 = _tiles(a["w1_2"][0]), a["w2_2"][0]
    for b in range(4):
        stream += [w1[8 * b:8 * b + 8], _tiles(w2[1024 * b:1024 * b + 1024])]
    w_stream = np.concatenate(stream, 0)
    assert w_stream.shape[0] == N_TILES

    small = np.concatenate(
        [_cols(a["norm_g"][0]), _cols(a["g_mix_2"][0]), _cols(a["g_mem_q_2"][0]), _cols(a["g_mem_kv_2"][0]),
         _cols(a["g_mlp_2"][0]), _cols(a["g_final_2"]), _cols(a["b_ada"][0]),
         np.tile(a["q_norm_g"][0], 2)[:, None], np.tile(a["k_norm_g"][0], 2)[:, None],
         _cols(a["conv_w"][0].reshape(-1)), _cols(a["conv_b"][0]), a["g_subln_2"][0][:, None],
         np.tile(a["b_forget_2"][0][None], (P, 1))], 1)
    assert small.shape == (P, V_COLS)
    lam4 = np.stack([a[f"lambda_{n}_2"][0] for n in ("q1", "k1", "q2", "k2")]).reshape(1, -1)
    w_fl = np.ascontiguousarray(w_in2[:, 3072:3080].reshape(KT, P, 8).transpose(1, 0, 2))
    ins = dict(x_t=x_t, ctx_t=ctx_t, mem_t=mem_t, cond_t=cond_t, small=small, lam4=lam4,
               consts=_constants(), rope=_rope(), masks=_masks(),
               rpb_pad=_place_rpb(a["rpb"][0]), rel_rows=_place_rel(a["rel_bias_2"]), w_fl=w_fl,
               w_ada=_tiles(a["w_ada"][0]), w_stream=w_stream)

    nc = bacc.Bacc("TRN2", target_bir_lowering=False, num_devices=1)
    arrays, aps = {}, {}
    for name, v in ins.items():
        v = np.ascontiguousarray(v)
        arrays[f"in_{name}_dram"] = v
        aps[name] = nc.dram_tensor(f"in_{name}_dram", v.shape, mybir.dt.from_np(v.dtype),
                                   kind="ExternalInput").ap()
    y_t = nc.dram_tensor(_OUT, (P, KT, T), F, kind="ExternalOutput").ap()
    program(nc, y_t=y_t, **aps)
    r = run_bass_kernel_spmd(nc, [arrays], core_ids=[0])
    y = r.results[0][_OUT]
    return np.ascontiguousarray(y.transpose(2, 1, 0).reshape(1, T, D))
```

```python
import math
from contextlib import ExitStack

import numpy as np

import concourse.bass as bass
from concourse import mybir

F = mybir.dt.float32
R = mybir.dt.float32r
ALU = mybir.AluOpType
ACT = mybir.ActivationFunctionType
AX = mybir.AxisListType

P = 128
D = 1024
T = 1024
C = 256
KT = D // P
NT = T // P
CT = C // P
BANK = 512
HD = 64
GRID_W = 64
NEG = -1.0e30
EPS = 1e-6
BIG = 3.0e38
LAMBDA_INIT = 0.8 - 0.6 * math.exp(-0.3 * 0)

T_ATT = 0
T_OUT = T_ATT + 32
T_MIX = T_OUT + 8
T_MERGE = T_MIX + 40
T_WO = T_MERGE + 8
T_MEM = T_WO + 8
T_WOM = T_MEM + 24
T_MLP = T_WOM + 8
N_TILES = T_MLP + 64

FILL = {n: i for i, n in enumerate(
    ["x0", "ctx", "mix", "x1", "y", "merged", "x2", "mem", "memo", "x3"])}
NORM = {n: i for i, n in enumerate(["x0", "ctx", "x1", "mem", "x2", "x3", "final"])}
SCALED = {n: i for i, n in enumerate(["x0", "ctx", "x1", "x2", "mem", "x3"])}
LINEAR = {"out": 0, "wo": 1, "wom": 2}
H_GATE = 4 * 6
H_MQ = H_GATE + 4 * 8

V_NORM, V_MIXG, V_MEMQ, V_MEMKV, V_MLPG, V_FIN, V_BADA = 0, 8, 16, 24, 32, 40, 48
V_QG, V_KG, V_CW, V_CB, V_SUB, V_BF = 72, 73, 74, 86, 90, 91
V_COLS = V_BF + 8
C_ID, C_TRI, C_ONE, C_BD, C_PERM = 0, 128, 256, 384, 512
C_COLS = 640

SEMS = """small_in ada_in0 ada_in1 ada_used ada_rows ada_turned x_in rows_in rope_in fl_in toeplitz
raw_in0 raw_in1 w_hi w_split tile_done c_sig c_silu ada_step const_ready sq_ready
acc_done ss_ready rms_ready rstd_ready rstd_spread scaled hi_ready lo_ready ck_sq ck_ss ck_rms ck_rstd
ck_done vc_raw vc_turned mask_in qk_sq qk_ss qk_rms qk_rstd qk_spread qk_normed qk_plain_hi
qk_plain_lo qk_perm qk_sin qk_cos qk_roped qk_hi qk_lo v_raw v_turned v_hi v_lo za_sig za_done c_hi
c_lo tile_in0 tile_in1 band_step na_scores
na_cmax na_logits na_probs na_pt na_pt_hi na_pt_lo na_pv na_inv na_out na_ot pair_done cv_u cv_sig
half_done cv_step conv_done conv_out lin_evac xres_in0 xres_in1 spilled fl_proj fl_z fl_exp fl_ln fl_logf
fl_cum fl_cumq fl_negc fl_out lam_step lam_exp op_hi op_lo strip_in df_scores df_logits df_probs
df_inv df_comb df_pt df_pt_hi df_pt_lo df_pv df_out df_ms df_rstd df_normed df_ot df_done
fx_ck_in fx_cq fx_bias fx_bias_m fx_scores fx_logits fx_probs fx_pt fx_pt_hi fx_pt_lo
fx_pv fx_inv fx_out fx_ot fx_done gate_copied gate_out0 gate_out1 mg_sig mg_step mq_split_hi
mq_split_lo mm_hi mm_lo mm_scores mm_max mm_probs mm_pt mm_pt_hi mm_pt_lo mm_pv mm_inv mm_out mm_ot mm_done a_relu a_sq a_hi a_lo mlp_acc y_ready y_out
issued""".split()


def program(nc, x_t, ctx_t, mem_t, cond_t, small, lam4, consts, rope, masks, rpb_pad, rel_rows,
            w_fl, w_ada, w_stream, y_t):
    ctx = ExitStack()
    with ctx:
        S = {n: ctx.enter_context(nc.semaphore(n)) for n in SEMS}

        def alloc(stack, name, shape, dt=F):
            return stack.enter_context(nc.sbuf_tensor(name, shape, dt))

        vec = alloc(ctx, "vec", [P, V_COLS])
        con = alloc(ctx, "con", [P, C_COLS])
        mod = alloc(ctx, "mod", [P, 24, 2])
        gs = alloc(ctx, "gs", [P, KT, 2])
        eps = alloc(ctx, "eps", [P, 1])
        one = alloc(ctx, "one", [P, 1])
        qg8 = alloc(ctx, "qg8", [P, 1])
        subg = alloc(ctx, "subg", [P, 1])
        rt = alloc(ctx, "rt", [P, 2 * NT])
        hr = alloc(ctx, "hr", [P, 2, 2 * NT])
        nm = alloc(ctx, "nm", [P, 4])
        cm = alloc(ctx, "cm", [P, 2])
        rsum = alloc(ctx, "rsum", [P, 4])
        rinv = alloc(ctx, "rinv", [P, 4])
        act_hi = alloc(ctx, "act_hi", [P, KT, T], R)
        act_lo = alloc(ctx, "act_lo", [P, KT, T], R)
        res = alloc(ctx, "res", [P, KT, T])
        raw = alloc(ctx, "raw", [P, 2, KT, P])
        w_hi = alloc(ctx, "w_hi", [P, 2, KT, P], R)
        w_lo = alloc(ctx, "w_lo", [P, 2, KT, P], R)
        stage = alloc(ctx, "stage", [P, 2, T])
        ps = ctx.enter_context(nc.psum_tensor("ps", [P, 8 * BANK], F))

        ident = con[:, C_ID:C_ID + P]
        tri = con[:, C_TRI:C_TRI + P]
        ones = con[:, C_ONE:C_ONE + P]
        bd64 = con[:, C_BD:C_BD + P]

        st1 = ExitStack()
        perm = alloc(st1, "perm", [P, P], R)
        hc_hi = alloc(st1, "hc_hi", [P, KT, C], R)
        hc_lo = alloc(st1, "hc_lo", [P, KT, C], R)
        st = ExitStack()
        ada = alloc(st, "ada", [P, 2, KT, BANK])
        cond = alloc(st, "cond", [P, KT, 2])
        csig = alloc(st, "csig", [P, KT, 2])
        mrow = alloc(st, "mrow", [2, 3 * D])
        acc0b = alloc(st, "acc0b", [P, T])
        ctxF = alloc(st, "ctxF", [P, KT, C])
        accc = alloc(st, "accc", [P, C])
        st.close()
        qp_hi = alloc(st1, "qp_hi", [P, T], R)
        qp_lo = alloc(st1, "qp_lo", [P, T], R)
        qr_hi = alloc(st1, "qr_hi", [P, T], R)
        qr_lo = alloc(st1, "qr_lo", [P, T], R)
        kr_hi = alloc(st1, "kr_hi", [P, T], R)
        kr_lo = alloc(st1, "kr_lo", [P, T], R)
        v_hi = alloc(st1, "v_hi", [P, NT, P], R)
        v_lo = alloc(st1, "v_lo", [P, NT, P], R)
        kc_hi = alloc(st1, "kc_hi", [P, C], R)
        kc_lo = alloc(st1, "kc_lo", [P, C], R)
        vc_hi = alloc(st1, "vc_hi", [P, CT, P], R)
        vc_lo = alloc(st1, "vc_lo", [P, CT, P], R)
        pt_hi = alloc(st1, "pt_hi", [P, 7 * P], R)
        pt_lo = alloc(st1, "pt_lo", [P, 7 * P], R)
        band_u = [res[:, 3, 0:14 * GRID_W].rearrange("p (j c) -> p j c", c=GRID_W),
                  alloc(st1, "band_u1", [P, 14, GRID_W])]
        rope_sb = alloc(st1, "rope_sb", [P, 2, T])
        mask_sb = alloc(st1, "mask_sb", [P, 10, GRID_W])
        st1.close()
        tA, tB, tC, tD = (res[:, j, :] for j in (4, 5, 6, 7))
        kraw, ksq, krs, vraw = (stage[:, 0, C * j:C * (j + 1)] for j in range(4))
        band_m = [tC[:, 0:576], tA[:, 0:576]]
        o1 = tD.rearrange("p (t d) -> p t d", d=P)

        cv_x, cv_y = rope_sb[:, 0, :], rope_sb[:, 1, :]

        st4 = ExitStack()
        acc = alloc(st4, "acc", [P, T])
        q_hi = alloc(st4, "q_hi", [P, T], R)
        q_lo = alloc(st4, "q_lo", [P, T], R)
        k_hi = alloc(st4, "k_hi", [P, T], R)
        k_lo = alloc(st4, "k_lo", [P, T], R)
        va_hi = alloc(st4, "va_hi", [P, NT, P], R)
        va_lo = alloc(st4, "va_lo", [P, NT, P], R)
        strip = alloc(st4, "strip", [P, T])
        pb = alloc(st4, "pb", [P, 2, T])
        p8_hi = alloc(st4, "p8_hi", [P, T], R)
        p8_lo = alloc(st4, "p8_lo", [P, T], R)
        o2 = alloc(st4, "o2", [P, NT, P])
        cumq = alloc(st4, "cumq", [P, NT, 8])
        cq2 = alloc(st4, "cq2", [P, NT, 2])
        nlam = alloc(st4, "nlam", [P, 1])
        ms8 = alloc(st4, "ms8", [P, NT])
        osq = alloc(st4, "osq", [P, P])
        gate_sb = alloc(st4, "gate_sb", [P, 2, BANK])
        st = ExitStack()
        wfl = alloc(st, "wfl", [P, KT, 8])
        wfl_hi = alloc(st, "wfl_hi", [P, KT, 8], R)
        wfl_lo = alloc(st, "wfl_lo", [P, KT, 8], R)
        zf = alloc(st, "zf", [P, NT, 8])
        ef = alloc(st, "ef", [P, NT, 8])
        logf = alloc(st, "logf", [P, NT, 8])
        negc = alloc(st, "negc", [8, T])
        lamv = alloc(st, "lamv", [P, 4, HD])
        lamp = alloc(st, "lamp", [P, HD])
        lam2 = alloc(st, "lam2", [P, 2])
        st.close()
        bt = alloc(st4, "bt", [P, 2, T])
        nck = [alloc(st4, f"nck{a}", [P, T]) for a in range(2)]
        st4.close()

        st = ExitStack()
        y_hi = alloc(st, "y_hi", [P, KT, T], R)
        y_lo = alloc(st, "y_lo", [P, KT, T], R)
        gate_g = [alloc(st, "gate_g", [P, 2, T]), stage]
        st.close()

        st = ExitStack()
        acc2 = alloc(st, "acc2", [P, T])
        accm = alloc(st, "accm", [P, C])
        memF = alloc(st, "memF", [P, KT, C])
        m_hi = alloc(st, "m_hi", [P, KT, C], R)
        m_lo = alloc(st, "m_lo", [P, KT, C], R)
        mq_hi = alloc(st, "mq_hi", [P, 2, T], R)
        mq_lo = alloc(st, "mq_lo", [P, 2, T], R)
        mk_hi = alloc(st, "mk_hi", [P, 2, C], R)
        mk_lo = alloc(st, "mk_lo", [P, 2, C], R)
        mv_hi = alloc(st, "mv_hi", [P, 2, C], R)
        mv_lo = alloc(st, "mv_lo", [P, 2, C], R)
        mp = alloc(st, "mp", [P, 2, C])
        mpt_hi = alloc(st, "mpt_hi", [P, 2, C], R)
        mpt_lo = alloc(st, "mpt_lo", [P, 2, C], R)
        mo = alloc(st, "mo", [P, NT, C])
        st.close()

        st = ExitStack()
        acc3 = alloc(st, "acc3", [P, T])
        stx = ExitStack()
        sq3 = alloc(stx, "sq3", [P, 2, T])
        stx.close()
        a_hi = alloc(st, "a_hi", [P, KT, T], R)
        a_lo = alloc(st, "a_lo", [P, KT, T], R)
        st.close()

        negc_dram = nc.dram_tensor("negc_dram", [8, T], F).ap()
        band_dram = nc.dram_tensor("band_dram", [8, P, 14, GRID_W], F).ap()
        conv_dram = nc.dram_tensor("conv_dram", [P, 4, T], F).ap()
        strip_dram = nc.dram_tensor("strip_dram", [4, P, T], F).ap()
        gate_dram = nc.dram_tensor("gate_dram", [P, 16, T], F).ap()
        spill = [nc.dram_tensor(f"spill{j}", [P, KT, T], F).ap() for j in range(2)]

        NB = {"x0": (res, T, act_hi, act_lo, acc0b), "ctx": (ctxF, C, hc_hi, hc_lo, accc),
              "x1": (res, T, act_hi, act_lo, acc), "mem": (memF, C, m_hi, m_lo, accm),
              "x2": (res, T, act_hi, act_lo, acc2), "x3": (res, T, act_hi, act_lo, acc3),
              "final": (res, T, None, None, acc3)}
        STAT_BANK = {"x0": 6, "ctx": 5, "x1": 6, "mem": 4, "x2": 6, "x3": 6, "final": 0}
        SQUARES = {"x1": pb, "x2": mo.rearrange("p t c -> p (t c)").rearrange("p (s t) -> p s t", s=2),
                   "x3": sq3}
        Q_TAKEN = {2: 0, 5: 1, 6: 2, 7: 3}
        GAIN = {"x1": V_MIXG, "mem": V_MEMKV, "x2": V_MEMQ, "x3": V_MLPG, "final": V_FIN}

        def gain(name, k):
            if name in ("x0", "ctx"):
                j = 0 if name == "x0" else 1
                return gs[:, k, j:j + 1]
            return vec[:, GAIN[name] + k:GAIN[name] + k + 1]

        def shift(name, k):
            if name in ("x0", "ctx"):
                j = 0 if name == "x0" else 1
                return mod[:, k, j:j + 1]
            return None

        def bank(b, c0=0, c1=BANK):
            return ps[:, b * BANK + c0:b * BANK + c1]

        na_o = ps[:, 6 * BANK - HD:6 * BANK]

        def bcast(src, n):
            return bass.AP(src.tensor, src.offset, [[0, P], [1, n]])

        def window(qt):
            if qt < 2:
                return 0, 512, 6 - 2 * qt
            if qt >= 6:
                return 512, 512, 14 - 2 * qt
            return (qt - 2) * P, 576, None

        HALF_TAKEN = {2: [0], 5: [1], 7: [2], 10: [3], 13: [4], 15: [5]}

        block = ctx.enter_context(nc.Block())

        @block.sync
        def _(sp):
            sp.dma_start(vec[:, :], small).then_inc(S["small_in"], 16)
            sp.dma_start(con[:, :], consts).then_inc(S["small_in"], 16)
            sp.dma_start(cond[:, :, :], cond_t).then_inc(S["small_in"], 16)
            for n in range(6):
                if n >= 2:
                    sp.wait_ge(S["ada_used"], n - 1)
                sp.dma_start(ada[:, n % 2, :, :], w_ada[n].rearrange("p (k c) -> p k c", k=KT)
                             ).then_inc(S[f"ada_in{n % 2}"], 16)
            for s in range(2):
                sp.dma_start(raw[:, s, :, :],
                             w_stream[s].rearrange("p (k c) -> p k c", k=KT)
                             ).then_inc(S[f"raw_in{s}"], 16)
            for h in range(8):
                for qa in range(2):
                    src = bass.AP(rpb_pad.tensor, h * 15 * 127 + (1 - qa) * 127 + 63,
                                  [[127, 14], [-1, GRID_W], [1, GRID_W]])
                    sp.dma_start(band_dram[h, 64 * qa:64 * qa + 64].rearrange("q j c -> j q c"), src
                                  ).then_inc(S["toeplitz"], 16)
            src = bass.AP(rel_rows.tensor, P - 1, [[T + P - 1, 4], [-1, P], [1, T]])
            sp.dma_start(strip_dram, src).then_inc(S["toeplitz"], 16)
            with sp.Fori(1, N_TILES // 2) as h:
                for s in range(2):
                    sp.wait_ge(S["w_split"], 2 * h + s - 1)
                    sp.dma_start(raw[:, s, :, :],
                                 w_stream[bass.ds(2 * h + s, 1)].rearrange("o p (k c) -> (o p) k c", k=KT)
                                 ).then_inc(S[f"raw_in{s}"], 16)
            for k in range(KT):
                sp.wait_ge(S["y_ready"], k + 1)
                sp.dma_start(y_t[:, k, :], res[:, k, :]).then_inc(S["y_out"], 16)
            sp.wait_ge(S["y_out"], 16 * KT)

        @block.gpsimd
        def _(pool):
            def split(h, s, free=True, in_turn=False):
                if in_turn:
                    pool.wait_ge(S["w_split"], 2 * h + s)
                pool.wait_ge(S[f"raw_in{s}"], 16 * h + 16)
                if free:
                    pool.wait_ge(S["tile_done"], 2 * h + s - 1)
                pool.sem_inc(S["issued"], 1)
                nc.gpsimd.tensor_copy(w_hi[:, s, :, :], raw[:, s, :, :]).then_inc(S["w_hi"], 1)
                pool.wait_ge(S["w_hi"], 2 * h + s + 1)
                nc.gpsimd.tensor_tensor(w_lo[:, s, :, :], raw[:, s, :, :], w_hi[:, s, :, :].bitcast(F),
                                        ALU.subtract).then_inc(S["w_split"], 1)

            def split_range(first, n):
                with pool.Fori(first // 2, (first + n) // 2) as h:
                    split(h, 0)
                    split(h, 1)

            split(0, 0, free=False)
            split(0, 1, free=False)
            pool.wait_ge(S["mask_in"], 16)
            with pool.Fori(0, 4) as i:
                h0 = 4 * i + (T_ATT // 2)
                split(h0 + 1, 0)
                split(h0 + 1, 1)
                split(h0 + 2, 0)
                pool.wait_ge(S["rope_in"], 16 * i + 16)
                pool.wait_ge(S["qk_plain_lo"], 2 * i + 1)
                nc.gpsimd.tensor_tensor(tA, tA, rope_sb[:, 0, :], ALU.mult).then_inc(S["qk_cos"], 1)
                pool.wait_ge(S["qk_plain_lo"], 2 * i + 2)
                nc.gpsimd.tensor_tensor(tC, tC, rope_sb[:, 0, :], ALU.mult).then_inc(S["qk_cos"], 1)
                split(h0 + 2, 1)
                pool.wait_ge(S["qk_lo"], 2 * i + 2)
                for a in range(2):
                    pool.wait_ge(S[f"tile_in{a}"], 16 * i + 16)
                    pool.sem_inc(S["issued"], 1)
                    nc.gpsimd.tensor_tensor(band_m[a].rearrange("p (r c) -> p r c", c=GRID_W),
                                            band_u[a][:, 2:11, :], mask_sb[:, 0:9, :],
                                            ALU.add).then_inc(S["band_step"], 1)
                    pool.wait_ge(S["band_step"], 4 * i + 2 * a + 1)
                    nc.gpsimd.tensor_tensor(band_u[a][:, :, :], band_u[a][:, :, :],
                                            mask_sb[:, 9:10, :].to_broadcast([P, 14, GRID_W]),
                                            ALU.add).then_inc(S["band_step"], 1)
                for n in range(3, 5):
                    split(h0 + n, 0)
                    split(h0 + n, 1)
            split_range(T_OUT + 2, 8)
            with pool.Fori(0, 4) as i:
                h0 = 5 * i + (T_MIX // 2)
                pool.wait_ge(S["fl_cumq"], 1)
                pool.wait_ge(S["fx_done"], i + 1)
                pool.sem_inc(S["issued"], 1)
                nc.gpsimd.tensor_copy(cq2[:, :, :], cumq[:, :, bass.ds(2 * i, 2)]).then_inc(S["fx_cq"], 1)
                for n in range(1, 4):
                    split(h0 + n, 0)
                    split(h0 + n, 1)

                def causal(u):
                    n = P * (u % NT + 1)
                    dg = bt[:, u % 2, n - P:n]
                    pool.wait_ge(S["fx_bias"], 16 * i + (u + 1))
                    pool.sem_inc(S["issued"], 1)
                    nc.gpsimd.affine_select(out=dg, in_=dg, compare_op=ALU.is_ge, fill=NEG, base=0,
                                            pattern=[[-1, P]], channel_multiplier=1
                                            ).then_inc(S["fx_bias_m"], 1)

                causal(0)
                causal(1)
                split(h0 + 4, 0)
                split(h0 + 4, 1)
                for u in range(2, 2 * NT):
                    causal(u)
                split(h0 + 5, 0)
                split(h0 + 5, 1)
            split_range(T_MERGE + 2, 8)
            split_range(T_WO + 2, 8)
            with pool.Fori(0, 4) as i:
                h0 = 3 * i + (T_MEM // 2)
                split(h0 + 1, 0)
                split(h0 + 2, 0, in_turn=True)
                split(h0 + 3, 0, in_turn=True)
                split(h0 + 3, 1)
            split_range(T_WOM + 2, 8)
            split_range(T_MLP + 2, 62)

        @block.scalar
        def _(act):
            def note():
                act.sem_inc(S["issued"], 1)

            def norm_squares(name, buf=stage):
                src, w = NB[name][0:2]
                r = NORM[name]
                for k in range(KT):
                    if 8 * r + k >= 2:
                        act.wait_ge(S["acc_done"], 8 * r + k - 1)
                    nc.scalar.activation(buf[:, k % 2, 0:w], src[:, k, :], ACT.Square
                                         ).then_inc(S["sq_ready"], 1)

            def norm_rms(name):
                r, w, b = NORM[name], NB[name][1], STAT_BANK[name]
                act.wait_ge(S["ss_ready"], r + 1)
                nc.scalar.activation(rt[:, 8 * (r % 2):8 * (r % 2) + w // P], bank(b, 0, w // P), ACT.Sqrt,
                                     bias=eps[:, 0:1], scale=1.0 / D).then_inc(S["rms_ready"], 1)

            def norm_hi(name, meanwhile=None):
                r, f = SCALED[name], FILL[name]
                w, hi = NB[name][1:3]
                for k in range(KT):
                    if k == 6 and meanwhile is not None:
                        meanwhile()
                    act.wait_ge(S["scaled"], 8 * r + k + 1)
                    if shift(name, k) is None:
                        nc.scalar.activation(hi[:, k, :], stage[:, k % 2, 0:w], ACT.Copy
                                             ).then_inc(S["hi_ready"], 1)
                    else:
                        nc.scalar.activation(hi[:, k, :], stage[:, k % 2, 0:w], ACT.Identity,
                                             bias=shift(name, k)).then_inc(S["hi_ready"], 1)

            def split_hi(hi, loaded=None, last=None):
                for k in range(KT):
                    if loaded is not None and k == 4:
                        act.wait_ge(loaded, 32)
                    src = last if last is not None and k == KT - 1 else res[:, k, :]
                    nc.scalar.activation(hi[:, k, :], src, ACT.Copy).then_inc(S["hi_ready"], 1)

            act.wait_ge(S["small_in"], 48)
            nc.scalar.activation(csig[:, :, :], cond[:, :, :], ACT.Sigmoid).then_inc(S["c_sig"], 1)
            act.dma_start(res[:, :, :], x_t).then_inc(S["x_in"], 16)
            act.dma_start(ctxF[:, :, :], ctx_t).then_inc(S["rows_in"], 16)
            act.wait_ge(S["x_in"], 16)
            act.wait_ge(S["const_ready"], 1)
            norm_squares("x0")
            act.wait_ge(S["rows_in"], 16)
            norm_squares("ctx")
            nc.scalar.activation(perm[:, :], con[:, C_PERM:C_PERM + P], ACT.Copy)
            act.wait_ge(S["ada_used"], 4)
            nc.scalar.activation(mrow[:, 0:2 * D], ps[0:2, 0:4 * BANK], ACT.Copy).then_inc(S["ada_rows"], 1)
            norm_rms("x0")
            norm_rms("ctx")

            def gate_rows():
                act.wait_ge(S["ada_used"], 6)
                nc.scalar.activation(mrow[:, 2 * D:3 * D], ps[0:2, 0:2 * BANK], ACT.Copy).then_inc(S["ada_rows"], 1)

            norm_hi("x0", gate_rows)
            norm_hi("ctx")
            act.wait_ge(S["lo_ready"], 8 * FILL["ctx"] + 8)
            act.wait_ge(S["ada_step"], 3)
            act.dma_start(mask_sb[:, :, :], masks).then_inc(S["mask_in"], 16)

            with act.Fori(0, 4) as i:
                t0 = 8 * i + T_ATT
                act.wait_ge(S["conv_out"], 16 * i + 16)
                act.dma_start(rope_sb[:, :, :], rope).then_inc(S["rope_in"], 16)
                for n, (full, sq, b0) in enumerate(((tA, tB, 0), (tC, tD, 2))):
                    act.wait_ge(S["tile_done"], t0 + n + 1)
                    nc.scalar.activation(full, ps[:, b0 * BANK:(b0 + 2) * BANK], ACT.Copy
                                         )
                    nc.scalar.activation(sq, ps[:, b0 * BANK:(b0 + 2) * BANK], ACT.Square
                                         ).then_inc(S["qk_sq"], 1)
                nc.scalar.activation(kraw, bank(6, 0, C), ACT.Copy)
                nc.scalar.activation(ksq, bank(6, 0, C), ACT.Square).then_inc(S["ck_sq"], 1)
                act.wait_ge(S["qk_ss"], 2 * i + 1)
                nc.scalar.activation(hr[:, 0, :], bank(0, 0, 2 * NT), ACT.Sqrt, bias=eps[:, 0:1],
                                     scale=1.0 / HD).then_inc(S["qk_rms"], 1)
                act.wait_ge(S["ck_ss"], i + 1)
                nc.scalar.activation(krs, bank(6, C, 2 * C), ACT.Sqrt, bias=eps[:, 0:1],
                                     scale=1.0 / HD).then_inc(S["ck_rms"], 1)
                act.wait_ge(S["ck_done"], i + 1)
                nc.scalar.activation(kc_hi[:, :], kraw, ACT.Copy).then_inc(S["c_hi"], 1)
                act.wait_ge(S["tile_done"], t0 + 3)
                nc.scalar.activation(vraw, bank(7, 0, C), ACT.Copy).then_inc(S["vc_raw"], 1)
                nc.scalar.activation(stage[:, 1, :], ps[:, 4 * BANK:6 * BANK], ACT.Copy).then_inc(S["v_raw"], 1)
                act.wait_ge(S["qk_normed"], 2 * i + 1)
                nc.scalar.activation(qp_hi[:, :], tA, ACT.Copy).then_inc(S["qk_plain_hi"], 1)
                act.wait_ge(S["vc_turned"], i + 1)
                nc.scalar.activation(vc_hi[:, :, :], bank(7, C, 2 * C).rearrange("p (t d) -> p t d", d=P),
                                     ACT.Copy).then_inc(S["c_hi"], 1)
                act.wait_ge(S["qk_ss"], 2 * i + 2)
                nc.scalar.activation(hr[:, 1, :], bank(2, 0, 2 * NT), ACT.Sqrt, bias=eps[:, 0:1],
                                     scale=1.0 / HD).then_inc(S["qk_rms"], 1)
                act.wait_ge(S["v_turned"], i + 1)
                nc.scalar.activation(v_hi[:, :, :], ps[:, 4 * BANK:6 * BANK].rearrange("p (t d) -> p t d", d=P),
                                     ACT.Copy).then_inc(S["v_hi"], 1)
                act.wait_ge(S["toeplitz"], 16 * 17)
                act.wait_ge(S["pair_done"], i + 1)
                for a in range(2):
                    act.dma_start(band_u[a][:, :, :], band_dram[bass.ds(2 * i + a, 1)].rearrange(
                        "o p j c -> (o p) j c")).then_inc(S[f"tile_in{a}"], 16)
                act.wait_ge(S["qk_normed"], 2 * i + 2)
                nc.scalar.activation(kr_hi[:, :], tC, ACT.Copy).then_inc(S["qk_plain_hi"], 1)
                act.wait_ge(S["qk_roped"], 2 * i + 1)
                nc.scalar.activation(qr_hi[:, :], tA, ACT.Copy).then_inc(S["qk_hi"], 1)
                act.wait_ge(S["tile_done"], t0 + 4)
                nc.scalar.activation(tB, ps[:, 6 * BANK:8 * BANK], ACT.Sigmoid).then_inc(S["za_sig"], 1)
                act.wait_ge(S["qk_roped"], 2 * i + 2)
                nc.scalar.activation(kr_hi[:, :], tC, ACT.Copy).then_inc(S["qk_hi"], 1)
                act.wait_ge(S["tile_done"], t0 + 5)
                nc.scalar.activation(cv_x, ps[:, 4 * BANK:6 * BANK], ACT.Copy).then_inc(S["cv_u"], 1)

                def exp_unit(u):
                    a, qt = divmod(u, NT)
                    w = window(qt)[1] + C
                    act.wait_ge(S["na_logits"], 16 * i + (u + 1))
                    nc.scalar.activation(stage[:, u % 2, 0:w], stage[:, u % 2, 0:w], ACT.Exp,
                                         bias=nm[:, u % 2:u % 2 + 1], scale=-1.0,
                                         accum_out=rsum[:, u % 2:u % 2 + 1]).then_inc(S["na_probs"], 1)

                exp_unit(0)
                for u in range(16):
                    if u < 15:
                        exp_unit(u + 1)
                    w = 6 * P if window(u % NT)[1] == 512 else 7 * P
                    act.wait_ge(S["na_pt"], 16 * i + (u + 1))
                    if u > 0:
                        act.wait_ge(S["na_pv"], 16 * i + u)
                    nc.scalar.activation(pt_hi[:, 0:w], ps[:, 4 * BANK:4 * BANK + w], ACT.Copy
                                         ).then_inc(S["na_pt_hi"], 1)
                    for h in HALF_TAKEN.get(u, []):
                        if h >= 4:
                            act.wait_ge(S["half_done"], 6 * i + (h + 1))
                            act.wait_ge(S["cv_step"], 9 * i + 5)
                            half = slice((h % 2) * BANK, (h % 2 + 1) * BANK)
                            nc.scalar.activation(cv_x[:, half], bank(6 + h % 2), ACT.Sigmoid
                                                 ).then_inc(S["cv_sig"], 1)
                act.wait_ge(S["conv_done"], i + 2)
                act.dma_start(conv_dram[:, bass.ds(i, 1), :].rearrange("p o t -> p (o t)"), cv_y
                              ).then_inc(S["conv_out"], 16)
            act.wait_ge(S["pair_done"], 5)
            act.dma_start(res[:, 4:7, :], conv_dram[:, 0:3, :]).then_inc(S["rows_in"], 16)
            act.wait_ge(S["tile_done"], T_OUT)
            split_hi(act_hi, S["rows_in"], cv_y)

            def residual_loads(name, src, norm, meanwhile=None):
                L, r = LINEAR[name], NORM[norm]

                def addend(s, m):
                    act.wait_ge(S["lin_evac"], m + (10 * L + s + 1))
                    act.dma_start(stage[:, s, :], src[:, bass.ds(m + s, 1), :].rearrange("p o t -> p (o t)")
                                  ).then_inc(S[f"xres_in{s}"], 16)

                def square(s, i):
                    act.wait_ge(S["lin_evac"], 2 * i + (10 * L + s + 3))
                    act.wait_ge(S["acc_done"], 2 * i + (8 * r + s - 1))
                    act.sem_inc(S["issued"], 1)
                    nc.scalar.activation(SQUARES[norm][:, s, :],
                                         res[:, bass.ds(2 * i + s, 1), :].rearrange("p o t -> p (o t)"),
                                         ACT.Square).then_inc(S["sq_ready"], 1)

                addend(0, 0)
                addend(1, 0)
                if meanwhile is not None:
                    meanwhile()
                with act.Fori(0, 3) as i:
                    for s in range(2):
                        square(s, i)
                        addend(s, 2 * i + 2)
                square(0, 3)
                square(1, 3)
                if norm == "x2":
                    norm_rms("mem")
                norm_rms(norm)

            residual_loads("out", x_t, "x1")
            act.wait_ge(S["lin_evac"], 10)
            act.dma_start(wfl[:, :, :], w_fl).then_inc(S["fl_in"], 16)
            act.dma_start(lamv[:, :, :], bcast(lam4, 4 * HD).rearrange("p (a d) -> p a d", a=4)
                          ).then_inc(S["fl_in"], 16)
            act.dma_start(spill[0], res[:, :, :]).then_inc(S["spilled"], 16)
            act.wait_ge(S["fl_in"], 32)
            nc.scalar.activation(wfl_hi[:, :, :], wfl[:, :, :], ACT.Copy).then_inc(S["fl_exp"], 1)
            norm_hi("x1")
            act.wait_ge(S["fl_proj"], 1)
            nc.scalar.activation(negc[:, :], ps[0:8, 0:2 * BANK], ACT.Copy).then_inc(S["fl_exp"], 1)
            act.wait_ge(S["fl_z"], 3)
            nc.scalar.activation(ef[:, :, :], ef[:, :, :], ACT.Exp, scale=-1.0).then_inc(S["fl_exp"], 1)
            act.wait_ge(S["fl_exp"], 3)
            nc.scalar.activation(ef[:, :, :], ef[:, :, :], ACT.Ln, bias=one[:, 0:1]).then_inc(S["fl_ln"], 1)
            act.wait_ge(S["lam_step"], 2)
            nc.scalar.activation(lam2[:, :], lam2[:, :], ACT.Exp).then_inc(S["lam_exp"], 1)
            act.wait_ge(S["fl_negc"], 1)
            act.dma_start(negc_dram, negc[:, :]).then_inc(S["fl_out"], 16)
            act.wait_ge(S["fl_out"], 16)
            act.wait_ge(S["lam_step"], 4)
            with act.Fori(0, 4) as i:
                t0 = 10 * i + T_MIX
                act.wait_ge(S["df_done"], i + 1)
                act.dma_start(strip[:, :], strip_dram[bass.ds(i, 1)].rearrange("o p c -> (o p) c")
                              ).then_inc(S["strip_in"], 16)
                act.wait_ge(S["fx_done"], i + 1)
                for a in range(2):
                    row = negc_dram[bass.ds(2 * i + a, 1), :]
                    act.dma_start(nck[a][:, :], row.to_broadcast([P, T])).then_inc(S["fx_ck_in"], 16)

                def operands(base):
                    act.wait_ge(S["tile_done"], t0 + base + 1)
                    nc.scalar.activation(stage[:, 1, :], ps[:, 4 * BANK:6 * BANK], ACT.Copy).then_inc(S["v_raw"], 1)
                    act.wait_ge(S["tile_done"], t0 + base + 2)
                    nc.scalar.activation(q_hi[:, :], ps[:, 0:2 * BANK], ACT.Copy, scale=0.125).then_inc(S["op_hi"], 1)
                    act.wait_ge(S["v_turned"], 2 * i + (5 + base // 5))
                    nc.scalar.activation(va_hi[:, :, :], ps[:, 4 * BANK:6 * BANK].rearrange("p (t d) -> p t d", d=P),
                                         ACT.Copy).then_inc(S["op_hi"], 1)
                    act.wait_ge(S["tile_done"], t0 + base + 3)
                    nc.scalar.activation(k_hi[:, :], ps[:, 2 * BANK:4 * BANK], ACT.Copy).then_inc(S["op_hi"], 1)

                def gate_half(h):
                    out = S[f"gate_out{h % 2}"]
                    act.wait_ge(S["half_done"], 8 * i + (H_GATE + h + 1))
                    act.wait_ge(out, 64 * i + 16 * (h // 2 + 1))
                    nc.scalar.activation(gate_sb[:, h % 2, :], bank(7), ACT.Copy).then_inc(S["gate_copied"], 1)
                    act.wait_ge(S["gate_copied"], 8 * i + (h + 2))
                    dst = gate_dram[:, bass.ds(4 * i + h // 2, 1), (h % 2) * BANK:(h % 2 + 1) * BANK]
                    act.dma_start(dst.rearrange("p o t -> p (o t)"), gate_sb[:, h % 2, :]).then_inc(out, 16)

                operands(0)

                def exps(u):
                    n = P * (u + 1)
                    for m, buf in enumerate((stage, pb)):
                        c = 2 * (u % 2) + m
                        act.wait_ge(S["df_logits"], 16 * i + (2 * u + m + 1))
                        nc.scalar.activation(buf[:, u % 2, 0:n], buf[:, u % 2, 0:n], ACT.Exp,
                                             bias=nm[:, c:c + 1], scale=-1.0,
                                             accum_out=rsum[:, c:c + 1]).then_inc(S["df_probs"], 1)

                exps(0)
                for u in range(NT):
                    n = P * (u + 1)
                    if u + 1 < NT:
                        exps(u + 1)
                    act.wait_ge(S["df_pt"], 8 * i + (u + 1))
                    if u > 0:
                        act.wait_ge(S["df_pv"], 8 * i + u)
                    nc.scalar.activation(p8_hi[:, 0:n], ps[:, 4 * BANK:4 * BANK + n], ACT.Copy
                                         ).then_inc(S["df_pt_hi"], 1)
                    if u % 2 == 1:
                        gate_half(u // 2)
                    act.wait_ge(S["df_pv"], 8 * i + (u + 1))
                    r1 = rinv[:, 2 * (u % 2):2 * (u % 2) + 1]
                    nc.scalar.activation(o2[:, u, :], bank(6, 0, P), ACT.Copy, scale=r1).then_inc(S["df_out"], 1)
                    if u > 0:
                        act.wait_ge(S["df_out"], 16 * i + 2 * u)
                    nc.scalar.activation(osq[:, :], bank(6, 0, P), ACT.Square, scale=r1,
                                         accum_out=ms8[:, u:u + 1]).then_inc(S["df_out"], 1)
                act.wait_ge(S["df_out"], 16 * i + 16)
                nc.scalar.activation(ms8[:, :], ms8[:, :], ACT.Sqrt, bias=eps[:, 0:1], scale=1.0 / P
                                     ).then_inc(S["df_ms"], 1)
                def fox_bias(u):
                    a, qt = divmod(u, NT)
                    n = P * (qt + 1)
                    if u >= 2:
                        act.wait_ge(S["fx_logits"], 16 * i + (u - 1))
                    nc.scalar.activation(bt[:, u % 2, 0:n], nck[a][:, 0:n], ACT.Identity, bias=cq2[:, qt, a:a + 1]
                                         ).then_inc(S["fx_bias"], 1)

                act.wait_ge(S["fx_ck_in"], 32 * i + 32)
                act.wait_ge(S["fx_cq"], i + 1)
                fox_bias(0)
                fox_bias(1)
                operands(5)

                def exp_fox(u):
                    n = P * (u % NT + 1)
                    act.wait_ge(S["fx_logits"], 16 * i + (u + 1))
                    nc.scalar.activation(stage[:, u % 2, 0:n], stage[:, u % 2, 0:n], ACT.Exp,
                                         bias=nm[:, u % 2:u % 2 + 1], scale=-1.0,
                                         accum_out=rsum[:, u % 2:u % 2 + 1]).then_inc(S["fx_probs"], 1)

                exp_fox(0)
                for u in range(2 * NT):
                    n = P * (u % NT + 1)
                    if u < 2 * NT - 1:
                        exp_fox(u + 1)
                    act.wait_ge(S["fx_pt"], 16 * i + (u + 1))
                    if u > 0:
                        act.wait_ge(S["fx_pv"], 16 * i + u)
                    nc.scalar.activation(p8_hi[:, 0:n], ps[:, 4 * BANK:4 * BANK + n], ACT.Copy
                                         ).then_inc(S["fx_pt_hi"], 1)
                    if u < 2 * NT - 2:
                        fox_bias(u + 2)
                    if u % 4 == 2:
                        gate_half(4 + u // 4)
            act.wait_ge(S["fx_done"], 5)
            act.wait_ge(S["df_done"], 5)
            for p in range(2):
                act.wait_ge(S[f"gate_out{p}"], 16 * 17)
            split_hi(y_hi)
            def load_gates(s, first, m=0):
                if not first:
                    act.wait_ge(S["lo_ready"], m + (8 * FILL["merged"] + s - 1))
                act.dma_start(gate_g[s][:, :, :], gate_dram[:, bass.ds(2 * m + 2 * s, 2), :]
                              if not first else gate_dram[:, 2 * s:2 * s + 2, :]).then_inc(S[f"tile_in{s}"], 16)

            def sigmoids(s, m):
                act.wait_ge(S[f"tile_in{s}"], 8 * m + 80)
                nc.scalar.activation(gate_g[s][:, :, :], gate_g[s][:, :, :], ACT.Sigmoid).then_inc(S["mg_sig"], 1)

            def merged_hi(s, m):
                act.wait_ge(S["mg_step"], 3 * m + (3 * s + 9))
                act.sem_inc(S["issued"], 1)
                nc.scalar.activation(act_hi[:, bass.ds(m + s, 1), :].rearrange("p o t -> p (o t)"),
                                     gate_g[s][:, 0, :], ACT.Copy).then_inc(S["hi_ready"], 1)

            load_gates(0, True)
            load_gates(1, True)
            sigmoids(0, 0)
            with act.Fori(0, 3) as i:
                sigmoids(1, 2 * i)
                merged_hi(0, 2 * i)
                load_gates(0, False, 2 * i + 2)
                merged_hi(1, 2 * i)
                load_gates(1, False, 2 * i + 2)
                sigmoids(0, 2 * i + 2)
            sigmoids(1, 6)
            merged_hi(0, 6)
            merged_hi(1, 6)
            act.wait_ge(S["spilled"], 16)
            act.wait_ge(S["tile_done"], T_WO)
            act.wait_ge(S["lo_ready"], 8 * FILL["merged"] + 8)
            act.dma_start(memF[:, :, :], mem_t).then_inc(S["rows_in"], 16)

            def memory_squares():
                act.wait_ge(S["rows_in"], 48)
                norm_squares("mem", mp)

            residual_loads("wo", spill[0], "x2", memory_squares)
            act.dma_start(spill[1], res[:, :, :]).then_inc(S["spilled"], 16)
            norm_hi("x2")
            act.wait_ge(S["lo_ready"], 8 * FILL["x2"] + 8)
            norm_hi("mem")
            act.wait_ge(S["spilled"], 32)
            def q_half(h, src, n):
                c, x = h // 2, slice((h % 2) * BANK, (h % 2 + 1) * BANK)
                nc.scalar.activation(mq_hi[:, c, x], src, ACT.Copy, scale=0.0625).then_inc(S["mq_split_hi"], 1)

            for h in range(4):
                act.wait_ge(S["tile_done"], T_MEM + h // 2 + 1)
                q_half(h, bank(h), h)

            def weight_hi(i, n):
                act.wait_ge(S["raw_in1"], 48 * i + (8 * (T_MEM + n - 1) + 16))
                act.wait_ge(S["tile_done"], 6 * i + (T_MEM + n - 1))
                act.wait_ge(S["w_hi"], 6 * i + (T_MEM + n))
                nc.scalar.activation(w_hi[:, 1, :, :], raw[:, 1, :, :], ACT.Copy).then_inc(S["w_hi"], 1)

            weight_hi(0, 3)

            def memory_head(i, ahead):
                t0 = 6 * i + T_MEM
                for c in range(2):
                    act.wait_ge(S["tile_done"], t0 + c + 3)
                    nc.scalar.activation(mk_hi[:, c, :], bank(4 + c, 0, C), ACT.Copy).then_inc(S["mm_hi"], 1)
                weight_hi(i, 5)
                act.wait_ge(S["tile_done"], t0 + 6)
                nc.scalar.activation(mo[:, 0:2, :], bank(6).rearrange("p (t d) -> p t d", d=C), ACT.Copy
                                     ).then_inc(S["v_raw"], 1)
                act.wait_ge(S["v_turned"], i + 13)
                nc.scalar.activation(mv_hi[:, :, :], bank(7).rearrange("p (t d) -> p t d", d=C), ACT.Copy
                                     ).then_inc(S["mm_hi"], 1)

                def exp_mem(u):
                    act.wait_ge(S["mm_max"], 8 * i + (u + 1))
                    if u >= 2:
                        act.wait_ge(S["mm_pt"], 8 * i + (u - 1))
                    nc.scalar.activation(mp[:, u % 2, :], bank(u % 2, 0, C), ACT.Exp, bias=nm[:, u % 2:u % 2 + 1],
                                         accum_out=rsum[:, u % 2:u % 2 + 1]).then_inc(S["mm_probs"], 1)

                exp_mem(0)
                for u in range(NT):
                    if u + 1 < NT:
                        exp_mem(u + 1)
                    act.wait_ge(S["mm_pt"], 8 * i + (u + 1))
                    if u >= 2:
                        act.wait_ge(S["mm_pv"], 8 * i + (u - 1))
                    nc.scalar.activation(mpt_hi[:, u % 2, :], bank(2 + u % 2, 0, C), ACT.Copy
                                         ).then_inc(S["mm_pt_hi"], 1)
                    if ahead and u in Q_TAKEN:
                        h = Q_TAKEN[u]
                        act.wait_ge(S["half_done"], 4 * i + (H_MQ + h + 1))
                        act.wait_ge(S["mm_scores"], 8 * i + (4 if h % 2 == 0 else 8))
                        q_half(h, bank(6 + h % 2), h)
                if ahead:
                    weight_hi(i, 9)
                act.wait_ge(S["mm_ot"], i + 1)
                note()
                nc.scalar.activation(res[:, bass.ds(2 * i, 2), :],
                                     ps[:, 0:4 * BANK].rearrange("p (c t) -> p c t", c=2), ACT.Copy
                                     ).then_inc(S["mm_done"], 1)

            with act.Fori(0, 3) as i:
                memory_head(i, True)
            memory_head(3, False)
            act.wait_ge(S["mm_done"], 4)
            split_hi(act_hi)
            residual_loads("wom", spill[1], "x3")
            norm_hi("x3")
            def hidden(b):
                with act.Fori(0, 4) as i:
                    for s in range(2):
                        n1 = 8 * b + 2 * i + s
                        act.wait_ge(S["tile_done"], 16 * b + 2 * i + (T_MLP + s + 1))
                        act.wait_ge(S["a_lo"], n1 + 1)
                        nc.scalar.activation(stage[:, s, :], ps[:, 2 * s * BANK:(2 * s + 2) * BANK], ACT.Relu
                                             ).then_inc(S["a_relu"], 1)
                        act.wait_ge(S["a_sq"], n1 + 1)
                        note()
                        nc.scalar.activation(a_hi[:, bass.ds(2 * i + s, 1), :].rearrange("p o t -> p (o t)"),
                                             stage[:, s, :], ACT.Copy).then_inc(S["a_hi"], 1)

            with act.Fori(0, 4) as b:
                hidden(b)
            r = NORM["final"]
            act.wait_ge(S["a_lo"], 34)
            with act.Fori(0, 4) as i:
                for s in range(2):
                    act.wait_ge(S["mlp_acc"], 2 * i + (27 + s))
                    act.wait_ge(S["acc_done"], 2 * i + (8 * r + s - 1))
                    note()
                    nc.scalar.activation(stage[:, s, :], res[:, bass.ds(2 * i + s, 1), :].rearrange("p o t -> p (o t)"),
                                         ACT.Square).then_inc(S["sq_ready"], 1)
            norm_rms("final")

        @block.vector
        def _(dve):
            def note():
                dve.sem_inc(S["issued"], 1)

            def accumulate(name, k, square):
                ac, w, r = NB[name][4], NB[name][1], NORM[name]
                dve.wait_ge(S["sq_ready"], 8 * r + k + 1)
                if k == 0:
                    nc.vector.tensor_copy(ac[:, 0:w], square[:, 0:w]).then_inc(S["acc_done"], 1)
                else:
                    dve.wait_ge(S["acc_done"], 8 * r + k)
                    nc.vector.tensor_tensor(ac[:, 0:w], ac[:, 0:w], square[:, 0:w], ALU.add
                                            ).then_inc(S["acc_done"], 1)

            def norm_sum(name, buf=stage):
                for k in range(KT):
                    accumulate(name, k, buf[:, k % 2, :])

            def norm_rstd(name):
                w, r = NB[name][1], NORM[name]
                dve.wait_ge(S["rms_ready"], r + 1)
                t = rt[:, 8 * (r % 2):8 * (r % 2) + w // P]
                nc.vector.reciprocal(t, t).then_inc(S["rstd_ready"], 1)

            def linear_starts(norm):
                nc.vector.memset(NB[norm][4][:, :], 0.0)
                dve.drain().then_inc(S["lin_evac"], 2)

            def norm_scale(name):
                src, w, hi, lo, _ = NB[name]
                rstd = ps[:, STAT_BANK[name] * BANK:STAT_BANK[name] * BANK + w]
                r, f = NORM[name], FILL[name]

                def low(k):
                    dve.wait_ge(S["hi_ready"], 8 * f + k + 1)
                    sh = shift(name, k)
                    if sh is None:
                        nc.vector.tensor_tensor(lo[:, k, :], stage[:, k % 2, 0:w], hi[:, k, :].bitcast(F),
                                                ALU.subtract).then_inc(S["lo_ready"], 1)
                    else:
                        nc.vector.scalar_tensor_tensor(out=lo[:, k, :], in0=stage[:, k % 2, 0:w], scalar=sh,
                                                       in1=hi[:, k, :].bitcast(F), op0=ALU.add,
                                                       op1=ALU.subtract).then_inc(S["lo_ready"], 1)

                dve.wait_ge(S["rstd_spread"], r + 1)
                if f:
                    dve.wait_ge(S["lo_ready"], 8 * f)
                for k in range(KT):
                    if k >= 2:
                        dve.wait_ge(S["lo_ready"], 8 * f + k - 1)
                    nc.vector.scalar_tensor_tensor(out=stage[:, k % 2, 0:w], in0=src[:, k, :], scalar=gain(name, k),
                                                   in1=rstd, op0=ALU.mult, op1=ALU.mult
                                                   ).then_inc(S["scaled"], 1)
                    if k >= 1:
                        low(k - 1)
                low(KT - 1)

            def split_lo(name, hi, lo, last=None):
                f = FILL[name]
                for k in range(KT):
                    dve.wait_ge(S["hi_ready"], 8 * f + k + 1)
                    src = last if last is not None and k == KT - 1 else res[:, k, :]
                    nc.vector.tensor_tensor(lo[:, k, :], src, hi[:, k, :].bitcast(F), ALU.subtract
                                            ).then_inc(S["lo_ready"], 1)

            nc.vector.memset(eps[:, :], EPS).then_inc(S["const_ready"], 1)
            nc.vector.memset(one[:, :], 1.0)
            dve.wait_ge(S["small_in"], 48)
            nc.vector.tensor_scalar(out=qg8[:, :], in0=vec[:, V_QG:V_QG + 1], scalar1=0.125, scalar2=None,
                                    op0=ALU.mult).then_inc(S["const_ready"], 1)
            nc.vector.tensor_scalar(out=subg[:, :], in0=vec[:, V_SUB:V_SUB + 1], scalar1=1.0 - LAMBDA_INIT,
                                    scalar2=None, op0=ALU.mult).then_inc(S["const_ready"], 1)
            dve.wait_ge(S["c_sig"], 1)
            nc.vector.tensor_tensor(cond[:, :, :], cond[:, :, :], csig[:, :, :], ALU.mult).then_inc(S["c_silu"], 1)
            norm_sum("x0")
            norm_sum("ctx")

            def modulation(m0, m1, b):
                nc.vector.tensor_tensor(mod[:, m0:m1, :], bank(b, 2 * m0, 2 * m1).rearrange("p (m j) -> p m j", j=2),
                                        vec[:, V_BADA + m0:V_BADA + m1].rearrange("p (m o) -> p m o", o=1)
                                        .to_broadcast([P, m1 - m0, 2]), ALU.add).then_inc(S["ada_step"], 1)

            dve.wait_ge(S["ada_turned"], 1)
            modulation(0, 16, 4)
            dve.wait_ge(S["ada_step"], 1)
            nc.vector.scalar_tensor_tensor(out=gs[:, :, :], in0=mod[:, 8:16, :], scalar=1.0,
                                           in1=vec[:, V_NORM:V_NORM + 8].rearrange("p (m o) -> p m o", o=1)
                                           .to_broadcast([P, 8, 2]), op0=ALU.add, op1=ALU.mult
                                           ).then_inc(S["ada_step"], 1)
            dve.wait_ge(S["ada_step"], 2)
            norm_rstd("x0")
            norm_rstd("ctx")
            dve.drain().then_inc(S["pair_done"], 1)
            dve.drain().then_inc(S["conv_done"], 1)
            dve.drain().then_inc(S["conv_out"], 16)
            norm_scale("x0")
            norm_scale("ctx")
            dve.wait_ge(S["ada_turned"], 2)
            modulation(16, 24, 2)
            with dve.Fori(0, 4) as i:
                def normed(n, full, sq, g):
                    b0 = 2 * n
                    dve.wait_ge(S["qk_rms"], 2 * i + (n + 1))
                    nc.vector.reciprocal(hr[:, n, :], hr[:, n, :]).then_inc(S["qk_rstd"], 1)
                    dve.wait_ge(S["qk_rstd"], 4 * i + (2 * n + 1))
                    nc.vector.tensor_copy(sq.rearrange("p (t d) -> p t d", d=HD),
                                          hr[:, n, :].rearrange("p (t o) -> p t o", o=1)
                                          .to_broadcast([P, 2 * NT, HD])).then_inc(S["qk_rstd"], 1)
                    dve.wait_ge(S["qk_spread"], 2 * i + (n + 1))
                    nc.vector.scalar_tensor_tensor(out=full, in0=full, scalar=g,
                                                   in1=ps[:, b0 * BANK:(b0 + 2) * BANK], op0=ALU.mult,
                                                   op1=ALU.mult).then_inc(S["qk_normed"], 1)

                def plain_lo(n, full, hi, lo):
                    dve.wait_ge(S["qk_plain_hi"], 2 * i + (n + 1))
                    nc.vector.tensor_tensor(lo[:, :], full, hi[:, :].bitcast(F), ALU.subtract
                                            ).then_inc(S["qk_plain_lo"], 1)

                def roped(n, full, b0):
                    dve.wait_ge(S["qk_perm"], 2 * i + (n + 1))
                    if n == 0:
                        dve.wait_ge(S["rope_in"], 16 * i + 16)
                        dve.wait_ge(S["c_lo"], 2 * i + 2)
                    nc.vector.tensor_tensor(stage[:, n, :], ps[:, b0 * BANK:(b0 + 2) * BANK], rope_sb[:, 1, :],
                                            ALU.mult).then_inc(S["qk_sin"], 1)
                    dve.wait_ge(S["qk_sin"], 2 * i + (n + 1))
                    dve.wait_ge(S["qk_cos"], 2 * i + (n + 1))
                    nc.vector.tensor_tensor(full, full, stage[:, n, :], ALU.add).then_inc(S["qk_roped"], 1)

                def rot_lo(n, full, hi, lo):
                    dve.wait_ge(S["qk_hi"], 2 * i + (n + 1))
                    nc.vector.tensor_tensor(lo[:, :], full, hi[:, :].bitcast(F), ALU.subtract
                                            ).then_inc(S["qk_lo"], 1)

                dve.wait_ge(S["ck_rms"], i + 1)
                nc.vector.reciprocal(krs, krs).then_inc(S["ck_rstd"], 1)
                dve.wait_ge(S["ck_rstd"], i + 1)
                nc.vector.scalar_tensor_tensor(out=kraw, in0=kraw, scalar=vec[:, V_KG:V_KG + 1], in1=krs,
                                               op0=ALU.mult, op1=ALU.mult).then_inc(S["ck_done"], 1)
                dve.wait_ge(S["c_hi"], 2 * i + 1)
                nc.vector.tensor_tensor(kc_lo[:, :], kraw, kc_hi[:, :].bitcast(F), ALU.subtract
                                        ).then_inc(S["c_lo"], 1)
                normed(0, tA, tB, qg8[:, 0:1])
                plain_lo(0, tA, qp_hi, qp_lo)
                dve.wait_ge(S["c_hi"], 2 * i + 2)
                nc.vector.tensor_tensor(vc_lo[:, :, :], bank(7, C, 2 * C).rearrange("p (t d) -> p t d", d=P),
                                        vc_hi[:, :, :].bitcast(F), ALU.subtract).then_inc(S["c_lo"], 1)
                normed(1, tC, tD, vec[:, V_KG:V_KG + 1])
                dve.wait_ge(S["v_hi"], i + 1)
                nc.vector.tensor_tensor(v_lo[:, :, :], ps[:, 4 * BANK:6 * BANK].rearrange("p (t d) -> p t d", d=P),
                                        v_hi[:, :, :].bitcast(F), ALU.subtract).then_inc(S["v_lo"], 1)
                plain_lo(1, tC, kr_hi, kr_lo)
                roped(0, tA, 0)
                rot_lo(0, tA, qr_hi, qr_lo)
                roped(1, tC, 2)
                rot_lo(1, tC, kr_hi, kr_lo)
                dve.wait_ge(S["za_sig"], i + 1)
                nc.vector.tensor_tensor(tB, ps[:, 6 * BANK:8 * BANK], tB, ALU.mult).then_inc(S["za_done"], 1)

                def logits(u):
                    a, qt = divmod(u, NT)
                    key0, nl, row0 = window(qt)
                    b0 = 2 * (u % 2) * BANK
                    g = 16 * i + u
                    dve.wait_ge(S["na_scores"], g + 1)
                    if u >= 2:
                        dve.wait_ge(S["na_pt"], g - 1)
                    elif u == 0:
                        dve.wait_ge(S["qk_roped"], 2 * i + 2)
                    if qt == 0:
                        dve.wait_ge(S["band_step"], 4 * i + 2 * a + 2)
                    nc.vector.tensor_scalar(out=stage[:, u % 2, nl:nl + C], in0=ps[:, b0 + nl:b0 + nl + C],
                                            scalar1=-1.0, scalar2=None, op0=ALU.mult, op1=ALU.min,
                                            accum_out=cm[:, u % 2:u % 2 + 1]).then_inc(S["na_cmax"], 1)
                    dve.wait_ge(S["na_cmax"], g + 1)
                    note()
                    if row0 is None:
                        band = band_m[a]
                    else:
                        band = band_u[a][:, row0:row0 + 8, :].rearrange("p r c -> p (r c)")
                    nc.vector.tensor_tensor_reduce(out=stage[:, u % 2, 0:nl], in0=ps[:, b0:b0 + nl], in1=band,
                                                   scale=-1.0, scalar=cm[:, u % 2:u % 2 + 1], op0=ALU.add,
                                                   op1=ALU.min, accum_out=nm[:, u % 2:u % 2 + 1]
                                                   ).then_inc(S["na_logits"], 1)

                def conv_half(h):
                    half = slice((h % 2) * BANK, (h % 2 + 1) * BANK)
                    src, x_, y_ = bank(6 + h % 2), cv_x[:, half], cv_y[:, half]
                    dve.wait_ge(S["half_done"], 6 * i + (h + 1))
                    if h < 2:
                        dve.wait_ge(S["cv_u"], i + 1)
                        nc.vector.tensor_tensor(x_, src, x_, ALU.mult).then_inc(S["cv_step"], 1)
                    elif h < 4:
                        dve.wait_ge(S["cv_step"], 9 * i + 5)
                        nc.vector.tensor_tensor(y_, src, y_, ALU.mult).then_inc(S["cv_step"], 1)
                    else:
                        dve.wait_ge(S["cv_sig"], 2 * i + (h - 3))
                        nc.vector.tensor_tensor(x_, src, x_, ALU.mult).then_inc(S["cv_step"], 1)

                def conv_tap(n):
                    tap = vec[:, bass.ds(V_CW + 4 * n + i, 1)]
                    if n == 1:
                        dve.wait_ge(S["cv_step"], 9 * i + 2)
                        nc.vector.tensor_scalar(out=cv_y, in0=cv_x, scalar1=tap,
                                                scalar2=vec[:, bass.ds(V_CB + i, 1)], op0=ALU.mult, op1=ALU.add
                                                ).then_inc(S["cv_step"], 1)
                        return
                    dve.wait_ge(S["cv_step"], 9 * i + (3 if n == 0 else 4))
                    x_, y_ = (cv_x[:, 0:T - 1], cv_y[:, 1:T]) if n == 0 else (cv_x[:, 1:T], cv_y[:, 0:T - 1])
                    nc.vector.scalar_tensor_tensor(out=y_, in0=x_, scalar=tap, in1=y_, op0=ALU.mult, op1=ALU.add
                                                   ).then_inc(S["cv_step"], 1)

                TAPS = {5: [1], 6: [0, 2]}

                logits(0)
                logits(1)
                for u in range(16):
                    a, qt = divmod(u, NT)
                    g = 16 * i + u
                    w = 6 * P if window(qt)[1] == 512 else 7 * P
                    dve.wait_ge(S["na_pt_hi"], g + 1)
                    nc.vector.tensor_tensor(pt_lo[:, 0:w], ps[:, 4 * BANK:4 * BANK + w], pt_hi[:, 0:w].bitcast(F),
                                            ALU.subtract).then_inc(S["na_pt_lo"], 1)
                    nc.vector.reciprocal(rinv[:, u % 2:u % 2 + 1], rsum[:, u % 2:u % 2 + 1]
                                         ).then_inc(S["na_inv"], 1)
                    if u + 2 < 16:
                        logits(u + 2)
                    for h in HALF_TAKEN.get(u, []):
                        conv_half(h)
                    for n in TAPS.get(u, []):
                        conv_tap(n)
                    dve.wait_ge(S["na_inv"], g + 1)
                    dve.wait_ge(S["na_pv"], g + 1)
                    nc.vector.tensor_scalar(out=o1[:, qt, a * HD:(a + 1) * HD], in0=na_o,
                                            scalar1=rinv[:, u % 2:u % 2 + 1], scalar2=None, op0=ALU.mult
                                            ).then_inc(S["na_out"], 1)
                dve.wait_ge(S["cv_step"], 9 * i + 9)
                nc.vector.tensor_tensor(cv_y, cv_x, cv_y, ALU.mult).then_inc(S["conv_done"], 1)
                dve.wait_ge(S["na_ot"], i + 1)
                nc.vector.tensor_tensor(res[:, bass.ds(i, 1), :].rearrange("p o t -> p (o t)"),
                                        ps[:, 0:2 * BANK], tB, ALU.mult).then_inc(S["pair_done"], 1)
            linear_starts("x1")
            split_lo("mix", act_hi, act_lo, cv_y)

            def residual(name, T0, gated, norm):
                L, r = LINEAR[name], NORM[norm]

                def add_square(s, i):
                    dve.wait_ge(S["sq_ready"], 2 * i + (8 * r + s + 1))
                    dve.wait_ge(S["acc_done"], 2 * i + (8 * r + s))
                    ac = NB[norm][4]
                    nc.vector.tensor_tensor(ac[:, :], ac[:, :], SQUARES[norm][:, s, :], ALU.add
                                            ).then_inc(S["acc_done"], 1)

                with dve.Fori(0, 4) as i:
                    for s in range(2):
                        dve.wait_ge(S["tile_done"], 2 * i + (T0 + s + 1))
                        dve.wait_ge(S[f"xres_in{s}"], 16 * i + (64 * L + 16))
                        out = res[:, bass.ds(2 * i + s, 1), :].rearrange("p o t -> p (o t)")
                        src = ps[:, 2 * s * BANK:(2 * s + 2) * BANK]
                        if gated:
                            gate = mod[:, bass.ds(16 + 2 * i + s, 1), 0:1].rearrange("p a b -> p (a b)")
                            nc.vector.scalar_tensor_tensor(out=out, in0=src, scalar=gate, in1=stage[:, s, :],
                                                           op0=ALU.mult, op1=ALU.add).then_inc(S["lin_evac"], 1)
                        else:
                            nc.vector.tensor_tensor(out, src, stage[:, s, :], ALU.add).then_inc(S["lin_evac"], 1)
                        add_square(s, i)

            residual("out", T_OUT, True, "x1")
            norm_rstd("x1")
            dve.wait_ge(S["fl_exp"], 1)
            nc.vector.tensor_tensor(wfl_lo[:, :, :], wfl[:, :, :], wfl_hi[:, :, :].bitcast(F), ALU.subtract
                                    ).then_inc(S["fl_z"], 1)
            norm_scale("x1")
            dve.wait_ge(S["fl_proj"], 2)
            nc.vector.tensor_tensor(zf[:, :, :], bank(2, 0, 64).rearrange("p (t h) -> p t h", h=8),
                                    vec[:, V_BF:V_BF + 8].rearrange("p (o h) -> p o h", o=1)
                                    .to_broadcast([P, NT, 8]), ALU.add).then_inc(S["fl_z"], 1)
            dve.wait_ge(S["fl_z"], 2)
            nc.vector.scalar_tensor_tensor(out=ef[:, :, :], in0=zf[:, :, :], scalar=-1.0, in1=zf[:, :, :],
                                           op0=ALU.mult, op1=ALU.max).then_inc(S["fl_z"], 1)
            dve.wait_ge(S["fl_ln"], 1)
            nc.vector.scalar_tensor_tensor(out=logf[:, :, :], in0=zf[:, :, :], scalar=0.0, in1=ef[:, :, :],
                                           op0=ALU.min, op1=ALU.subtract).then_inc(S["fl_logf"], 1)
            dve.wait_ge(S["fl_in"], 32)
            for j in range(2):
                if j:
                    dve.wait_ge(S["lam_step"], 1)
                nc.vector.tensor_tensor_reduce(out=lamp[:, :], in0=lamv[:, 2 * j, :], in1=lamv[:, 2 * j + 1, :],
                                               scale=1.0, scalar=0.0, op0=ALU.mult, op1=ALU.add,
                                               accum_out=lam2[:, j:j + 1]).then_inc(S["lam_step"], 1)
            dve.wait_ge(S["lam_exp"], 1)
            nc.vector.tensor_scalar(out=nlam[:, :], in0=lam2[:, 1:2], scalar1=-LAMBDA_INIT, scalar2=None,
                                    op0=ALU.add).then_inc(S["lam_step"], 1)
            dve.wait_ge(S["lam_step"], 3)
            nc.vector.tensor_tensor(nlam[:, :], nlam[:, :], lam2[:, 0:1], ALU.subtract).then_inc(S["lam_step"], 1)
            dve.wait_ge(S["fl_cum"], 1)
            nc.vector.tensor_copy(cumq[:, :, :], bank(1, 0, 64).rearrange("p (t h) -> p t h", h=8)
                                  ).then_inc(S["fl_cumq"], 1)
            dve.wait_ge(S["fl_cum"], 2)
            nc.vector.tensor_scalar(out=negc[:, :], in0=ps[0:8, 2 * BANK:4 * BANK], scalar1=-1.0, scalar2=None,
                                    op0=ALU.mult).then_inc(S["fl_negc"], 1)
            dve.wait_ge(S["lam_step"], 4)
            dve.wait_ge(S["fl_out"], 16)
            dve.wait_ge(S["spilled"], 16)
            dve.drain().then_inc(S["df_done"], 1)
            dve.drain().then_inc(S["fx_done"], 1)
            dve.drain().then_inc(S["gate_out0"], 16)
            dve.drain().then_inc(S["gate_out1"], 16)
            dve.drain().then_inc(S["gate_copied"], 1)
            with dve.Fori(0, 4) as i:
                def low_parts(done):
                    dve.wait_ge(S["op_hi"], 6 * i + (done + 1))
                    nc.vector.scalar_tensor_tensor(out=q_lo[:, :], in0=ps[:, 0:2 * BANK], scalar=0.125,
                                                   in1=q_hi[:, :].bitcast(F), op0=ALU.mult,
                                                   op1=ALU.subtract).then_inc(S["op_lo"], 1)
                    dve.wait_ge(S["op_hi"], 6 * i + (done + 2))
                    nc.vector.tensor_tensor(va_lo[:, :, :], ps[:, 4 * BANK:6 * BANK].rearrange(
                        "p (t d) -> p t d", d=P), va_hi[:, :, :].bitcast(F), ALU.subtract).then_inc(S["op_lo"], 1)
                    dve.wait_ge(S["op_hi"], 6 * i + (done + 3))
                    nc.vector.tensor_tensor(k_lo[:, :], ps[:, 2 * BANK:4 * BANK], k_hi[:, :].bitcast(F),
                                            ALU.subtract).then_inc(S["op_lo"], 1)

                low_parts(0)
                dve.wait_ge(S["strip_in"], 16 * i + 16)

                def logits(u):
                    n = P * (u + 1)
                    for m, buf in enumerate((stage, pb)):
                        c = 2 * (u % 2) + m
                        dve.wait_ge(S["df_scores"], 16 * i + (2 * u + m + 1))
                        if u >= 2:
                            dve.wait_ge(S["df_pt"], 8 * i + (u - 1))
                        note()
                        nc.vector.tensor_tensor_reduce(out=buf[:, u % 2, 0:n], in0=ps[:, 2 * m * BANK:2 * m * BANK + n],
                                                       in1=strip[:, T - n:T], scale=-1.0, scalar=BIG,
                                                       op0=ALU.add, op1=ALU.min, accum_out=nm[:, c:c + 1]
                                                       ).then_inc(S["df_logits"], 1)

                logits(0)
                for u in range(NT):
                    n = P * (u + 1)
                    g = 8 * i + u
                    c = 2 * (u % 2)
                    dve.wait_ge(S["df_probs"], 16 * i + (2 * u + 2))
                    if u >= 2:
                        dve.wait_ge(S["df_out"], 16 * i + (2 * u - 2))
                    nc.vector.reciprocal(rinv[:, c:c + 2], rsum[:, c:c + 2]).then_inc(S["df_inv"], 1)
                    dve.wait_ge(S["df_inv"], 16 * i + (2 * u + 1))
                    nc.vector.tensor_scalar(out=rinv[:, c + 1:c + 2], in0=rinv[:, c + 1:c + 2], scalar1=nlam[:, 0:1],
                                            scalar2=rsum[:, c:c + 1], op0=ALU.mult, op1=ALU.mult
                                            ).then_inc(S["df_inv"], 1)
                    dve.wait_ge(S["df_inv"], 16 * i + (2 * u + 2))
                    nc.vector.scalar_tensor_tensor(out=stage[:, u % 2, 0:n], in0=pb[:, u % 2, 0:n],
                                                   scalar=rinv[:, c + 1:c + 2], in1=stage[:, u % 2, 0:n],
                                                   op0=ALU.mult, op1=ALU.add).then_inc(S["df_comb"], 1)
                    if u + 1 < NT:
                        logits(u + 1)
                    dve.wait_ge(S["df_pt_hi"], g + 1)
                    nc.vector.tensor_tensor(p8_lo[:, 0:n], ps[:, 4 * BANK:4 * BANK + n], p8_hi[:, 0:n].bitcast(F),
                                            ALU.subtract).then_inc(S["df_pt_lo"], 1)
                dve.wait_ge(S["df_ms"], i + 1)
                nc.vector.reciprocal(ms8[:, :], ms8[:, :]).then_inc(S["df_rstd"], 1)
                dve.wait_ge(S["df_rstd"], i + 1)
                nc.vector.tensor_tensor(o2[:, :, :], o2[:, :, :],
                                        ms8[:, :].rearrange("p (t o) -> p t o", o=1).to_broadcast([P, NT, P]),
                                        ALU.mult).then_inc(S["df_normed"], 1)
                low_parts(3)
                dve.wait_ge(S["df_ot"], i + 1)
                nc.vector.tensor_scalar(out=res[:, bass.ds(i, 1), :].rearrange("p o t -> p (o t)"),
                                        in0=ps[:, 4 * BANK:6 * BANK], scalar1=subg[:, 0:1], scalar2=None,
                                        op0=ALU.mult).then_inc(S["df_done"], 1)

                def fox_logits(u):
                    n = P * (u % NT + 1)
                    g = 16 * i + u
                    b0 = 2 * (u % 2) * BANK
                    dve.wait_ge(S["fx_scores"], g + 1)
                    dve.wait_ge(S["fx_bias_m"], g + 1)
                    if u >= 2:
                        dve.wait_ge(S["fx_pt"], g - 1)
                    note()
                    nc.vector.tensor_tensor_reduce(out=stage[:, u % 2, 0:n], in0=ps[:, b0:b0 + n],
                                                   in1=bt[:, u % 2, 0:n], scale=-1.0, scalar=BIG, op0=ALU.add,
                                                   op1=ALU.min, accum_out=nm[:, u % 2:u % 2 + 1]
                                                   ).then_inc(S["fx_logits"], 1)

                fox_logits(0)
                fox_logits(1)
                for u in range(2 * NT):
                    a, qt = divmod(u, NT)
                    n = P * (qt + 1)
                    g = 16 * i + u
                    dve.wait_ge(S["fx_pt_hi"], g + 1)
                    nc.vector.tensor_tensor(p8_lo[:, 0:n], ps[:, 4 * BANK:4 * BANK + n], p8_hi[:, 0:n].bitcast(F),
                                            ALU.subtract).then_inc(S["fx_pt_lo"], 1)
                    nc.vector.reciprocal(rinv[:, u % 2:u % 2 + 1], rsum[:, u % 2:u % 2 + 1]
                                         ).then_inc(S["fx_inv"], 1)
                    if u + 2 < 2 * NT:
                        fox_logits(u + 2)
                    dve.wait_ge(S["fx_inv"], g + 1)
                    dve.wait_ge(S["fx_pv"], g + 1)
                    nc.vector.tensor_scalar(out=o2[:, qt, a * HD:(a + 1) * HD], in0=bank(6, 0, HD),
                                            scalar1=rinv[:, u % 2:u % 2 + 1], scalar2=None, op0=ALU.mult
                                            ).then_inc(S["fx_out"], 1)
                dve.wait_ge(S["fx_ot"], i + 1)
                nc.vector.tensor_copy(res[:, bass.ds(4 + i, 1), :].rearrange("p o t -> p (o t)"),
                                      ps[:, 0:2 * BANK]).then_inc(S["fx_done"], 1)
            dve.drain().then_inc(S["mg_step"], 6)
            split_lo("y", y_hi, y_lo)
            dve.drain().then_inc(S["lin_evac"], 2)
            with dve.Fori(0, 4) as i:
                for s in range(2):
                    g = gate_g[s]
                    dve.wait_ge(S["mg_sig"], 2 * i + (s + 1))
                    dve.wait_ge(S["tile_done"], 2 * i + (T_MERGE + s + 1))
                    for n in range(2):
                        src = ps[:, (4 * s + 2 * n) * BANK:(4 * s + 2 * n + 2) * BANK]
                        nc.vector.tensor_tensor(g[:, n, :], src, g[:, n, :], ALU.mult).then_inc(S["mg_step"], 1)
                    dve.wait_ge(S["mg_step"], 6 * i + (3 * s + 8))
                    nc.vector.tensor_tensor(g[:, 0, :], g[:, 0, :], g[:, 1, :], ALU.add).then_inc(S["mg_step"], 1)
                    dve.wait_ge(S["hi_ready"], 2 * i + (8 * FILL["merged"] + s + 1))
                    note()
                    nc.vector.tensor_tensor(act_lo[:, bass.ds(2 * i + s, 1), :].rearrange("p o t -> p (o t)"),
                                            g[:, 0, :],
                                            act_hi[:, bass.ds(2 * i + s, 1), :].rearrange("p o t -> p (o t)")
                                            .bitcast(F), ALU.subtract).then_inc(S["lo_ready"], 1)
            nc.vector.memset(acc2[:, :], 0.0)
            dve.drain()
            norm_sum("mem", mp)
            residual("wo", T_WO, False, "x2")
            norm_rstd("mem")
            norm_rstd("x2")
            dve.drain().then_inc(S["mm_out"], 1)
            norm_scale("x2")
            norm_scale("mem")
            def q_half_low(h, src, wait):
                c, x = h // 2, slice((h % 2) * BANK, (h % 2 + 1) * BANK)
                dve.wait_ge(S["mq_split_hi"], wait)
                nc.vector.scalar_tensor_tensor(out=mq_lo[:, c, x], in0=src, scalar=0.0625,
                                               in1=mq_hi[:, c, x].bitcast(F), op0=ALU.mult,
                                               op1=ALU.subtract).then_inc(S["mq_split_lo"], 1)

            for h in range(4):
                q_half_low(h, bank(h), h + 1)

            def weight_lo(i, n):
                dve.wait_ge(S["w_hi"], 6 * i + (T_MEM + n + 1))
                dve.wait_ge(S["w_split"], 6 * i + (T_MEM + n))
                nc.vector.tensor_tensor(w_lo[:, 1, :, :], raw[:, 1, :, :], w_hi[:, 1, :, :].bitcast(F),
                                        ALU.subtract).then_inc(S["w_split"], 1)

            weight_lo(0, 3)

            def memory_head(i, ahead):
                for c in range(2):
                    dve.wait_ge(S["mm_hi"], 3 * i + (c + 1))
                    nc.vector.tensor_tensor(mk_lo[:, c, :], bank(4 + c, 0, C), mk_hi[:, c, :].bitcast(F),
                                            ALU.subtract).then_inc(S["mm_lo"], 1)
                weight_lo(i, 5)
                dve.wait_ge(S["mm_hi"], 3 * i + 3)
                nc.vector.tensor_tensor(mv_lo[:, :, :], bank(7).rearrange("p (t d) -> p t d", d=C),
                                        mv_hi[:, :, :].bitcast(F), ALU.subtract).then_inc(S["mm_lo"], 1)

                def row_max(u):
                    dve.wait_ge(S["mm_scores"], 8 * i + (u + 1))
                    if u >= 2:
                        dve.wait_ge(S["mm_probs"], 8 * i + (u - 1))
                    nc.vector.tensor_reduce(out=nm[:, u % 2:u % 2 + 1], in_=bank(u % 2, 0, C), axis=AX.X,
                                            op=ALU.max, negate=True).then_inc(S["mm_max"], 1)

                row_max(0)
                row_max(1)
                for u in range(NT):
                    g = 8 * i + u
                    dve.wait_ge(S["mm_pt_hi"], g + 1)
                    nc.vector.tensor_tensor(mpt_lo[:, u % 2, :], bank(2 + u % 2, 0, C),
                                            mpt_hi[:, u % 2, :].bitcast(F), ALU.subtract
                                            ).then_inc(S["mm_pt_lo"], 1)
                    nc.vector.reciprocal(rinv[:, u % 2:u % 2 + 1], rsum[:, u % 2:u % 2 + 1]
                                         ).then_inc(S["mm_inv"], 1)
                    if u + 2 < NT:
                        row_max(u + 2)
                    dve.wait_ge(S["mm_inv"], g + 1)
                    dve.wait_ge(S["mm_pv"], g + 1)
                    nc.vector.tensor_scalar(out=mo[:, u, :], in0=bank(4 + u % 2, 0, C),
                                            scalar1=rinv[:, u % 2:u % 2 + 1], scalar2=None, op0=ALU.mult
                                            ).then_inc(S["mm_out"], 1)
                    if ahead and u in Q_TAKEN:
                        h = Q_TAKEN[u]
                        q_half_low(h, bank(6 + h % 2), 4 * i + (4 + h + 1))
                if ahead:
                    weight_lo(i, 9)

            with dve.Fori(0, 3) as i:
                memory_head(i, True)
            memory_head(3, False)
            linear_starts("x3")
            split_lo("memo", act_hi, act_lo)
            residual("wom", T_WOM, False, "x3")
            norm_rstd("x3")
            dve.drain().then_inc(S["a_lo"], 2)
            dve.drain().then_inc(S["mlp_acc"], 2)
            norm_scale("x3")
            def hidden(b):
                with dve.Fori(0, 4) as i:
                    for s in range(2):
                        n1 = 8 * b + 2 * i + s
                        dve.wait_ge(S["a_relu"], n1 + 1)
                        nc.vector.tensor_tensor(stage[:, s, :], stage[:, s, :], stage[:, s, :], ALU.mult
                                                ).then_inc(S["a_sq"], 1)
                        dve.wait_ge(S["a_hi"], n1 + 1)
                        nc.vector.tensor_tensor(a_lo[:, bass.ds(2 * i + s, 1), :].rearrange("p o t -> p (o t)"),
                                                stage[:, s, :],
                                                a_hi[:, bass.ds(2 * i + s, 1), :].rearrange("p o t -> p (o t)")
                                                .bitcast(F), ALU.subtract).then_inc(S["a_lo"], 1)

            def outputs(b, last=False):
                with dve.Fori(0, 4) as i:
                    for s in range(2):
                        dve.wait_ge(S["tile_done"], 16 * b + 2 * i + (T_MLP + 8 + s + 1))
                        out = res[:, bass.ds(2 * i + s, 1), :].rearrange("p o t -> p (o t)")
                        dve.wait_ge(S["mlp_acc"], 8 * b + 2)
                        nc.vector.tensor_tensor(out, ps[:, (4 + 2 * s) * BANK:(6 + 2 * s) * BANK], out, ALU.add
                                                ).then_inc(S["mlp_acc"], 1)
                        if last:
                            r = NORM["final"]
                            dve.wait_ge(S["sq_ready"], 2 * i + (8 * r + s + 1))
                            dve.wait_ge(S["acc_done"], 2 * i + (8 * r + s))
                            nc.vector.tensor_tensor(acc3[:, :], acc3[:, :], stage[:, s, :], ALU.add
                                                    ).then_inc(S["acc_done"], 1)

            with dve.Fori(0, 3) as b:
                hidden(b)
                outputs(b)
            hidden(3)
            nc.vector.memset(acc3[:, :], 0.0)
            dve.drain()
            outputs(3, last=True)
            norm_rstd("final")
            dve.wait_ge(S["rstd_spread"], NORM["final"] + 1)
            for k in range(KT):
                nc.vector.scalar_tensor_tensor(out=res[:, k, :], in0=res[:, k, :], scalar=gain("final", k),
                                               in1=ps[:, 0:2 * BANK], op0=ALU.mult, op1=ALU.mult
                                               ).then_inc(S["y_ready"], 1)

        @block.tensor
        def _(pe):
            def mm3(out, wh, wl, xh, xl, start, stop):
                nc.tensor.matmul(out, wh, xh, start=start, stop=False)
                nc.tensor.matmul(out, wh, xl, start=False, stop=False)
                return nc.tensor.matmul(out, wl, xh, start=False, stop=stop)

            def project(s, b0, xh, xl, width, ks=range(KT), ready=None):
                for c in range(0, width, BANK):
                    n = min(BANK, width - c)
                    for k in ks:
                        if ready is not None and c == 0:
                            ready(k)
                        last = mm3(ps[:, b0 * BANK + c:b0 * BANK + c + n], w_hi[:, s, k, :], w_lo[:, s, k, :],
                                   xh[:, k, c:c + n], xl[:, k, c:c + n], k == ks[0], k == ks[-1])
                return last

            def filled(name):
                return lambda k: pe.wait_ge(S["lo_ready"], 8 * FILL[name] + k + 1)

            def project_half(s, b0, c):
                x = slice(c * BANK, (c + 1) * BANK)
                for k in range(KT):
                    last = mm3(bank(b0 + c), w_hi[:, s, k, :], w_lo[:, s, k, :], act_hi[:, k, x], act_lo[:, k, x],
                               k == 0, k == KT - 1)
                return last

            def tile_ready(idx):
                pe.wait_ge(S["w_split"], idx + 1)

            def sum_squares(name):
                w, ac, r, b = NB[name][1], NB[name][4], NORM[name], STAT_BANK[name]
                pe.wait_ge(S["acc_done"], 8 * r + 8)
                for t in range(w // P):
                    last = nc.tensor.matmul(bank(b, t, t + 1), ac[:, t * P:(t + 1) * P], ones[:, 0:1],
                                            start=True, stop=True)
                last.then_inc(S["ss_ready"], 1)

            def spread(name):
                w, r, b = NB[name][1], NORM[name], STAT_BANK[name]
                pe.wait_ge(S["rstd_ready"], r + 1)
                for t in range(w // P):
                    j = 8 * (r % 2) + t
                    last = nc.tensor.matmul(ps[:, b * BANK + t * P:b * BANK + (t + 1) * P],
                                            rt[:, j:j + 1].to_broadcast([P, P]), ident, start=True, stop=True)
                last.then_inc(S["rstd_spread"], 1)

            pe.wait_ge(S["c_silu"], 1)

            def ada_chunk(n):
                pe.wait_ge(S[f"ada_in{n % 2}"], 16 * (n // 2) + 16)
                for k in range(KT):
                    last = nc.tensor.matmul(ps[0:2, (n % 4) * BANK:(n % 4 + 1) * BANK], cond[:, k, :],
                                            ada[:, n % 2, k, :], start=(k == 0), stop=(k == KT - 1))
                last.then_inc(S["ada_used"], 1)

            def turn_rows(m0, m1, b):
                for m in range(m0, m1):
                    last = nc.tensor.transpose(bank(b, 2 * m, 2 * m + 2), mrow[:, m * P:(m + 1) * P], ident[0:2, 0:2])
                last.then_inc(S["ada_turned"], 1)

            for n in range(4):
                ada_chunk(n)
            sum_squares("x0")
            pe.wait_ge(S["ada_rows"], 1)
            turn_rows(0, 16, 4)
            sum_squares("ctx")
            spread("x0")
            spread("ctx")
            ada_chunk(4)
            ada_chunk(5)
            pe.wait_ge(S["ada_rows"], 2)
            turn_rows(16, 24, 2)
            with pe.Fori(0, 4) as i:
                t0 = 8 * i + T_ATT
                tile_ready(t0)
                pe.wait_ge(S["pair_done"], i + 1)
                project(0, 0, act_hi, act_lo, T, ready=filled("x0")).then_inc(S["tile_done"], 1)
                tile_ready(t0 + 1)
                pe.wait_ge(S["ada_step"], 3)
                project(1, 2, act_hi, act_lo, T)
                pe.wait_ge(S["conv_done"], i + 1)
                project(1, 6, hc_hi, hc_lo, C, ready=filled("ctx")).then_inc(S["tile_done"], 1)

                def head_ss(n, sq, b0):
                    pe.wait_ge(S["qk_sq"], 2 * i + (n + 1))
                    for t in range(NT):
                        last = nc.tensor.matmul(bank(b0, 2 * t, 2 * t + 2), sq[:, t * P:(t + 1) * P],
                                                bd64[:, 0:P:HD], start=True, stop=True)
                    last.then_inc(S["qk_ss"], 1)

                def head_spread(n, sq, b0):
                    pe.wait_ge(S["qk_rstd"], 4 * i + (2 * n + 2))
                    for t in range(NT):
                        last = nc.tensor.transpose(ps[:, b0 * BANK + t * P:b0 * BANK + (t + 1) * P],
                                                   sq[:, t * P:(t + 1) * P], ident)
                    last.then_inc(S["qk_spread"], 1)

                def half_turn(n, hi, lo, b0):
                    pe.wait_ge(S["qk_plain_lo"], 2 * i + (n + 1))
                    for c in range(2):
                        nc.tensor.matmul(bank(b0 + c), perm[:, :], hi[:, c * BANK:(c + 1) * BANK],
                                         start=True, stop=False)
                        last = nc.tensor.matmul(bank(b0 + c), perm[:, :], lo[:, c * BANK:(c + 1) * BANK],
                                                start=False, stop=True)
                    last.then_inc(S["qk_perm"], 1)

                head_ss(0, tB, 0)
                tile_ready(t0 + 2)
                project_half(0, 4, 0)
                pe.wait_ge(S["ck_sq"], i + 1)
                nc.tensor.matmul(bank(6, C, 2 * C), bd64, ksq, start=True, stop=True).then_inc(S["ck_ss"], 1)
                project_half(0, 4, 1)
                project(0, 7, hc_hi, hc_lo, C).then_inc(S["tile_done"], 1)
                head_spread(0, tB, 0)
                head_ss(1, tD, 2)
                pe.wait_ge(S["vc_raw"], i + 1)
                for t in range(CT):
                    last = nc.tensor.transpose(bank(7, C + t * P, C + (t + 1) * P), vraw[:, t * P:(t + 1) * P], ident)
                last.then_inc(S["vc_turned"], 1)
                pe.wait_ge(S["v_raw"], i + 1)
                for t in range(NT):
                    last = nc.tensor.transpose(ps[:, 4 * BANK + t * P:4 * BANK + (t + 1) * P],
                                               stage[:, 1, t * P:(t + 1) * P], ident)
                last.then_inc(S["v_turned"], 1)
                tile_ready(t0 + 3)
                pe.wait_ge(S["ck_rms"], i + 1)
                project_half(1, 6, 0)
                head_spread(1, tD, 2)
                half_turn(0, qp_hi, qp_lo, 0)
                pe.wait_ge(S["c_lo"], 2 * i + 2)
                project_half(1, 6, 1).then_inc(S["tile_done"], 1)
                half_turn(1, kr_hi, kr_lo, 2)
                tile_ready(t0 + 4)
                pe.wait_ge(S["v_lo"], i + 1)
                project(0, 4, act_hi, act_lo, T).then_inc(S["tile_done"], 1)

                def conv_steps(first, n_steps):
                    for step in range(first, first + n_steps):
                        n, c, k = step // 16, step // 8 % 2, step % 8
                        w, h = (n + 1) % 2, step // 8
                        if step % 16 == 0:
                            tile_ready(t0 + 5 + n)
                        if k == 0:
                            if h == 0:
                                pe.wait_ge(S["za_done"], i + 1)
                            elif h >= 2:
                                pe.wait_ge(S["cv_step"], 9 * i + (1, 2, 6, 7)[h - 2])
                        x = slice(c * BANK, (c + 1) * BANK)
                        last = mm3(bank(6 + c), w_hi[:, w, k, :], w_lo[:, w, k, :], act_hi[:, k, x], act_lo[:, k, x],
                                   k == 0, k == KT - 1)
                        if k == KT - 1:
                            last.then_inc(S["half_done"], 1)
                            if c == 1:
                                pe.drain().then_inc(S["tile_done"], 1)

                def scores(u):
                    a, qt = divmod(u, NT)
                    key0, nl, _ = window(qt)
                    b0 = 2 * (u % 2) * BANK
                    h = slice(a * HD, (a + 1) * HD)
                    q = slice(qt * P, (qt + 1) * P)
                    if u == 0:
                        pe.wait_ge(S["qk_lo"], 2 * i + 2)
                        pe.wait_ge(S["c_lo"], 2 * i + 2)
                    if u >= 2:
                        pe.wait_ge(S["na_logits"], 16 * i + (u - 1))
                    for c in range(0, nl, BANK):
                        n = min(BANK, nl - c)
                        mm3(ps[:, b0 + c:b0 + c + n], qr_hi[h, q], qr_lo[h, q],
                            kr_hi[h, key0 + c:key0 + c + n], kr_lo[h, key0 + c:key0 + c + n], True, True)
                    mm3(ps[:, b0 + nl:b0 + nl + C], qp_hi[h, q], qp_lo[h, q], kc_hi[h, :], kc_lo[h, :],
                        True, True).then_inc(S["na_scores"], 1)

                scores(0)
                scores(1)
                conv_steps(0, 1)
                for u in range(16):
                    a, qt = divmod(u, NT)
                    key0, nl, _ = window(qt)
                    g = 16 * i + u
                    lat = [(c, min(P, nl - c)) for c in range(0, nl, P)]
                    blocks = lat + [(nl, P), (nl + P, P)]
                    pe.wait_ge(S["na_probs"], g + 1)
                    if u > 0:
                        pe.wait_ge(S["na_out"], g)
                    else:
                        pe.wait_ge(S["cv_u"], i + 1)
                    for j, (c, n) in enumerate(blocks):
                        last = nc.tensor.transpose(ps[:, 4 * BANK + j * P:4 * BANK + (j + 1) * P],
                                                   stage[:, u % 2, c:c + P], ident)
                    last.then_inc(S["na_pt"], 1)
                    if u + 2 < 16:
                        scores(u + 2)
                    conv_steps(3 * u + 1, 2)
                    pe.wait_ge(S["na_pt_lo"], g + 1)
                    hv = slice(a * HD, (a + 1) * HD)
                    for j, (c, n) in enumerate(blocks):
                        if j < len(lat):
                            vh, vl = v_hi[0:n, key0 // P + j, hv], v_lo[0:n, key0 // P + j, hv]
                        else:
                            vh, vl = vc_hi[:, j - len(lat), hv], vc_lo[:, j - len(lat), hv]
                        last = mm3(na_o, pt_hi[0:n, j * P:(j + 1) * P],
                                   pt_lo[0:n, j * P:(j + 1) * P], vh, vl, j == 0, j == len(blocks) - 1)
                    last.then_inc(S["na_pv"], 1)
                    if u < 15:
                        conv_steps(3 * u + 3, 1)
                pe.wait_ge(S["na_out"], 16 * i + 16)
                for t in range(NT):
                    last = nc.tensor.transpose(ps[:, t * P:(t + 1) * P], o1[:, t, :], ident)
                last.then_inc(S["na_ot"], 1)
            def linear(name, T0, operand):
                L = LINEAR[name]
                with pe.Fori(0, 4) as i:
                    for s in range(2):
                        tile_ready(2 * i + (T0 + s))
                        pe.wait_ge(S["lin_evac"], 2 * i + (10 * L + s + 1))
                        project(s, 2 * s, act_hi, act_lo, T, ready=filled(operand)).then_inc(S["tile_done"], 1)

            linear("out", T_OUT, "mix")
            sum_squares("x1")
            spread("x1")
            for c in range(2):
                x = slice(c * BANK, (c + 1) * BANK)
                for k in range(KT):
                    if c == 0:
                        filled("x1")(k)
                    last = mm3(ps[0:8, x], wfl_hi[:, k, :], wfl_lo[:, k, :], act_hi[:, k, x], act_lo[:, k, x],
                               k == 0, k == KT - 1)
            last.then_inc(S["fl_proj"], 1)
            pe.wait_ge(S["fl_exp"], 2)
            for t in range(NT):
                last = nc.tensor.transpose(bank(2, 8 * t, 8 * t + 8), negc[:, t * P:(t + 1) * P], ident[0:8, 0:8])
            last.then_inc(S["fl_proj"], 1)
            pe.wait_ge(S["fl_logf"], 1)
            rows = logf[:, :, :].rearrange("p t h -> p (t h)")
            nc.tensor.matmul(bank(1, 0, 64), tri, rows, start=True, stop=False)
            for d in range(1, NT):
                last = nc.tensor.matmul(bank(1, 8 * d, 64), ones, rows[:, 0:64 - 8 * d], start=False,
                                        stop=(d == NT - 1))
            last.then_inc(S["fl_cum"], 1)
            pe.wait_ge(S["fl_cumq"], 1)
            for t in range(NT):
                last = nc.tensor.transpose(ps[0:8, 2 * BANK + t * P:2 * BANK + (t + 1) * P], cumq[:, t, :], ident)
            last.then_inc(S["fl_cum"], 1)
            pe.wait_ge(S["fl_negc"], 1)
            with pe.Fori(0, 4) as i:
                t0 = 10 * i + T_MIX

                def operands(base):
                    tile_ready(t0 + base)
                    project(base % 2, 4, act_hi, act_lo, T).then_inc(S["tile_done"], 1)
                    tile_ready(t0 + base + 1)
                    project((base + 1) % 2, 0, act_hi, act_lo, T).then_inc(S["tile_done"], 1)
                    pe.wait_ge(S["v_raw"], 2 * i + (5 + base // 5))
                    for t in range(NT):
                        last = nc.tensor.transpose(ps[:, 4 * BANK + t * P:4 * BANK + (t + 1) * P],
                                                   stage[:, 1, t * P:(t + 1) * P], ident)
                    last.then_inc(S["v_turned"], 1)
                    tile_ready(t0 + base + 2)
                    project(base % 2, 2, act_hi, act_lo, T).then_inc(S["tile_done"], 1)

                def gate_steps(first, n_steps):
                    for step in range(first, first + n_steps):
                        n, h, k = step // 16, step // 8, step % 8
                        tile = (3, 4, 8, 9)[n]
                        if step % 16 == 0:
                            tile_ready(t0 + tile)
                        if k == 0:
                            pe.wait_ge(S["gate_copied"], 8 * i + (h + 1))
                        x = slice((h % 2) * BANK, (h % 2 + 1) * BANK)
                        last = mm3(bank(7), w_hi[:, tile % 2, k, :], w_lo[:, tile % 2, k, :], act_hi[:, k, x],
                                   act_lo[:, k, x], k == 0, k == KT - 1)
                        if k == KT - 1:
                            last.then_inc(S["half_done"], 1)
                            if h % 2 == 1:
                                pe.drain().then_inc(S["tile_done"], 1)

                pe.wait_ge(S["fx_done"], i + 1)
                operands(0)
                gate_steps(0, 2)

                def scores(u):
                    n = P * (u + 1)
                    q = slice(u * P, (u + 1) * P)
                    for m in range(2):
                        h = slice(m * HD, (m + 1) * HD)
                        if u == 0:
                            pe.wait_ge(S["op_lo"], 6 * i + 3)
                        else:
                            pe.wait_ge(S["df_logits"], 16 * i + (2 * u - 1 + m))
                        for c in range(0, n, BANK):
                            w = min(BANK, n - c)
                            last = mm3(ps[:, 2 * m * BANK + c:2 * m * BANK + c + w], q_hi[h, q], q_lo[h, q],
                                       k_hi[h, c:c + w], k_lo[h, c:c + w], True, True)
                        last.then_inc(S["df_scores"], 1)

                scores(0)
                for u in range(NT):
                    g = 8 * i + u
                    if u + 1 < NT:
                        scores(u + 1)
                    if u > 0:
                        gate_steps(4 * u, 2)
                    pe.wait_ge(S["df_comb"], g + 1)
                    if u > 0:
                        pe.wait_ge(S["df_pt_lo"], g)
                    for j in range(u + 1):
                        last = nc.tensor.transpose(ps[:, 4 * BANK + j * P:4 * BANK + (j + 1) * P],
                                                   stage[:, u % 2, j * P:(j + 1) * P], ident)
                    last.then_inc(S["df_pt"], 1)
                    gate_steps(4 * u + 2, 2)
                    pe.wait_ge(S["df_pt_lo"], g + 1)
                    if u >= 1:
                        pe.wait_ge(S["df_out"], 16 * i + 2 * u)
                    for j in range(u + 1):
                        last = mm3(bank(6, 0, P), p8_hi[:, j * P:(j + 1) * P], p8_lo[:, j * P:(j + 1) * P],
                                   va_hi[:, j, :], va_lo[:, j, :], j == 0, j == u)
                    last.then_inc(S["df_pv"], 1)
                operands(5)
                pe.wait_ge(S["df_normed"], i + 1)
                pe.wait_ge(S["op_lo"], 6 * i + 5)
                for t in range(NT):
                    last = nc.tensor.transpose(ps[:, 4 * BANK + t * P:4 * BANK + (t + 1) * P], o2[:, t, :], ident)
                last.then_inc(S["df_ot"], 1)
                gate_steps(32, 4)

                def fox_scores(u):
                    a, qt = divmod(u, NT)
                    n = P * (qt + 1)
                    b0 = 2 * (u % 2) * BANK
                    h = slice(a * HD, (a + 1) * HD)
                    q = slice(qt * P, (qt + 1) * P)
                    if u == 0:
                        pe.wait_ge(S["op_lo"], 6 * i + 6)
                    if u >= 2:
                        pe.wait_ge(S["fx_logits"], 16 * i + (u - 1))
                    for c in range(0, n, BANK):
                        w = min(BANK, n - c)
                        last = mm3(ps[:, b0 + c:b0 + c + w], q_hi[h, q], q_lo[h, q], k_hi[h, c:c + w],
                                   k_lo[h, c:c + w], True, True)
                    last.then_inc(S["fx_scores"], 1)

                fox_scores(0)
                fox_scores(1)
                for u in range(2 * NT):
                    a, qt = divmod(u, NT)
                    g = 16 * i + u
                    pe.wait_ge(S["fx_probs"], g + 1)
                    if u > 0:
                        pe.wait_ge(S["fx_pt_lo"], g)
                    else:
                        pe.wait_ge(S["df_done"], i + 2)
                    for j in range(qt + 1):
                        last = nc.tensor.transpose(ps[:, 4 * BANK + j * P:4 * BANK + (j + 1) * P],
                                                   stage[:, u % 2, j * P:(j + 1) * P], ident)
                    last.then_inc(S["fx_pt"], 1)
                    if u + 2 < 2 * NT:
                        fox_scores(u + 2)
                    if 0 < u < 15:
                        gate_steps(34 + 2 * u, 2)
                    pe.wait_ge(S["fx_pt_lo"], g + 1)
                    if u > 0:
                        pe.wait_ge(S["fx_out"], g)
                    hv = slice(a * HD, (a + 1) * HD)
                    for j in range(qt + 1):
                        last = mm3(bank(6, 0, HD), p8_hi[:, j * P:(j + 1) * P], p8_lo[:, j * P:(j + 1) * P],
                                   va_hi[:, j, hv], va_lo[:, j, hv], j == 0, j == qt)
                    last.then_inc(S["fx_pv"], 1)
                pe.wait_ge(S["fx_out"], 16 * i + 16)
                for t in range(NT):
                    last = nc.tensor.transpose(ps[:, t * P:(t + 1) * P], o2[:, t, :], ident)
                last.then_inc(S["fx_ot"], 1)
            with pe.Fori(0, 4) as i:
                for s in range(2):
                    tile_ready(2 * i + (T_MERGE + s))
                    pe.wait_ge(S["mg_step"], 6 * i + (3 * s + 2))
                    project(s, 4 * s, y_hi, y_lo, T, range(0, 4), filled("y"))
                    project(s, 4 * s + 2, y_hi, y_lo, T, range(4, 8), filled("y")).then_inc(S["tile_done"], 1)
            pe.wait_ge(S["lo_ready"], 8 * FILL["merged"] + 7)
            linear("wo", T_WO, "merged")
            sum_squares("mem")
            sum_squares("x2")
            spread("mem")
            spread("x2")
            for c in range(2):
                tile_ready(T_MEM + c)
                project(c, 2 * c, act_hi, act_lo, T, ready=filled("x2")).then_inc(S["tile_done"], 1)
            pe.wait_ge(S["lo_ready"], 8 * FILL["mem"] + 8)
            pe.wait_ge(S["mm_out"], 1)

            def memory_head(i, ahead):
                t0 = 6 * i + T_MEM
                for c in range(2):
                    tile_ready(t0 + 2 + c)
                    project(c, 4 + c, m_hi, m_lo, C).then_inc(S["tile_done"], 1)
                pe.wait_ge(S["mq_split_lo"], 4 * i + 4)
                for c in range(2):
                    tile_ready(t0 + 4 + c)
                    for k in range(KT):
                        last = mm3(bank(6, c * C, (c + 1) * C), w_hi[:, c, k, :], w_lo[:, c, k, :], m_hi[:, k, :],
                                   m_lo[:, k, :], k == 0, k == KT - 1)
                    last.then_inc(S["tile_done"], 1)
                pe.wait_ge(S["v_raw"], i + 13)
                for t in range(CT):
                    for c in range(2):
                        last = nc.tensor.transpose(bank(7, t * C + c * P, t * C + (c + 1) * P),
                                                   mo[:, c, t * P:(t + 1) * P], ident)
                last.then_inc(S["v_turned"], 1)

                def q_steps(first, n_steps):
                    for step in range(first, first + n_steps):
                        c, h, k = step // 16, step // 8, step % 8
                        if k == 0:
                            if h % 2 == 0:
                                tile_ready(t0 + 6 + c)
                            if h >= 2:
                                pe.wait_ge(S["mq_split_lo"], 4 * i + (4 + h - 1))
                        x = slice((h % 2) * BANK, (h % 2 + 1) * BANK)
                        last = mm3(bank(6 + h % 2), w_hi[:, c, k, :], w_lo[:, c, k, :], act_hi[:, k, x],
                                   act_lo[:, k, x], k == 0, k == KT - 1)
                        if k == KT - 1:
                            last.then_inc(S["half_done"], 1)
                            if h % 2 == 1:
                                pe.drain().then_inc(S["tile_done"], 1)

                def scores(u):
                    if u == 0:
                        pe.wait_ge(S["mm_lo"], 3 * i + 3)
                    if u >= 2:
                        pe.wait_ge(S["mm_probs"], 8 * i + (u - 1))
                    q = slice(u * P, (u + 1) * P)
                    for c in range(2):
                        last = mm3(bank(u % 2, 0, C), mq_hi[:, c, q], mq_lo[:, c, q], mk_hi[:, c, :], mk_lo[:, c, :],
                                   c == 0, c == 1)
                    last.then_inc(S["mm_scores"], 1)

                scores(0)
                scores(1)
                for u in range(NT):
                    g = 8 * i + u
                    pe.wait_ge(S["mm_probs"], g + 1)
                    if u >= 2:
                        pe.wait_ge(S["mm_pt_lo"], g - 1)
                    for j in range(2):
                        last = nc.tensor.transpose(bank(2 + u % 2, j * P, (j + 1) * P), mp[:, u % 2, j * P:(j + 1) * P],
                                                   ident)
                    last.then_inc(S["mm_pt"], 1)
                    if u + 2 < NT:
                        scores(u + 2)
                    if ahead:
                        if u == 0:
                            pe.wait_ge(S["mm_lo"], 3 * i + 3)
                        q_steps(4 * u, 4)
                    pe.wait_ge(S["mm_pt_lo"], g + 1)
                    if u >= 2:
                        pe.wait_ge(S["mm_out"], g)
                    for j in range(2):
                        last = mm3(bank(4 + u % 2, 0, C), mpt_hi[:, u % 2, j * P:(j + 1) * P],
                                   mpt_lo[:, u % 2, j * P:(j + 1) * P], mv_hi[:, j, :], mv_lo[:, j, :], j == 0, j == 1)
                    last.then_inc(S["mm_pv"], 1)
                pe.wait_ge(S["mm_out"], 8 * i + 9)
                for c in range(2):
                    for t in range(NT):
                        last = nc.tensor.transpose(ps[:, 2 * c * BANK + t * P:2 * c * BANK + (t + 1) * P],
                                                   mo[:, t, c * P:(c + 1) * P], ident)
                last.then_inc(S["mm_ot"], 1)
                pe.wait_ge(S["mm_done"], i + 1)

            with pe.Fori(0, 3) as i:
                memory_head(i, True)
            memory_head(3, False)
            linear("wom", T_WOM, "memo")
            sum_squares("x3")
            spread("x3")
            with pe.Fori(0, 4) as b:
                with pe.Fori(0, 4) as i:
                    for s in range(2):
                        tile_ready(16 * b + 2 * i + (T_MLP + s))
                        pe.wait_ge(S["a_lo"], 8 * b + 2 * i + (s + 1))
                        project(s, 2 * s, act_hi, act_lo, T, ready=filled("x3")).then_inc(S["tile_done"], 1)
                pe.sem_inc(S["issued"], 1)
                with pe.Fori(0, 4) as i:
                    for s in range(2):
                        tile_ready(16 * b + 2 * i + (T_MLP + 8 + s))
                        pe.wait_ge(S["mlp_acc"], 8 * b + 2 * i + (s + 1))
                        project(s, 4 + 2 * s, a_hi, a_lo, T,
                                ready=lambda k: pe.wait_ge(S["a_lo"], 8 * b + (k + 3))
                                ).then_inc(S["tile_done"], 1)
            sum_squares("final")
            spread("final")


def _tiles(w, cols=P):
    n = w.shape[1] // cols
    return w.reshape(KT, P, n, cols).transpose(2, 1, 0, 3).reshape(n, P, KT * cols)


def _cols(v):
    return v.reshape(-1, P).T


def _feature_major(a):
    return np.ascontiguousarray(a.T.reshape(KT, P, -1).transpose(1, 0, 2))


def _constants():
    ident = np.eye(P)
    tri = np.triu(np.ones((P, P)))
    ones = np.ones((P, P))
    bd = np.kron(np.eye(2), np.ones((HD, HD)))
    perm = np.zeros((P, P))
    for h in range(2):
        for ax in range(2):
            for f in range(16):
                lo, hi = h * 64 + ax * 32 + f, h * 64 + ax * 32 + 16 + f
                perm[hi, lo] = -1.0
                perm[lo, hi] = 1.0
    return np.concatenate([ident, tri, ones, bd, perm], 1).astype(np.float32)


def _rope():
    nf = HD // 4
    inv = (np.float32(10000.0) ** (-np.arange(nf, dtype=np.float32) / nf)).astype(np.float32)
    pos = np.arange(T)
    out = np.zeros((P, 2, T), np.float32)
    for p in range(P):
        ax, f = (p % HD) // 32, p % 16
        coord = (pos // GRID_W if ax == 0 else pos % GRID_W).astype(np.float32)
        ang = (coord * inv[f]).astype(np.float32)
        out[p, 0], out[p, 1] = np.cos(ang), np.sin(ang)
    return out


def _masks():
    q = np.arange(GRID_W)
    start = np.clip(q - 8, 0, GRID_W - 16)
    ok = (q[None, :] >= start[:, None]) & (q[None, :] < start[:, None] + 16)
    col = np.where(ok, 0.0, NEG)
    out = np.zeros((P, 10, GRID_W), np.float32)
    for a in range(2):
        for r in range(9):
            row_ok = r <= 7 if a == 0 else 1 <= r <= 8
            out[a * 64:(a + 1) * 64, r] = col if row_ok else NEG
        out[a * 64:(a + 1) * 64, 9] = col
    return out


def _buckets(n):
    d = np.arange(n)
    large = 16 + (np.log(np.maximum(d, 1) / 16.0) / math.log(8.0) * 16).astype(np.int64)
    return np.where(d < 16, d, np.minimum(large, 31))


def _place_rpb(rpb):
    out = np.zeros((8, 15, 127), rpb.dtype)
    out[:, :, 48:79] = rpb
    return out


def _place_rel(rel_bias):
    out = np.full((4, T + P - 1), NEG, rel_bias.dtype)
    out[:, :T] = rel_bias[_buckets(T)[::-1]].T
    return out


_OUT = "out_0_dram"


def kernel(**inputs):
    import concourse.bacc as bacc
    from concourse.bass_utils import run_bass_kernel_spmd

    a = {k: np.asarray(v) for k, v in inputs.items()}
    x_t, ctx_t, mem_t = (_feature_major(a[n][0]) for n in ("x", "ctx", "mem_2"))
    cond_t = np.stack([_cols(a["c"][0]), _cols(a["c_ctx"])], axis=-1)
    w_in, w_in2 = _tiles(a["w_in"][0]), a["w_in_2"][0]
    stream = []
    for i in range(4):
        stream += [w_in[[i, 4 + i, 8 + i, 12 + i]]]
        stream += [w_in[[16 + i, 24 + i, 20 + i, 28 + i]]]
    stream += [_tiles(a["w_out"][0])]
    w2a, w2g = _tiles(w_in2[:, :3072]), _tiles(w_in2[:, 3080:])
    for i in range(4):
        stream += [w2a[[8 + i, i, 4 + i]], w2g[[2 * i, 8 + 2 * i]]]
        stream += [w2a[[20 + i, 12 + i, 16 + i]], w2g[[2 * i + 1, 9 + 2 * i]]]
    stream += [_tiles(np.concatenate([a["w_diff_out_2"][0], a["w_fox_out_2"][0]], 0))]
    stream += [_tiles(a["w_o_2"][0])]
    wq, wkv = _tiles(a["w_q_mem_2"][0]), _tiles(a["w_kv_mem_2"][0])
    for i in range(4):
        stream += [wq[2 * i:2 * i + 2], wkv[2 * i:2 * i + 2], wkv[8 + 2 * i:10 + 2 * i]]
    stream += [_tiles(a["w_o_mem_2"][0])]
    w1, w2 = _tiles(a["w1_2"][0]), a["w2_2"][0]
    for b in range(4):
        stream += [w1[8 * b:8 * b + 8], _tiles(w2[1024 * b:1024 * b + 1024])]
    w_stream = np.concatenate(stream, 0)
    assert w_stream.shape[0] == N_TILES

    small = np.concatenate(
        [_cols(a["norm_g"][0]), _cols(a["g_mix_2"][0]), _cols(a["g_mem_q_2"][0]), _cols(a["g_mem_kv_2"][0]),
         _cols(a["g_mlp_2"][0]), _cols(a["g_final_2"]), _cols(a["b_ada"][0]),
         np.tile(a["q_norm_g"][0], 2)[:, None], np.tile(a["k_norm_g"][0], 2)[:, None],
         _cols(a["conv_w"][0].reshape(-1)), _cols(a["conv_b"][0]), a["g_subln_2"][0][:, None],
         np.tile(a["b_forget_2"][0][None], (P, 1))], 1)
    assert small.shape == (P, V_COLS)
    lam4 = np.stack([a[f"lambda_{n}_2"][0] for n in ("q1", "k1", "q2", "k2")]).reshape(1, -1)
    w_fl = np.ascontiguousarray(w_in2[:, 3072:3080].reshape(KT, P, 8).transpose(1, 0, 2))
    ins = dict(x_t=x_t, ctx_t=ctx_t, mem_t=mem_t, cond_t=cond_t, small=small, lam4=lam4,
               consts=_constants(), rope=_rope(), masks=_masks(),
               rpb_pad=_place_rpb(a["rpb"][0]), rel_rows=_place_rel(a["rel_bias_2"]), w_fl=w_fl,
               w_ada=_tiles(a["w_ada"][0], BANK), w_stream=w_stream)

    nc = bacc.Bacc("TRN2", target_bir_lowering=False, num_devices=1)
    arrays, aps = {}, {}
    for name, v in ins.items():
        v = np.ascontiguousarray(v)
        arrays[f"in_{name}_dram"] = v
        aps[name] = nc.dram_tensor(f"in_{name}_dram", v.shape, mybir.dt.from_np(v.dtype),
                                   kind="ExternalInput").ap()
    y_t = nc.dram_tensor(_OUT, (P, KT, T), F, kind="ExternalOutput").ap()
    program(nc, y_t=y_t, **aps)
    r = run_bass_kernel_spmd(nc, [arrays], core_ids=[0])
    y = r.results[0][_OUT]
    return np.ascontiguousarray(y.transpose(2, 1, 0).reshape(1, T, D))
```
